# Optimizing a Trainium2 kernel written in Bass

```python
import math
import jax, jax.numpy as jnp
from jax import lax
import numpy as np

D_MODEL = 1024
BATCH = 1
SEQ = 1024
DEPTH = 2

CHUNK = 64
Q_BLOCK = 128
F32 = jnp.float32

HEAD_DIM = 64
N_HEADS_SB = 8
N_HEADS_FOX = 8
FORGET_BIAS = 3.0

N_HEADS_DSA = 16
DSA_LATENT = 192
DSA_ROPE = 64
DSA_KEY_DIM = DSA_ROPE + DSA_LATENT
DSA_V_HEAD = 64
IDX_HEADS = 16
IDX_DIM = 64
IDX_TOPK = 256
IDX_SCALE = (IDX_HEADS * IDX_DIM) ** -0.5

ROPE_THETA = 500000.0
D_FF = 2816
CONV_WIDTH = 3
LN_EPS = 1e-5
ALPHA = (2 * DEPTH) ** 0.25
BETA = (8 * DEPTH) ** -0.25

W_IN_AB = 3 * (N_HEADS_SB + N_HEADS_FOX) * HEAD_DIM + N_HEADS_FOX
W_IN_C = N_HEADS_DSA * DSA_KEY_DIM + DSA_ROPE + DSA_LATENT + IDX_HEADS * IDX_DIM + IDX_DIM + IDX_HEADS

kernel_name = 'hybrid_stickbreak_fox_dsa_convffn'

def layer_norm(x, g, b):
    xf = x.astype(F32)
    mu = xf.mean(-1, keepdims=True)
    var = jnp.square(xf - mu).mean(-1, keepdims=True)
    y = (xf - mu) * lax.rsqrt(var + LN_EPS)
    return (y * g.astype(F32) + b.astype(F32)).astype(x.dtype)

def partial_rope(x, positions):
    d = x.shape[-1]
    rot = d // 4
    half = rot // 2
    freqs = ROPE_THETA ** (-jnp.arange(half, dtype=F32) / half)
    ang = positions.astype(F32)[..., None] * freqs
    ang = ang.reshape(ang.shape[:2] + (1,) * (x.ndim - 3) + (half,))
    cos, sin = jnp.cos(ang), jnp.sin(ang)
    xf = x.astype(F32)
    x1, x2, rest = xf[..., :half], xf[..., half:rot], xf[..., rot:]
    out = jnp.concatenate([x1 * cos - x2 * sin, x2 * cos + x1 * sin, rest], axis=-1)
    return out.astype(x.dtype)

def to_blocks(a):
    b, s = a.shape[:2]
    return a.reshape((b, s // Q_BLOCK, Q_BLOCK) + a.shape[2:]).swapaxes(0, 1)

def from_blocks(a):
    nb, b = a.shape[:2]
    return a.swapaxes(0, 1).reshape((b, nb * Q_BLOCK) + a.shape[3:])

def stick_breaking_attention(q, k, v):
    s_len, dh = q.shape[1], q.shape[3]
    scale = dh ** -0.5
    kf, vf = k.astype(F32), v.astype(F32)
    key_pos = jnp.arange(s_len)

    def block(args):
        i, qb = args
        qpos = i * Q_BLOCK + jnp.arange(Q_BLOCK)
        mask = key_pos[None, :] < qpos[:, None]
        z = jnp.einsum('bqhd,bshd->bhqs', qb.astype(F32), kf) * scale
        log_stay = jnp.where(mask, jax.nn.log_sigmoid(-z), 0.0)
        after = lax.cumsum(log_stay, axis=3, reverse=True) - log_stay
        w = jnp.where(mask, jnp.exp(jax.nn.log_sigmoid(z) + after), 0.0)
        return jnp.einsum('bhqs,bshd->bqhd', w, vf)

    out = lax.map(block, (jnp.arange(s_len // Q_BLOCK), to_blocks(q)))
    return from_blocks(out).astype(q.dtype)

def forgetting_attention(q, k, v, f_logit):
    s_len, dh = q.shape[1], q.shape[3]
    scale = dh ** -0.5
    kf, vf = k.astype(F32), v.astype(F32)
    cum = jnp.cumsum(jax.nn.log_sigmoid(f_logit.astype(F32)), axis=1)
    cum_k = cum.transpose(0, 2, 1)
    key_pos = jnp.arange(s_len)

    def block(args):
        i, qb, cq = args
        qpos = i * Q_BLOCK + jnp.arange(Q_BLOCK)
        mask = key_pos[None, :] <= qpos[:, None]
        logits = (jnp.einsum('bqhd,bshd->bhqs', qb.astype(F32), kf) * scale
                  + cq.transpose(0, 2, 1)[..., None] - cum_k[:, :, None, :])
        p = jax.nn.softmax(jnp.where(mask, logits, -jnp.inf), axis=-1)
        return jnp.einsum('bhqs,bshd->bqhd', p, vf)

    out = lax.map(block, (jnp.arange(s_len // Q_BLOCK), to_blocks(q), to_blocks(cum)))
    return from_blocks(out).astype(q.dtype)

def dsa_attention(q, k_lat, q_idx, k_idx, w_idx):
    s_len = q.shape[1]
    topk = min(IDX_TOPK, s_len // 4)
    scale = DSA_KEY_DIM ** -0.5
    klf, kif = k_lat.astype(F32), k_idx.astype(F32)
    key_pos = jnp.arange(s_len)

    def block(args):
        i, qb, qib, wb = args
        qpos = i * Q_BLOCK + jnp.arange(Q_BLOCK)
        visible = key_pos[None, :] < (qpos[:, None] // CHUNK + 1) * CHUNK
        idx_logits = jax.nn.relu(jnp.einsum('bqhd,bsd->bqhs', qib.astype(F32), kif))
        score = jnp.einsum('bqh,bqhs->bqs', wb.astype(F32), idx_logits) * IDX_SCALE
        score = jnp.where(visible[None], score, -jnp.inf)
        top_val, top_idx = lax.top_k(score, topk)
        valid = jnp.isfinite(top_val)
        k_sel = jax.vmap(lambda kb, ib: kb[ib])(klf, top_idx)
        logits = jnp.einsum('bqhd,bqkd->bqhk', qb.astype(F32), k_sel) * scale
        p = jax.nn.softmax(jnp.where(valid[:, :, None, :], logits, -jnp.inf), axis=-1)
        return jnp.einsum('bqhk,bqkc->bqhc', p, k_sel[..., DSA_ROPE:])

    out = lax.map(block, (jnp.arange(s_len // Q_BLOCK), to_blocks(q), to_blocks(q_idx), to_blocks(w_idx)))
    return from_blocks(out).astype(q.dtype)

def mixer_sb_fox(x, w_in, b_f, w_o):
    b, s, _ = x.shape
    gw = N_HEADS_SB * HEAD_DIM
    h = x @ w_in
    parts = jnp.split(h, [gw, 2 * gw, 3 * gw, 4 * gw, 5 * gw, 6 * gw], axis=-1)
    qa, ka, va = [p.reshape(b, s, N_HEADS_SB, HEAD_DIM) for p in parts[:3]]
    qb, kb, vb = [p.reshape(b, s, N_HEADS_FOX, HEAD_DIM) for p in parts[3:6]]
    f_logit = parts[6] + b_f
    oa = stick_breaking_attention(qa, ka, va).reshape(b, s, -1)
    ob = forgetting_attention(qb, kb, vb, f_logit).reshape(b, s, -1)
    return jnp.concatenate([oa, ob], axis=-1) @ w_o

def mixer_dsa(x, positions, w_in, w_uv, w_o):
    b, s, _ = x.shape
    h = x @ w_in
    c0 = N_HEADS_DSA * DSA_KEY_DIM
    c1 = c0 + DSA_ROPE
    c2 = c1 + DSA_LATENT
    c3 = c2 + IDX_HEADS * IDX_DIM
    c4 = c3 + IDX_DIM
    q, k_r, c_lat, q_idx, k_idx, w_idx = jnp.split(h, [c0, c1, c2, c3, c4], axis=-1)
    q = partial_rope(q.reshape(b, s, N_HEADS_DSA, DSA_KEY_DIM), positions)
    k_lat = partial_rope(jnp.concatenate([k_r, c_lat], axis=-1), positions)
    q_idx = partial_rope(q_idx.reshape(b, s, IDX_HEADS, IDX_DIM), positions)
    k_idx = partial_rope(k_idx, positions)
    ctx = dsa_attention(q, k_lat, q_idx, k_idx, w_idx)
    o = jnp.einsum('bshc,hcd->bshd', ctx, w_uv).reshape(b, s, -1)
    return o @ w_o

def conv_ffn(x, w_up, conv_w, conv_b, w_down):
    s = x.shape[1]
    gate, up = jnp.split(x @ w_up, 2, axis=-1)
    gp = jnp.pad(gate, ((0, 0), (CONV_WIDTH - 1, 0), (0, 0)))
    conv = conv_b + conv_w[0] * gp[:, 0:s]
    for j in range(1, CONV_WIDTH):
        conv = conv + conv_w[j] * gp[:, j:j + s]
    return (jax.nn.gelu(conv) * up) @ w_down

def setup_inputs(seed: int = 0) -> dict:
    key = jax.random.key(seed)
    ks = jax.random.split(key, 32)
    nrm = lambda k, shape, scale: jax.random.normal(k, shape, F32) * scale
    offsets = jax.random.randint(ks[1], (BATCH, 1), 0, 4096, dtype=jnp.int32)
    positions = (offsets + jnp.arange(SEQ, dtype=jnp.int32)[None, :]).astype(jnp.int32)
    inp = {'x': nrm(ks[0], (BATCH, SEQ, D_MODEL), 1.0), 'positions': positions}
    d_in = D_MODEL ** -0.5
    inp['l0_w_in'] = nrm(ks[2], (D_MODEL, W_IN_AB), d_in)
    inp['l0_b_f'] = FORGET_BIAS + nrm(ks[3], (N_HEADS_FOX,), 0.1)
    inp['l0_w_o'] = nrm(ks[4], (D_MODEL, D_MODEL), d_in * BETA)
    inp['l0_ln1_g'] = 1.0 + nrm(ks[5], (D_MODEL,), 0.02)
    inp['l0_ln1_b'] = nrm(ks[6], (D_MODEL,), 0.02)
    inp['l0_w_up'] = nrm(ks[7], (D_MODEL, 2 * D_FF), d_in)
    inp['l0_conv_w'] = nrm(ks[8], (CONV_WIDTH, D_FF), CONV_WIDTH ** -0.5)
    inp['l0_conv_b'] = nrm(ks[9], (D_FF,), 0.02)
    inp['l0_w_down'] = nrm(ks[10], (D_FF, D_MODEL), D_FF ** -0.5 * BETA)
    inp['l0_ln2_g'] = 1.0 + nrm(ks[11], (D_MODEL,), 0.02)
    inp['l0_ln2_b'] = nrm(ks[12], (D_MODEL,), 0.02)
    inp['l1_w_in'] = nrm(ks[13], (D_MODEL, W_IN_C), d_in)
    inp['l1_w_uv'] = nrm(ks[14], (N_HEADS_DSA, DSA_LATENT, DSA_V_HEAD), DSA_LATENT ** -0.5)
    inp['l1_w_o'] = nrm(ks[15], (N_HEADS_DSA * DSA_V_HEAD, D_MODEL), (N_HEADS_DSA * DSA_V_HEAD) ** -0.5 * BETA)
    inp['l1_ln1_g'] = 1.0 + nrm(ks[16], (D_MODEL,), 0.02)
    inp['l1_ln1_b'] = nrm(ks[17], (D_MODEL,), 0.02)
    inp['l1_w_up'] = nrm(ks[18], (D_MODEL, 2 * D_FF), d_in)
    inp['l1_conv_w'] = nrm(ks[19], (CONV_WIDTH, D_FF), CONV_WIDTH ** -0.5)
    inp['l1_conv_b'] = nrm(ks[20], (D_FF,), 0.02)
    inp['l1_w_down'] = nrm(ks[21], (D_FF, D_MODEL), D_FF ** -0.5 * BETA)
    inp['l1_ln2_g'] = 1.0 + nrm(ks[22], (D_MODEL,), 0.02)
    inp['l1_ln2_b'] = nrm(ks[23], (D_MODEL,), 0.02)
    return inp

def reference(x, positions,
              l0_w_in, l0_b_f, l0_w_o, l0_ln1_g, l0_ln1_b,
              l0_w_up, l0_conv_w, l0_conv_b, l0_w_down, l0_ln2_g, l0_ln2_b,
              l1_w_in, l1_w_uv, l1_w_o, l1_ln1_g, l1_ln1_b,
              l1_w_up, l1_conv_w, l1_conv_b, l1_w_down, l1_ln2_g, l1_ln2_b):
    mixer_params = [(l0_w_in, l0_b_f, l0_w_o), (l1_w_in, l1_w_uv, l1_w_o)]
    norm1 = [(l0_ln1_g, l0_ln1_b), (l1_ln1_g, l1_ln1_b)]
    ffn_params = [(l0_w_up, l0_conv_w, l0_conv_b, l0_w_down), (l1_w_up, l1_conv_w, l1_conv_b, l1_w_down)]
    norm2 = [(l0_ln2_g, l0_ln2_b), (l1_ln2_g, l1_ln2_b)]
    for i in range(DEPTH):
        if i % 2 == 0:
            m = mixer_sb_fox(x, *mixer_params[i])
        else:
            m = mixer_dsa(x, positions, *mixer_params[i])
        x = layer_norm(ALPHA * x + m, *norm1[i])
        x = layer_norm(ALPHA * x + conv_ffn(x, *ffn_params[i]), *norm2[i])
    return x


_drawn_inputs = setup_inputs


def setup_inputs(seed=0):
    import zlib

    import numpy as np

    out = dict(_drawn_inputs(seed))
    spreads = {}
    factors = {'l0_b_f': 64.0,
     'l0_conv_b': 8.0,
     'l0_ln2_g': 2.688,
     'l1_ln1_g': 2.785,
     'l1_ln1_b': 2.782,
     'l1_conv_b': 8.0,
     'l1_ln2_g': 7.971,
     'l1_ln2_b': 8.211}
    for name, (base, spread) in spreads.items():
        noise = np.random.default_rng([zlib.crc32(name.encode()), seed]).standard_normal(out[name].shape)
        drawn = base * np.exp(spread * noise) if base else spread * noise
        out[name] = __import__('jax').numpy.asarray(drawn.astype(out[name].dtype))
    for name, factor in factors.items():
        out[name] = (out[name] * factor).astype(out[name].dtype)
    return out
```

```python
import numpy as np
from contextlib import ExitStack

import concourse.bass as bass
from concourse import mybir

F32 = mybir.dt.float32
BF16 = mybir.dt.bfloat16
I32 = mybir.dt.int32
ALU = mybir.AluOpType
ACT = mybir.ActivationFunctionType
AX = mybir.AxisListType

P = 128
D_MODEL = 1024
SEQ = 1024
DEPTH = 2
KT = D_MODEL // P
TB = SEQ // P
HALF = SEQ // 2
CHUNK = 64
HEAD_DIM = 64
N_SB = 8
N_FOX = 8
N_PAIRS = (N_SB + N_FOX) // 2
N_DSA = 16
LATENT = 192
ROPE = 64
KEY_DIM = ROPE + LATENT
IDX_HEADS = 16
IDX_DIM = 64
TOPK = min(256, SEQ // 4)
IDX_SCALE = float(IDX_HEADS * IDX_DIM) ** -0.5
SB_SCALE = float(HEAD_DIM) ** -0.5
DSA_SCALE = float(KEY_DIM) ** -0.5
THETA = 500000.0
D_FF = 2816
FT = D_FF // P
ALPHA = float((2 * DEPTH) ** 0.25)
LN_EPS = 1e-5
MASKED = -1e30
HIDDEN_SCORE = -1e38
TAKEN_SCORE = -3e38
SLOTS = 4
DOWN_CUT = [(0, 6), (6, 12), (12, 17), (17, 22)]
STEPS = 16
TR_LAG = 3
EV_LAG = 4

assert SEQ % P == 0 and D_FF % P == 0 and N_DSA == 2 * N_PAIRS


def query_block(t):
    return TB - 1 - t % TB


def batches_through(t):
    return sum(2 if query_block(s) >= 4 else 1 for s in range(t + 1))


BATCHES = batches_through(STEPS - 1)


def since(first, n):
    return first + max(n, 0)


def wait_apart(eng, always, *waits):
    values = [(s, v if isinstance(v, int) else eng.to_reg(v)) for s, v in waits]
    eng.wait_ge(*always)
    for s, v in values:
        eng.wait_ge(s, v)


class Feed:

    def __init__(self, uses, used, dram, pieces, iters, counted=True):
        self.dram, self.pieces, self.iters = dram, pieces, iters
        self.base, self.used_base = dict(uses), dict(used)
        self.order, self.per_iter = [], {s: 0 for s in range(SLOTS)}
        for slot, _ in pieces:
            self.order.append(self.per_iter[slot])
            self.per_iter[slot] += 1
        for s in range(SLOTS):
            uses[s] += iters * self.per_iter[s]
            if counted:
                used[s] += iters * self.per_iter[s]

    def slot(self, n):
        return self.pieces[n][0]

    def use(self, n, i):
        slot = self.slot(n)
        return self.base[slot] + i * self.per_iter[slot] + self.order[n]

    def used(self, n, i):
        slot = self.slot(n)
        return self.used_base[slot] + i * self.per_iter[slot] + self.order[n]


def program(nc, t_in, out):
    with ExitStack() as ctx:
        start = (nc.sbuf_base + 63) // 64 * 64
        KB = 1024
        limit = nc.sbuf_usable_end - start

        def sb(name, shape, dt, at):
            size = int(np.prod(shape[1:])) * (2 if dt == BF16 else 4)
            assert at + size <= limit, (name, at + size, limit)
            return nc.alloc_sbuf_tensor_at(name, shape, dt, offset=start + at)

        class Room:

            def __init__(self, at):
                self.at = at

            def __call__(self, name, shape, dt):
                t = sb(name, shape, dt, self.at)
                self.at += (int(np.prod(shape[1:])) * (2 if dt == BF16 else 4) + 31) // 32 * 32
                return t

        layer_sems = []

        def sem(name):
            layer_sems.append(nc.alloc_semaphore(name))
            return layer_sems[-1]

        def clear_sems():
            nc.clear_and_free_semaphores(layer_sems)
            layer_sems.clear()
            nc.all_engine_barrier(sem_only=True)

        keep = Room(0)
        ident = keep("ident", [P, P], F32)
        ident_b = keep("ident_b", [P, P], BF16)
        mask_strict = keep("mask_strict", [P, P], BF16)
        mask_causal = keep("mask_causal", [P, P], BF16)
        ln_stats = keep("ln_stats", [P, TB, 12], F32)
        ln_mv = keep("ln_mv", [P, TB, 2], F32)
        ln_rstd = keep("ln_rstd", [P, TB], F32)
        row_max = keep("row_max", [P, 4], F32)
        neg_max = keep("neg_max", [P, 4], F32)
        row_sum = keep("row_sum", [P, 4], F32)
        row_inv = keep("row_inv", [P, 4], F32)
        tiny = keep("tiny", [P, 8], F32)
        ones = keep("ones", [P, 1], F32)
        assert keep.at <= 3 * KB
        wroom = Room(3 * KB)
        w_stage = [wroom(f"w_stage{s}", [P, KT * P], F32) for s in range(SLOTS)]
        w_hi = [wroom(f"w_hi{s}", [P, KT * P], BF16) for s in range(SLOTS)]
        w_lo = [wroom(f"w_lo{s}", [P, KT * P], BF16) for s in range(SLOTS)]
        xt_hi = wroom("xt_hi", [P, KT, SEQ], BF16)
        xt_lo = wroom("xt_lo", [P, KT, SEQ], BF16)
        res_at = wroom.at
        x_res = wroom("x_res", [P, TB, D_MODEL], F32)
        arena = wroom.at

        ps = ctx.enter_context(nc.psum_tensor("ps", [P, 8, 512], F32))

        def banks(b):
            return ps[:, b:b + 2, :].rearrange("p a n -> p (a n)")

        w_loaded = [sem(f"w_loaded{s}") for s in range(SLOTS)]
        w_cast = [sem(f"w_cast{s}") for s in range(SLOTS)]
        w_split = [sem(f"w_split{s}") for s in range(SLOTS)]
        w_used = [sem(f"w_used{s}") for s in range(SLOTS)]
        layer_sems.clear()
        uses = {s: 0 for s in range(SLOTS)}
        used = {s: 0 for s in range(SLOTS)}

        feed_qkv = Feed(uses, used, lambda n, i: t_in["l0_qkv"][3 * i + n], [(0, 1024), (1, 1024), (2, 1024)],
                        N_PAIRS, counted=False)

        def strips(name, per_body, iters):
            return Feed(uses, used, lambda n, i: t_in[name][per_body * i + n],
                        [(n, KT * P) for n in range(per_body)], iters)

        def down(name):
            def dram(n, i):
                a, b = DOWN_CUT[n % 4]
                return t_in[name][2 * i + n // 4][:, a * P:b * P]
            return Feed(uses, used, dram,
                        [(n % 4, (DOWN_CUT[n % 4][1] - DOWN_CUT[n % 4][0]) * P) for n in range(8)], KT // 2)

        feed_o0 = strips("l0_o", 4, 2)
        feed_up0 = strips("l0_up", 4, FT // 2)
        feed_down0 = down("l0_down")
        small_cols = [1024, 1024, 1024, 1024, KT * 80]
        small_names = ["l1_kidx", "l1_klat0", "l1_klat1", "l1_v128", "l1_v64w"]
        feed_small = Feed(uses, used, lambda n, i: t_in[small_names[n]],
                          [(s, c) for s, c in zip([0, 1, 2, 3, 0], small_cols)], 1)
        feed_qidx = strips("l1_qidx", 4, 2)
        feed_q = strips("l1_q", 4, 8)
        feed_o1 = strips("l1_o", 4, 2)
        feed_up1 = strips("l1_up", 4, FT // 2)
        feed_down1 = down("l1_down")

        def load_piece(sp, feed, n, i):
            slot, cols = feed.pieces[n]
            sp.wait_ge(w_split[slot], feed.use(n, i))
            sp.dma_start(w_stage[slot][:, 0:cols], feed.dram(n, i)).then_inc(w_loaded[slot], 16)

        def load_first(sp, feed):
            for n in range(len(feed.pieces)):
                if feed.order[n] == 0:
                    load_piece(sp, feed, n, 0)

        def load_rest(sp, feed):
            for n in range(len(feed.pieces)):
                if feed.order[n] > 0:
                    load_piece(sp, feed, n, 0)
            if feed.iters > 1:
                with sp.Fori(1, feed.iters) as i:
                    for n in range(len(feed.pieces)):
                        load_piece(sp, feed, n, i)

        def split_piece(pool, feed, n, i):
            slot, cols = feed.pieces[n]
            pool.wait_ge(w_loaded[slot], 16 * (feed.use(n, i) + 1))
            pool.wait_ge(w_used[slot], feed.used(n, i))
            pool.tensor_tensor(w_hi[slot][:, 0:cols], w_stage[slot][:, 0:cols], ones[:, 0:1].to_broadcast([P, cols]),
                               ALU.mult).then_inc(w_cast[slot], 1)
            pool.wait_ge(w_cast[slot], feed.use(n, i) + 1)
            pool.tensor_tensor(w_lo[slot][:, 0:cols], w_stage[slot][:, 0:cols], w_hi[slot][:, 0:cols],
                               ALU.subtract).then_inc(w_split[slot], 1)

        def split_all(pool, feed):
            if feed.iters == 1:
                for n in range(len(feed.pieces)):
                    split_piece(pool, feed, n, 0)
            else:
                with pool.Fori(0, feed.iters) as i:
                    for n in range(len(feed.pieces)):
                        split_piece(pool, feed, n, i)

        def products(pe, feed, n, i, bank, act_hi, act_lo, k0, k1, first, last):
            slot = feed.slot(n)
            pe.wait_ge(w_split[slot], feed.use(n, i) + 1)
            for k in range(k0, k1):
                wh = w_hi[slot][:, (k - k0) * P:(k - k0 + 1) * P]
                wl = w_lo[slot][:, (k - k0) * P:(k - k0 + 1) * P]
                for m, (w, a) in enumerate(((wh, act_hi), (wh, act_lo), (wl, act_hi))):
                    for h in range(2):
                        mm = pe.matmul(ps[:, bank + h, :], w, a[:, k, h * HALF:(h + 1) * HALF],
                                       start=(first and k == k0 and m == 0),
                                       stop=(last and k == k1 - 1 and m == 2))
            mm.then_inc(w_used[slot], 1)

        room = Room(arena)
        xt_f = room("xt_f", [P, KT, SEQ], F32)
        pos_i = room("pos_i", [P, SEQ], I32)
        pos_f = room("pos_f", [P, SEQ], F32)
        angle = room("angle", [P, SEQ], F32)
        turns = room("turns", [P, SEQ], F32)
        rope_c = room("rope_c", [P, SEQ], F32)
        rope_s = room("rope_s", [P, SEQ], F32)
        rope_rows = room("rope_rows", [P, 4], F32)
        wf_f = room("wf_f", [P, KT, 8], F32)
        wf_hi = room("wf_hi", [P, KT, 8], BF16)
        wf_lo = room("wf_lo", [P, KT, 8], BF16)
        gate_b = room("gate_b", [8, 1], F32)
        low = Room(res_at)
        cum_rows = low("cum_rows", [96, SEQ], BF16)
        cum_pick = low("cum_pick", [96, N_FOX, P], BF16)
        gate_x = low("gate_x", [8, SEQ], F32)
        gate_a = low("gate_a", [8, SEQ], F32)
        gate_m = low("gate_m", [8, SEQ], F32)
        gate_c = low("gate_c", [8, SEQ], F32)
        gate_p = low("gate_p", [8, SEQ], BF16)
        tables = nc.dram_tensor("rope_tables", (4, P, SEQ), F32, kind="Internal").ap()
        s_pos, s_wf = sem("pos_loaded"), sem("wf_loaded")
        s_xt = [sem(f"xt_loaded{k}") for k in range(KT)]
        s_xh, s_xl = sem("xt_hi_written"), sem("xt_lo_written")
        s_const = sem("const_step")
        s_wfh, s_wfl = sem("wf_hi_written"), sem("wf_lo_written")
        s_tab, s_sin, s_tabst = sem("table_step"), sem("table_sin"), sem("table_stored")
        s_gmm, s_gact, s_gdve = sem("gate_product"), sem("gate_act"), sem("gate_dve")
        inv_2pi = float(np.float32(1 / (2 * np.pi)))
        pi_a = 6.28125
        rest = 2 * np.pi - pi_a
        pi_b = float(np.floor(rest * 2 ** 17) / 2 ** 17)
        pi_c = float(np.float32(rest - pi_b))
        magic = 1.5 * 2 ** 23
        pi_max = 3.1415925

        with nc.Block() as block:
            @block.sync
            def _(sp):
                sp.dma_start(pos_i[:, :], t_in["positions"]).then_inc(s_pos, 16)
                sp.dma_start(rope_rows[:, :], t_in["rope_rows"]).then_inc(s_pos, 16)
                for k in range(0, KT, 2):
                    sp.dma_start(xt_f[:, k, :], t_in["xt"][:, k, :]).then_inc(s_xt[k], 16)
                load_first(sp, feed_qkv)
                for t in range(2):
                    for c in range(2):
                        sp.wait_ge(s_tab, 11 * t + (10 if c == 0 else 11))
                        sp.dma_start(tables[2 * t + c], (rope_c if c == 0 else rope_s)[:, :]).then_inc(s_tabst, 16)
                sp.wait_ge(s_tabst, 64)

            @block.scalar
            def _(act):
                act.dma_start(wf_f[:, :, :], t_in["l0_wf"]).then_inc(s_wf, 16)
                act.dma_start(gate_b[:, :], t_in["l0_bf"]).then_inc(s_wf, 16)
                for k in range(1, KT, 2):
                    act.dma_start(xt_f[:, k, :], t_in["xt"][:, k, :]).then_inc(s_xt[k], 16)
                for t in range(2):
                    act.wait_ge(s_tab, 11 * t + 8)
                    if t:
                        act.wait_ge(s_tabst, 32)
                    act.activation(rope_s[:, :], angle[:, :], ACT.Sin).then_inc(s_sin, 1)
                    act.activation(rope_c[:, :], angle[:, :], ACT.Sin, scale=0.5).then_inc(s_sin, 1)
                for k in range(KT):
                    act.wait_ge(s_xt[k], 16)
                    act.activation(xt_hi[:, k, :], xt_f[:, k, :], ACT.Copy).then_inc(s_xh, 1)
                act.preload_act_table_set("natural_log_exp_and_others")
                act.wait_ge(s_gmm, 1)
                act.wait_ge(s_wf, 32)
                act.activation(gate_x[:, :], banks(0)[0:8, :], ACT.Identity, bias=gate_b[:, 0:1]).then_inc(s_gact, 1)
                act.wait_ge(s_gact, 1)
                act.activation(gate_a[:, :], gate_x[:, :], ACT.Abs).then_inc(s_gact, 1)
                act.wait_ge(s_gact, 2)
                act.activation(gate_a[:, :], gate_a[:, :], ACT.Exp, scale=-1.0).then_inc(s_gact, 1)
                act.wait_ge(s_gact, 3)
                act.activation(gate_a[:, :], gate_a[:, :], ACT.Ln, bias=1.0).then_inc(s_gact, 1)

            @block.gpsimd
            def _(pool):
                steps = 0

                def done(ins):
                    nonlocal steps
                    steps += 1
                    ins.then_inc(s_const, 1)

                done(pool.memset(ident[:, :], 0.0))
                done(pool.memset(ident_b[:, :], 0.0))
                done(pool.memset(mask_strict[:, :], 0.0))
                done(pool.memset(mask_causal[:, :], 0.0))
                done(pool.memset(cum_pick[:, :, :], 0.0))
                done(pool.memset(cum_rows[:, :], 0.0))
                done(pool.memset(ones[:, :], 1.0))
                pool.wait_ge(s_const, 7)
                for m in (ident, ident_b):
                    done(pool.affine_select(out=m[:, :], in_=m[:, :], compare_op=ALU.not_equal, fill=1.0,
                                            base=0, pattern=[[-1, P]], channel_multiplier=1))
                done(pool.affine_select(out=mask_strict[:, :], in_=mask_strict[:, :], compare_op=ALU.is_gt,
                                        fill=MASKED, base=0, pattern=[[-1, P]], channel_multiplier=1))
                done(pool.affine_select(out=mask_causal[:, :], in_=mask_causal[:, :], compare_op=ALU.is_ge,
                                        fill=MASKED, base=0, pattern=[[-1, P]], channel_multiplier=1))
                for r in range(3):
                    done(pool.affine_select(out=cum_pick[:, :, :], in_=cum_pick[:, :, :],
                                            compare_op=ALU.not_equal, fill=-1.0 / SB_SCALE, base=-32 * r,
                                            pattern=[[-1, N_FOX], [0, P]], channel_multiplier=1))
                    pool.wait_ge(s_const, steps)
                pool.wait_ge(s_wf, 32)
                pool.tensor_copy(wf_hi[:, :, :], wf_f[:, :, :]).then_inc(s_wfh, 1)
                pool.wait_ge(s_wfh, 1)
                pool.tensor_tensor(wf_lo[:, :, :], wf_f[:, :, :], wf_hi[:, :, :], ALU.subtract).then_inc(s_wfl, 1)
                split_piece(pool, feed_qkv, 0, 0)
                split_piece(pool, feed_qkv, 1, 0)
                split_piece(pool, feed_qkv, 2, 0)

            @block.tensor
            def _(pe):
                pe.wait_ge(s_wfl, 1)
                for k in range(KT):
                    pe.wait_ge(s_xl, k + 1)
                    for h in range(2):
                        for m, (w, a) in enumerate(((wf_hi, xt_hi), (wf_hi, xt_lo), (wf_lo, xt_hi))):
                            mm = pe.matmul(ps[0:8, h, :], w[:, k, :], a[:, k, h * HALF:(h + 1) * HALF],
                                           start=(k == 0 and m == 0), stop=(k == KT - 1 and m == 2))
                mm.then_inc(s_gmm, 1)

            @block.vector
            def _(dve):
                dve.wait_ge(s_pos, 32)
                step = 0

                def then(ins):
                    nonlocal step
                    step += 1
                    ins.then_inc(s_tab, 1)
                    dve.wait_ge(s_tab, step)

                for t in range(2):
                    if t == 0:
                        then(dve.tensor_copy(pos_f[:, :], pos_i[:, :]))
                    else:
                        then(dve.tensor_copy(tiny[:, 0:1], rope_rows[:, 0:1]))
                    then(dve.tensor_scalar(angle[:, :], pos_f[:, :], rope_rows[:, 2 * t:2 * t + 1], None, ALU.mult))
                    then(dve.tensor_scalar(turns[:, :], angle[:, :], inv_2pi, magic, ALU.mult, ALU.add))
                    then(dve.tensor_scalar(turns[:, :], turns[:, :], -magic, None, ALU.add))
                    for c in (pi_a, pi_b, pi_c):
                        then(dve.scalar_tensor_tensor(angle[:, :], turns[:, :], -c, angle[:, :], ALU.mult, ALU.add))
                    then(dve.tensor_scalar(angle[:, :], angle[:, :], pi_max, -pi_max, ALU.min, ALU.max))
                    dve.wait_ge(s_sin, 2 * t + 2)
                    then(dve.tensor_tensor(rope_c[:, :], rope_c[:, :], rope_c[:, :], ALU.mult))
                    then(dve.tensor_scalar(rope_c[:, :], rope_c[:, :], -2.0, 1.0, ALU.mult, ALU.add))
                    then(dve.tensor_scalar(rope_s[:, :], rope_s[:, :], rope_rows[:, 2 * t + 1:2 * t + 2], None, ALU.mult))
                for k in range(KT):
                    dve.wait_ge(s_xh, k + 1)
                    dve.tensor_tensor(xt_lo[:, k, :], xt_f[:, k, :], xt_hi[:, k, :], ALU.subtract).then_inc(s_xl, 1)
                gstep = 0

                def gthen(ins):
                    nonlocal gstep
                    gstep += 1
                    ins.then_inc(s_gdve, 1)
                    dve.wait_ge(s_gdve, gstep)

                dve.wait_ge(s_gact, 1)
                gthen(dve.tensor_scalar(gate_m[:, :], gate_x[:, :], 0.0, None, ALU.min))
                dve.wait_ge(s_gact, 4)
                gthen(dve.tensor_tensor_scan(gate_c[:, :], gate_m[:, :], gate_a[:, :], 0.0, ALU.add, ALU.subtract))
                dve.wait_ge(s_const, 6)
                for r in range(3):
                    gthen(dve.tensor_copy(gate_p[:, :], gate_c[:, :]))
                    gthen(dve.tensor_copy(cum_rows[32 * r:32 * r + 8, :], gate_p[:, :]))
                    if r < 2:
                        gthen(dve.tensor_tensor(gate_c[:, :], gate_c[:, :], gate_p[:, :], ALU.subtract))

        low = Room(res_at + 4 * KB)
        pick_now = low("pick_now", [96, 2, P], BF16)
        score_z = [low(f"score_z{b}", [P, SEQ], F32) for b in range(2)]
        soft_a = [low(f"soft_a{b}", [P, SEQ], F32) for b in range(2)]
        prob = [low(f"prob{b}", [P, SEQ], F32) for b in range(2)]
        assert low.at <= arena
        room = Room(arena)
        mix_hi = room("mix_hi", [P, KT, SEQ], BF16)
        mix_lo = room("mix_lo", [P, KT, SEQ], BF16)
        prob += [room(f"prob{b}", [P, SEQ], F32) for b in range(2, 4)]
        q_hi, q_lo, k_hi, k_lo = [room(n, [P, SEQ], BF16) for n in ("q_hi", "q_lo", "k_hi", "k_lo")]
        nq_hi, nq_lo, nk_hi, nk_lo = [room(n, [P, SEQ], BF16) for n in ("nq_hi", "nq_lo", "nk_hi", "nk_lo")]
        v_hi, v_lo, nv_hi, nv_lo = [room(n, [P, TB, P], BF16) for n in ("v_hi", "v_lo", "nv_hi", "nv_lo")]
        pt_hi = [room("pt_hi0", [P, TB, 512], BF16), room("pt_hi1", [P, TB // 2, 512], BF16)]
        pt_lo = [room("pt_lo0", [P, TB, 512], BF16), room("pt_lo1", [P, TB // 2, 512], BF16)]

        s_qk = sem("scores_ready")
        s_sfree = sem("score_bank_read")
        s_r, s_ab, s_e, s_ln, s_sc, s_sub = [sem(n) for n in
            ("relu_ready", "abs_ready", "exp_ready", "log1p_ready", "suffix_ready", "exponent_ready")]
        s_mx, s_nm, s_ri = sem("max_ready"), sem("neg_max_ready"), sem("inverse_ready")
        s_w = sem("weights_ready")
        s_pv, s_oh, s_ol = sem("pv_ready"), sem("mix_hi_written"), sem("mix_lo_written")
        s_pj, s_pjh, s_pjl = sem("projected"), sem("proj_hi_written"), sem("proj_lo_written")
        s_cur, s_curv, s_pick = sem("qk_current"), sem("v_current"), sem("pick_current")

        def proj_unit(pe, u, pair):
            slot, h, k = u // 16, u // 8 % 2, u % 8
            if u % 16 == 0:
                pe.wait_ge(w_split[slot], feed_qkv.use(slot, pair) + 1)
            if k == 0:
                pe.wait_ge(s_pjl, 6 * pair + 2 * slot + h)
            wh, wl = w_hi[slot][:, k * P:(k + 1) * P], w_lo[slot][:, k * P:(k + 1) * P]
            for m, (w, a) in enumerate(((wh, xt_hi), (wh, xt_lo), (wl, xt_hi))):
                mm = pe.matmul(ps[:, 4, :], w, a[:, k, h * HALF:(h + 1) * HALF],
                               start=(k == 0 and m == 0), stop=(k == KT - 1 and m == 2))
            if k == KT - 1:
                mm.then_inc(s_pj, 1)

        def proj_v(pe, b, pair):
            if b == 0:
                pe.wait_ge(w_split[2], feed_qkv.use(2, pair) + 1)
            if b % 4 == 0:
                pe.wait_ge(s_pjl, 6 * pair + 4 + b // 4)
            for k in range(KT):
                for m, (a, w) in enumerate(((xt_hi, w_hi), (xt_lo, w_hi), (xt_hi, w_lo))):
                    mm = pe.matmul(ps[:, 4, b % 4 * P:(b % 4 + 1) * P], a[:, k, b * P:(b + 1) * P],
                                   w[2][:, k * P:(k + 1) * P],
                                   start=(k == 0 and m == 0), stop=(k == KT - 1 and m == 2))
            if b % 4 == 3:
                mm.then_inc(s_pj, 1)

        def proj_dst(e):
            if e < 4:
                hi, lo = ((nq_hi, nq_lo), (nk_hi, nk_lo))[e // 2]
                cols = slice(e % 2 * HALF, (e % 2 + 1) * HALF)
                return hi[:, cols], lo[:, cols], ps[:, 4, :]
            hv = e - 4
            return (nv_hi[:, 4 * hv:4 * hv + 4, :], nv_lo[:, 4 * hv:4 * hv + 4, :],
                    ps[:, 4, :].rearrange("p (b n) -> p b n", b=4))

        def proj_evac_hi(act, e, pair):
            hi, _, src = proj_dst(e)
            act.wait_ge(s_pj, 6 * pair + e + 1)
            if e == 0:
                act.wait_ge(s_cur, 4 * pair)
            if e == 4:
                act.wait_ge(s_curv, 2 * pair)
            act.activation(hi, src, ACT.Copy).then_inc(s_pjh, 1)

        def proj_evac_lo(dve, e, pair):
            hi, lo, src = proj_dst(e)
            dve.wait_ge(s_pjh, 6 * pair + e + 1)
            dve.tensor_tensor(lo, src, hi, ALU.subtract).then_inc(s_pjl, 1)

        def make_current_qk(dve, pair):
            if not isinstance(pair, int) or pair:
                dve.wait_ge(s_qk, STEPS * pair)
            dve.wait_ge(s_pjl, 6 * pair + 4)
            for dst, src in ((q_hi, nq_hi), (q_lo, nq_lo), (k_hi, nk_hi), (k_lo, nk_lo)):
                dve.tensor_copy(dst[:, :], src[:, :]).then_inc(s_cur, 1)

        def make_current_v(dve, pair):
            if not isinstance(pair, int) or pair:
                dve.wait_ge(s_pv, 4 * pair)
            dve.wait_ge(s_pjl, 6 * pair + 6)
            for dst, src in ((v_hi, nv_hi), (v_lo, nv_lo)):
                dve.tensor_copy(dst[:, :, :], src[:, :, :]).then_inc(s_curv, 1)

        def batch_list(t):
            i, at = query_block(t), batches_through(t) - (2 if query_block(t) >= 4 else 1)
            if i < 4:
                return [(at, 0, i + 1)]
            return [(at, 0, 4), (at + 1, 4, i - 3)]

        def group_end(t):
            return t % 8 // 4 if t % 4 == 3 else None

        class Turning:

            def __init__(self, tag, order, prob, pt_hi, pt_lo, weights, group_done):
                self.order, self.count = {k: n for n, k in enumerate(order)}, len(order)
                self.prob, self.pt_hi, self.pt_lo = prob, pt_hi, pt_lo
                self.weights, self.group_done = weights, group_done
                self.made = sem(f"{tag}_turned")
                self.hi = sem(f"{tag}_turned_hi")
                self.lo = sem(f"{tag}_turned_lo")
                assert self.count % 2 == 0

            def bank(self, key):
                return 5 + self.order[key] % 2

            def through(self, t):
                return self.order[batch_list(t)[-1][0]] + 1

            def turn(self, pe, t, pair):
                pe.wait_ge(self.weights, STEPS * pair + t + 1)
                for key, j0, m in batch_list(t):
                    n = self.order[key]
                    pe.wait_ge(self.lo, since(self.count * pair, n - 1))
                    for j in range(m):
                        mm = pe.transpose(ps[:, self.bank(key), j * P:(j + 1) * P],
                                          self.prob[t % 4][:, (j0 + j) * P:(j0 + j + 1) * P], ident[:, :])
                    mm.then_inc(self.made, 1)

            def views(self, t, key, j0, m):
                g, qs = t % 8 // 4, query_block(t) % 4 * P
                src = ps[:, self.bank(key), 0:m * P].rearrange("p (b n) -> p b n", b=m)
                return self.pt_hi[g][:, j0:j0 + m, qs:qs + P], self.pt_lo[g][:, j0:j0 + m, qs:qs + P], src

            def write_hi(self, act, t, pair):
                for key, j0, m in batch_list(t):
                    hi, _, src = self.views(t, key, j0, m)
                    if t % 4 == 0 and j0 == 0:
                        act.wait_ge(self.group_done, since(4 * pair, t // 4 - 1))
                    act.wait_ge(self.made, self.count * pair + self.order[key] + 1)
                    act.activation(hi, src, ACT.Copy).then_inc(self.hi, 1)

            def write_lo(self, dve, t, pair):
                for key, j0, m in batch_list(t):
                    hi, lo, src = self.views(t, key, j0, m)
                    dve.wait_ge(self.hi, self.count * pair + self.order[key] + 1)
                    dve.tensor_tensor(lo, src, hi, ALU.subtract).then_inc(self.lo, 1)

            def prob_free(self, pair, t):
                return since(self.count * pair, self.through(t - 4) if t >= 4 else 0)

        turning = Turning("att0", list(range(BATCHES)), prob, pt_hi, pt_lo, s_w, s_pv)

        def pair_tensor(pe, pair, kind, project):
            for slot in range(STEPS + 6):
                t = slot
                if t < STEPS:
                    i, hh = query_block(t), t // 8
                    n = (i + 1) * P
                    rows = slice(hh * HEAD_DIM, (hh + 1) * HEAD_DIM)
                    if t == 0:
                        pe.wait_ge(s_cur, 4 * (pair + 1))
                        if kind == "fox":
                            pe.wait_ge(s_pick, pair - N_SB // 2 + 1)
                    pe.wait_ge(s_sfree, since(STEPS * pair, t - 1))
                    for c in range(0, n, 512):
                        w = min(512, n - c)
                        bank = ps[:, 2 * (t % 2) + c // 512, :]
                        ends = c + w == n
                        qs = slice(i * P, (i + 1) * P)
                        parts = [(q_hi[rows, qs], k_hi[rows, c:c + w]), (q_lo[rows, qs], k_hi[rows, c:c + w]),
                                 (q_hi[rows, qs], k_lo[rows, c:c + w])]
                        for m, (a, b) in enumerate(parts):
                            mm = pe.matmul(bank[:, 0:w], a, b, start=(m == 0), stop=(m == 2 and kind == "sb" and not ends))
                        if kind == "fox":
                            mm = pe.matmul(bank[:, 0:w], pick_now[:, hh, :], cum_rows[:, c:c + w],
                                           start=False, stop=not ends)
                        if ends:
                            mask = mask_strict if kind == "sb" else mask_causal
                            mm = pe.matmul(bank[:, w - P:w], ident_b[:, :], mask[:, :], start=False, stop=True)
                    mm.then_inc(s_qk, 1)
                    if project:
                        proj_unit(pe, 2 * t, pair + 1)
                        proj_unit(pe, 2 * t + 1, pair + 1)
                elif project and t < STEPS + 4:
                    proj_v(pe, 2 * (t - STEPS), pair + 1)
                    proj_v(pe, 2 * (t - STEPS) + 1, pair + 1)
                done = slot - TR_LAG - 2
                if 0 <= done < STEPS and group_end(done) is not None:
                    hh, g = done // 8, group_end(done)
                    group = 2 * hh + g
                    if done == 3:
                        pe.wait_ge(s_curv, 2 * (pair + 1))
                    pe.wait_ge(turning.lo, turning.count * pair + turning.through(done))
                    pe.wait_ge(s_ol, 4 * pair + group)
                    jend = 8 if g == 0 else 4
                    for j in range(jend):
                        qs = max(0, j - 4) * P if g == 0 else j * P
                        parts = ((v_hi, pt_hi), (v_lo, pt_hi), (v_hi, pt_lo))
                        for m, (v, pt) in enumerate(parts):
                            mm = pe.matmul(ps[hh * 64:hh * 64 + 64, 7, qs:512], v[:, j, hh * 64:hh * 64 + 64],
                                           pt[g][:, j, qs:512], start=(j == 0 and m == 0),
                                           stop=(j == jend - 1 and m == 2), skip_group_check=True)
                    mm.then_inc(s_pv, 1)
                tr = slot - TR_LAG
                if 0 <= tr < STEPS:
                    turning.turn(pe, tr, pair)

        def mix_views(group, pair):
            hh, g = group // 2, group % 2
            rows, cols = slice(hh * 64, hh * 64 + 64), slice((1 - g) * 512, (1 - g) * 512 + 512)
            return mix_hi[rows, pair, cols], mix_lo[rows, pair, cols], ps[rows, 7, :]

        def group_of_slot(slot, lag):
            done = slot - lag
            if 0 <= done < STEPS and group_end(done) is not None:
                return 2 * (done // 8) + group_end(done)
            return None

        def pair_scalar(act, pair, kind, project):
            for slot in range(STEPS + 7):
                t = slot
                if project and slot in (4, 8, 12, 16, 18, 20):
                    proj_evac_hi(act, (4, 8, 12, 16, 18, 20).index(slot), pair + 1)
                if kind == "sb":
                    if t < STEPS:
                        n = (query_block(t) + 1) * P
                        act.wait_ge(s_qk, STEPS * pair + t + 1)
                        act.wait_ge(s_sub, since(STEPS * pair, t - 1))
                        act.activation(score_z[t % 2][:, 0:n], banks(2 * (t % 2))[:, 0:n], ACT.Copy,
                                       scale=SB_SCALE).then_inc(s_sfree, 1)
                    w = slot - 2
                    if 0 <= w < STEPS:
                        n = (query_block(w) + 1) * P
                        act.wait_ge(s_sub, STEPS * pair + w + 1)
                        act.activation(prob[w % 4][:, 0:n], prob[w % 4][:, 0:n], ACT.Exp).then_inc(s_w, 1)
                    if t < STEPS:
                        n = (query_block(t) + 1) * P
                        act.wait_ge(s_ab, STEPS * pair + t + 1)
                        act.activation(soft_a[t % 2][:, 0:n], soft_a[t % 2][:, 0:n], ACT.Exp,
                                       scale=-1.0).then_inc(s_e, 1)
                    ev = slot - EV_LAG
                    if 0 <= ev < STEPS:
                        turning.write_hi(act, ev, pair)
                    if t < STEPS:
                        act.wait_ge(s_e, STEPS * pair + t + 1)
                        act.activation(soft_a[t % 2][:, 0:n], soft_a[t % 2][:, 0:n], ACT.Ln,
                                       bias=1.0).then_inc(s_ln, 1)
                else:
                    if t < STEPS:
                        n = (query_block(t) + 1) * P
                        act.wait_ge(s_nm, STEPS * (pair - N_SB // 2) + t + 1)
                        act.wait_ge(turning.made, turning.prob_free(pair, t))
                        act.activation(prob[t % 4][:, 0:n], banks(2 * (t % 2))[:, 0:n], ACT.Exp, scale=SB_SCALE,
                                       bias=neg_max[:, t % 4:t % 4 + 1],
                                       accum_out=row_sum[:, t % 4:t % 4 + 1]).then_inc(s_sfree, 1)
                    ev = slot - EV_LAG
                    if 0 <= ev < STEPS:
                        turning.write_hi(act, ev, pair)
                group = group_of_slot(slot, 6)
                if group is not None:
                    hi, _, src = mix_views(group, pair)
                    act.wait_ge(s_pv, 4 * pair + group + 1)
                    act.activation(hi, src, ACT.Copy).then_inc(s_oh, 1)

        def pair_vector(dve, pair, kind, project):
            for slot in range(STEPS + 7):
                t = slot
                if project and slot in (4, 8, 12, 16, 18, 20):
                    proj_evac_lo(dve, (4, 8, 12, 16, 18, 20).index(slot), pair + 1)
                if project and slot == 17:
                    make_current_qk(dve, pair + 1)
                ev = slot - EV_LAG
                if kind == "sb":
                    if t < STEPS:
                        n = (query_block(t) + 1) * P
                        dve.wait_ge(s_sfree, STEPS * pair + t + 1)
                        dve.wait_ge(s_sc, since(STEPS * pair, t - 1))
                        z = score_z[t % 2][:, 0:n]
                        dve.scalar_tensor_tensor(soft_a[t % 2][:, 0:n], z, -1.0, z, ALU.mult,
                                                 ALU.max).then_inc(s_ab, 1)
                        dve.wait_ge(turning.made, turning.prob_free(pair, t))
                        dve.tensor_scalar(prob[t % 4][:, 0:n], score_z[t % 2][:, 0:n], 0.0, None,
                                          ALU.max).then_inc(s_r, 1)
                    if 0 <= ev < STEPS:
                        turning.write_lo(dve, ev, pair)
                    if t < STEPS:
                        dve.wait_ge(s_r, STEPS * pair + t + 1)
                        dve.wait_ge(s_ln, STEPS * pair + t + 1)
                        back = slice(n - 1, None, -1)
                        dve.tensor_tensor_scan(prob[t % 4][:, back], prob[t % 4][:, back], soft_a[t % 2][:, back],
                                               0.0, ALU.add, ALU.add).then_inc(s_sc, 1)
                else:
                    own = pair - N_SB // 2
                    if t < STEPS:
                        n = (query_block(t) + 1) * P
                        dve.wait_ge(s_qk, STEPS * pair + t + 1)
                        dve.tensor_reduce(row_max[:, t % 4:t % 4 + 1], banks(2 * (t % 2))[:, 0:n], AX.X,
                                          ALU.max).then_inc(s_mx, 1)
                    w = slot - 1
                    if 0 <= w < STEPS:
                        dve.wait_ge(s_sfree, STEPS * pair + w + 1)
                        dve.reciprocal(row_inv[:, w % 4:w % 4 + 1], row_sum[:, w % 4:w % 4 + 1]).then_inc(s_ri, 1)
                    if t < STEPS:
                        dve.wait_ge(s_mx, STEPS * own + t + 1)
                        dve.tensor_scalar(neg_max[:, t % 4:t % 4 + 1], row_max[:, t % 4:t % 4 + 1], -SB_SCALE, None,
                                          ALU.mult).then_inc(s_nm, 1)
                    if 0 <= w < STEPS:
                        n = (query_block(w) + 1) * P
                        dve.wait_ge(s_ri, STEPS * own + w + 1)
                        dve.tensor_scalar(prob[w % 4][:, 0:n], prob[w % 4][:, 0:n], row_inv[:, w % 4:w % 4 + 1], None,
                                          ALU.mult).then_inc(s_w, 1)
                    if 0 <= ev < STEPS:
                        turning.write_lo(dve, ev, pair)
                group = group_of_slot(slot, 6)
                if group is not None:
                    hi, lo, src = mix_views(group, pair)
                    dve.wait_ge(s_oh, 4 * pair + group + 1)
                    dve.tensor_tensor(lo, src, hi, ALU.subtract).then_inc(s_ol, 1)
            if project:
                make_current_v(dve, pair + 1)

        def split_qkv(pool, n, pair):
            pool.wait_ge(w_loaded[n], 16 * (feed_qkv.use(n, pair) + 1))
            pool.wait_ge(s_pj, 6 * (pair - 1) + 2 * (n + 1))
            pool.tensor_tensor(w_hi[n][:, :], w_stage[n][:, :], ones[:, 0:1].to_broadcast([P, KT * P]),
                               ALU.mult).then_inc(w_cast[n], 1)
            pool.wait_ge(w_cast[n], feed_qkv.use(n, pair) + 1)
            pool.tensor_tensor(w_lo[n][:, :], w_stage[n][:, :], w_hi[n][:, :], ALU.subtract).then_inc(w_split[n], 1)

        def pair_gpsimd_sb(pool, pair):
            for t in range(STEPS):
                n = (query_block(t) + 1) * P
                pool.wait_ge(s_sc, STEPS * pair + t + 1)
                pool.tensor_tensor(prob[t % 4][:, 0:n], score_z[t % 2][:, 0:n], prob[t % 4][:, 0:n],
                                   ALU.subtract).then_inc(s_sub, 1)
                if t == 9:
                    split_qkv(pool, 0, pair + 2)
            split_qkv(pool, 1, pair + 2)
            split_qkv(pool, 2, pair + 2)

        def pick_pair(pool, pair):
            pool.wait_ge(s_qk, STEPS * pair)
            pool.tensor_copy(pick_now[:, :, :],
                             cum_pick[:, bass.ds(2 * (pair - N_SB // 2), 2), :]).then_inc(s_pick, 1)

        with nc.Block() as block:
            @block.sync
            def _(sp):
                load_rest(sp, feed_qkv)
                load_first(sp, feed_o0)

            @block.gpsimd
            def _(pool):
                for n in range(3):
                    split_qkv(pool, n, 1)
                with pool.Fori(0, N_SB // 2) as pair:
                    pair_gpsimd_sb(pool, pair)
                with pool.Fori(N_SB // 2, N_PAIRS - 2) as pair:
                    pick_pair(pool, pair)
                    for n in range(3):
                        split_qkv(pool, n, pair + 2)
                with pool.Fori(N_PAIRS - 2, N_PAIRS) as pair:
                    pick_pair(pool, pair)

            @block.tensor
            def _(pe):
                for u in range(32):
                    proj_unit(pe, u, 0)
                for b in range(TB):
                    proj_v(pe, b, 0)
                with pe.Fori(0, N_SB // 2) as pair:
                    pair_tensor(pe, pair, "sb", True)
                with pe.Fori(N_SB // 2, N_PAIRS - 1) as pair:
                    pair_tensor(pe, pair, "fox", True)
                pair_tensor(pe, N_PAIRS - 1, "fox", False)

            @block.scalar
            def _(act):
                act.preload_act_table_set("natural_log_exp_and_others")
                for e in range(6):
                    proj_evac_hi(act, e, 0)
                with act.Fori(0, N_SB // 2) as pair:
                    pair_scalar(act, pair, "sb", True)
                with act.Fori(N_SB // 2, N_PAIRS - 1) as pair:
                    pair_scalar(act, pair, "fox", True)
                pair_scalar(act, N_PAIRS - 1, "fox", False)

            @block.vector
            def _(dve):
                for e in range(6):
                    proj_evac_lo(dve, e, 0)
                make_current_qk(dve, 0)
                make_current_v(dve, 0)
                with dve.Fori(0, N_SB // 2) as pair:
                    pair_vector(dve, pair, "sb", True)
                with dve.Fori(N_SB // 2, N_PAIRS - 1) as pair:
                    pair_vector(dve, pair, "fox", True)
                pair_vector(dve, N_PAIRS - 1, "fox", False)

        def back_and_norm(tag, feed, act_hi, act_lo, cuts, names, free_at, next_feed, load_x=None, final=None):
            pps = len(cuts)
            body = len(feed.pieces) // pps
            room = Room(free_at)
            yt = [room(f"yt{b}_{tag}", [P, SEQ], F32) for b in range(2)]
            g_rows = room(f"g_rows_{tag}", [P, D_MODEL], F32)
            b_rows = room(f"b_rows_{tag}", [P, D_MODEL], F32)
            s_gb, s_x = sem(f"{tag}_gb_loaded"), sem(f"{tag}_x_loaded")
            s_yt, s_yT, s_acc = sem(f"{tag}_yt_written"), sem(f"{tag}_yt_transposed"), sem(f"{tag}_accumulated")
            s_st, s_mv, s_sd, s_rs = [sem(f"{tag}_{n}") for n in ("stats", "moments", "deviation", "rstd")]
            s_n, s_g, s_b = sem(f"{tag}_normed"), sem(f"{tag}_scaled"), sem(f"{tag}_shifted")
            s_nt, s_nh, s_nl = sem(f"{tag}_norm_transposed"), sem(f"{tag}_norm_hi"), sem(f"{tag}_norm_lo")
            s_out = sem(f"{tag}_stored")

            def col_slice(strip):
                return bass.ds(strip * P, P)

            with nc.Block() as block:
                @block.sync
                def _(sp):
                    if load_x is not None:
                        sp.dma_start(x_res[:, :, :], load_x).then_inc(s_x, 16)
                    sp.dma_start(g_rows[:, :], names[0]).then_inc(s_gb, 16)
                    sp.dma_start(b_rows[:, :], names[1]).then_inc(s_gb, 16)
                    load_rest(sp, feed)
                    if next_feed is not None:
                        load_first(sp, next_feed)
                    if final is not None:
                        for b in range(TB):
                            sp.wait_ge(s_b, b + 1)
                            sp.dma_start(final[b], x_res[:, b, :]).then_inc(s_out, 16)
                        sp.wait_ge(s_out, 16 * TB)

                @block.gpsimd
                def _(pool):
                    split_all(pool, feed)
                    pool.wait_ge(s_gb, 32)
                    for b in range(TB):
                        pool.wait_ge(s_g, b + 1)
                        pool.tensor_tensor(x_res[:, b, :], x_res[:, b, :], b_rows[:, :], ALU.add).then_inc(s_b, 1)

                @block.tensor
                def _(pe):
                    def turn(i, r):
                        strip = body * i + r
                        pe.wait_ge(s_yt, strip + 1)
                        pe.wait_ge(s_acc, 2 * since(body * i, r - 1))
                        for b in range(TB):
                            mm = pe.transpose(ps[:, 4 + 2 * (r % 2) + b // 4, b % 4 * P:(b % 4 + 1) * P],
                                              yt[r % 2][:, b * P:(b + 1) * P], ident[:, :])
                        mm.then_inc(s_yT, 1)

                    with pe.Fori(0, feed.iters) as i:
                        for r in range(body):
                            pe.wait_ge(s_yt, since(body * i, r - 1))
                            for c, (a, b) in enumerate(cuts):
                                products(pe, feed, r * pps + c, i, 2 * (r % 2), act_hi, act_lo, a, b,
                                         c == 0, c == pps - 1)
                            if r:
                                turn(i, r - 1)
                        turn(i, body - 1)
                    if final is None:
                        for b in range(TB):
                            pe.wait_ge(s_b, b + 1)
                            pe.wait_ge(s_nl, max(2 * (b - 1), 0))
                            for k in range(KT):
                                mm = pe.transpose(ps[:, 2 * (b % 2) + k // 4, k % 4 * P:(k % 4 + 1) * P],
                                                  x_res[:, b, k * P:(k + 1) * P], ident[:, :])
                            mm.then_inc(s_nt, 1)

                @block.scalar
                def _(act):
                    with act.Fori(0, feed.iters) as i:
                        for r in range(body):
                            n = r * pps + pps - 1
                            act.wait_ge(w_used[feed.slot(n)], feed.used(n, i) + 1)
                            act.wait_ge(s_yT, since(body * i, r - 1))
                            act.activation(yt[r % 2][:, :], banks(2 * (r % 2)), ACT.Copy).then_inc(s_yt, 1)
                    act.wait_ge(s_mv, TB + 1)
                    act.activation(ln_rstd[:, :], ln_rstd[:, :], ACT.Sqrt).then_inc(s_sd, 1)
                    if final is None:
                        for b in range(TB):
                            act.wait_ge(s_nt, b + 1)
                            for h in range(2):
                                act.activation(xt_hi[:, 4 * h:4 * h + 4, b * P:(b + 1) * P],
                                               ps[:, 2 * (b % 2) + h, :].rearrange("p (k n) -> p k n", k=4),
                                               ACT.Copy).then_inc(s_nh, 1)

                @block.vector
                def _(dve):
                    if load_x is not None:
                        dve.wait_ge(s_x, 16)
                    with dve.Fori(0, feed.iters) as i:
                        for r in range(body):
                            dve.wait_ge(s_yT, body * i + r + 1)
                            for h in range(2):
                                cell = x_res[:, 4 * h:4 * h + 4, col_slice(body * i + r)]
                                dve.scalar_tensor_tensor(
                                    cell, cell, ALPHA,
                                    ps[:, 4 + 2 * (r % 2) + h, :].rearrange("p (b n) -> p b n", b=4),
                                    ALU.mult, ALU.add).then_inc(s_acc, 1)
                    dve.wait_ge(s_acc, 2 * body * feed.iters)
                    for b in range(TB):
                        for h in range(2):
                            dve.bn_stats(ln_stats[:, b, 6 * h:6 * h + 6], x_res[:, b, h * 512:(h + 1) * 512]).then_inc(s_st, 1)
                    for b in range(TB):
                        dve.wait_ge(s_st, 2 * (b + 1))
                        dve.bn_aggr(ln_mv[:, b, :], ln_stats[:, b, :]).then_inc(s_mv, 1)
                    dve.wait_ge(s_mv, TB)
                    dve.tensor_scalar(ln_rstd[:, :], ln_mv[:, :, 1], LN_EPS, None, ALU.add).then_inc(s_mv, 1)
                    dve.wait_ge(s_sd, 1)
                    dve.reciprocal(ln_rstd[:, :], ln_rstd[:, :]).then_inc(s_rs, 1)
                    dve.wait_ge(s_rs, 1)
                    dve.wait_ge(s_gb, 32)

                    def norm(b):
                        dve.tensor_scalar(x_res[:, b, :], x_res[:, b, :], ln_mv[:, b, 0:1], ln_rstd[:, b:b + 1],
                                          ALU.subtract, ALU.mult).then_inc(s_n, 1)

                    def lows(b):
                        for h in range(2):
                            dve.wait_ge(s_nh, 2 * b + h + 1)
                            dve.tensor_tensor(xt_lo[:, 4 * h:4 * h + 4, b * P:(b + 1) * P],
                                              ps[:, 2 * (b % 2) + h, :].rearrange("p (k n) -> p k n", k=4),
                                              xt_hi[:, 4 * h:4 * h + 4, b * P:(b + 1) * P],
                                              ALU.subtract).then_inc(s_nl, 1)

                    norm(0)
                    for b in range(TB):
                        if b + 1 < TB:
                            norm(b + 1)
                        dve.wait_ge(s_n, b + 1)
                        dve.tensor_tensor(x_res[:, b, :], x_res[:, b, :], g_rows[:, :], ALU.mult).then_inc(s_g, 1)
                        if final is None and b >= 2:
                            lows(b - 2)
                    if final is None:
                        lows(TB - 2)
                        lows(TB - 1)

        hroom = Room(arena)
        hid_hi = hroom("hid_hi", [P, FT, SEQ], BF16)
        hid_lo = hroom("hid_lo", [P, FT, SEQ], BF16)
        after_hid = hroom.at

        def feed_forward_up(tag, feed, conv_rows, next_feed):
            room = Room(after_hid)
            gate = [room(f"gate{a}_{tag}", [P, SEQ + 2], F32) for a in range(2)]
            conv = [room(f"conv{a}_{tag}", [P, SEQ], F32) for a in range(2)]
            conv_w = sb(f"conv_w_{tag}", [P, FT * 4], F32, 2560)
            assert keep.at <= 2560
            s_cw, s_zero = sem(f"{tag}_conv_w"), sem(f"{tag}_gate_pad")
            s_gt, s_cv, s_ge, s_hm, s_hh, s_hl = [sem(f"{tag}_{n}") for n in
                ("gate_copied", "conv_step", "gelu", "hidden", "hidden_hi", "hidden_lo")]

            with nc.Block() as block:
                @block.sync
                def _(sp):
                    sp.dma_start(conv_w[:, :], conv_rows).then_inc(s_cw, 16)
                    load_rest(sp, feed)
                    load_first(sp, next_feed)

                @block.gpsimd
                def _(pool):
                    for a in range(2):
                        pool.memset(gate[a][:, 0:2], 0.0).then_inc(s_zero, 1)
                    split_all(pool, feed)

                @block.tensor
                def _(pe):
                    with pe.Fori(0, feed.iters) as i:
                        for a in range(2):
                            pe.wait_ge(s_gt, 2 * i)
                            products(pe, feed, 2 * a, i, 4 * a, xt_hi, xt_lo, 0, KT, True, True)
                            pe.wait_ge(s_hm, 2 * i)
                            products(pe, feed, 2 * a + 1, i, 4 * a + 2, xt_hi, xt_lo, 0, KT, True, True)

                @block.scalar
                def _(act):
                    with act.Fori(0, feed.iters) as i:
                        for a in range(2):
                            act.wait_ge(w_used[2 * a], feed.used(2 * a, i) + 1)
                            act.wait_ge(s_cv, 3 * (2 * i))
                            act.activation(gate[a][:, 2:SEQ + 2], banks(4 * a), ACT.Copy).then_inc(s_gt, 1)
                            act.wait_ge(s_cv, 3 * (2 * i + a + 1))
                            act.activation(conv[a][:, :], conv[a][:, :], ACT.Gelu_apprx_tanh).then_inc(s_ge, 1)
                            act.wait_ge(s_hm, 2 * i + a + 1)
                            act.activation(hid_hi[:, 2 * i + a, :], conv[a][:, :], ACT.Copy).then_inc(s_hh, 1)

                @block.vector
                def _(dve):
                    dve.wait_ge(s_cw, 16)
                    dve.wait_ge(s_zero, 2)
                    with dve.Fori(0, feed.iters) as i:
                        for a in range(2):
                            m = 2 * i + a

                            def tap(j):
                                return conv_w[:, bass.ds(4 * m + j, 1)]

                            dve.wait_ge(s_gt, m + 1)
                            dve.wait_ge(s_hl, 2 * i)
                            dve.tensor_scalar(conv[a][:, :], gate[a][:, 0:SEQ], tap(0), tap(3), ALU.mult,
                                              ALU.add).then_inc(s_cv, 1)
                            dve.wait_ge(s_cv, 3 * m + 1)
                            dve.scalar_tensor_tensor(conv[a][:, :], gate[a][:, 1:SEQ + 1], tap(1), conv[a][:, :],
                                                     ALU.mult, ALU.add).then_inc(s_cv, 1)
                            dve.wait_ge(s_cv, 3 * m + 2)
                            dve.scalar_tensor_tensor(conv[a][:, :], gate[a][:, 2:SEQ + 2], tap(2), conv[a][:, :],
                                                     ALU.mult, ALU.add).then_inc(s_cv, 1)
                            dve.wait_ge(s_ge, m + 1)
                            dve.wait_ge(w_used[2 * a + 1], feed.used(2 * a + 1, i) + 1)
                            dve.tensor_tensor(conv[a][:, :], conv[a][:, :], banks(4 * a + 2), ALU.mult).then_inc(s_hm, 1)
                            dve.wait_ge(s_hh, m + 1)
                            dve.tensor_tensor(hid_lo[:, m, :], conv[a][:, :], hid_hi[:, m, :],
                                              ALU.subtract).then_inc(s_hl, 1)

        back_and_norm("o0", feed_o0, mix_hi, mix_lo, [(0, KT)], (t_in["l0_ln1_g"], t_in["l0_ln1_b"]),
                      arena + 32 * KB, feed_up0, load_x=t_in["x"])
        feed_forward_up("up0", feed_up0, t_in["l0_conv"], feed_down0)
        back_and_norm("dn0", feed_down0, hid_hi, hid_lo, DOWN_CUT, (t_in["l0_ln2_g"], t_in["l0_ln2_b"]),
                      after_hid, feed_small)

        clear_sems()

        span = [(i + 1) * P for i in range(TB)]
        at_of = [sum(span[:i]) for i in range(TB)]
        picky = [i for i in range(TB) if (i + 1) * P > TOPK]
        sc_at = {i: at_of[i] - at_of[picky[0]] for i in picky}
        room = Room(arena)
        lat_hi, lat_lo = [room(n, [P, 2, SEQ], BF16) for n in ("lat_hi", "lat_lo")]
        val_hi, val_lo = [room(n, [P, TB, LATENT], BF16) for n in ("val_hi", "val_lo")]
        hide = room("hide", [P, sum(span)], BF16)
        score = room("score", [P, sum(span[i] for i in picky)], F32)
        rope_q = [room(n, [ROPE, SEQ], F32) for n in ("rope_q_cos", "rope_q_sin")]
        after_score = room.at
        rope_i = [room(n, [P, SEQ], F32) for n in ("rope_i_cos", "rope_i_sin")]
        w_idx = room("w_idx", [P, TB, IDX_HEADS], F32)
        qi_hi, qi_lo = [room(n, [P, KT, SEQ], BF16) for n in ("qi_hi", "qi_lo")]
        ki_hi = [room(f"ki_hi{h}", [P, SEQ], BF16) for h in range(2)]
        ki_lo = [room(f"ki_lo{h}", [P, SEQ], BF16) for h in range(2)]
        strip_f = room("strip_f", [P, SEQ], F32)
        strip_w = room("strip_w", [P, SEQ], F32)
        relu = [strip_f, strip_w]

        s_tl5 = sem("tables_loaded")
        s_f5, s_c5, s_s5, s_a5, s_h5, s_l5 = [sem(n) for n in
            ("strip_copied", "strip_cos", "strip_sin", "strip_rotated", "strip_hi", "strip_lo")]
        s_v5h, s_v5l, s_w5, s_z5 = sem("val_hi_written"), sem("val_lo_written"), sem("w_idx_written"), sem("zeros_written")
        s_iq, s_ir, s_ia, s_i0 = sem("idx_product"), sem("idx_relu"), sem("idx_added"), sem("score_zeroed")

        def copy_strip(act, bank, kind, wait_prev):
            act.wait_ge(s_l5, wait_prev)
            src = banks(bank)
            swaps = {"idx": (0, 32, 64, 96), "lat": (0, 32), "plain": ()}[kind]
            for a in swaps:
                b = a + 32 if a % 64 == 0 else a - 32
                act.activation(strip_w[b:b + 32, :], src[a:a + 32, :], ACT.Copy)
            act.activation(strip_f[:, :], src, ACT.Copy).then_inc(s_f5, 1)

        with nc.Block() as block:
            def strip_kind(m):
                return "idx" if m == 0 or m >= 3 else ("lat" if m == 1 else "plain")

            @block.sync
            def _(sp):
                for t, tab in ((0, rope_i), (2, rope_q)):
                    for c in range(2):
                        rows = P if t == 0 else ROPE
                        sp.dma_start(tab[c][0:rows, :], tables[t + c][0:rows, :]).then_inc(s_tl5, 16)
                load_rest(sp, feed_small)
                load_first(sp, feed_qidx)
                load_rest(sp, feed_qidx)
                load_first(sp, feed_q)

            @block.gpsimd
            def _(pool):
                split_all(pool, feed_small)
                split_all(pool, feed_qidx)

            def v_strip(pe, n, cols, bank):
                slot = feed_small.slot(n)
                pe.wait_ge(w_split[slot], feed_small.use(n, 0) + 1)
                for b in range(TB):
                    for k in range(KT):
                        for m, (a, w) in enumerate(((xt_hi, w_hi), (xt_lo, w_hi), (xt_hi, w_lo))):
                            mm = pe.matmul(ps[:, bank + b // 4, b % 4 * cols:(b % 4 + 1) * cols],
                                           a[:, k, b * P:(b + 1) * P], w[slot][:, k * cols:(k + 1) * cols],
                                           start=(k == 0 and m == 0), stop=(k == KT - 1 and m == 2))
                mm.then_inc(w_used[slot], 1)

            @block.tensor
            def _(pe):
                for n in range(3):
                    products(pe, feed_small, n, 0, 2 * n, xt_hi, xt_lo, 0, KT, True, True)
                v_strip(pe, 3, P, 6)
                pe.wait_ge(s_f5, 1)
                v_strip(pe, 4, 80, 0)
                pe.wait_ge(s_f5, 3)
                with pe.Fori(0, feed_qidx.iters) as i:
                    for r in range(4):
                        pe.wait_ge(s_f5, 4 * i + r)
                        if r == 2:
                            pe.wait_ge(s_v5l, 2)
                        if r == 3:
                            pe.wait_ge(s_v5l, 4)
                            pe.wait_ge(s_w5, 2)
                        products(pe, feed_qidx, r, i, 2 * ((r + 1) % 4), xt_hi, xt_lo, 0, KT, True, True)
                pe.wait_ge(s_l5, 11 + 1)
                with pe.Fori(0, KT) as p:
                    for t in range(2 * len(picky)):
                        hh, i = t // len(picky), picky[t % len(picky)]
                        n = span[i]
                        pe.wait_ge(s_ir, since(2 * len(picky) * p, t - 3))
                        for c in range(0, n, 512):
                            w = min(512, n - c)
                            for m, (a, b) in enumerate(((qi_hi, ki_hi), (qi_lo, ki_hi), (qi_hi, ki_lo))):
                                mm = pe.matmul(ps[:, 2 * (t % 4) + c // 512, 0:w], a[:, p, i * P:(i + 1) * P],
                                               b[hh][:, c:c + w], start=(m == 0), stop=(m == 2))
                        mm.then_inc(s_iq, 1)

            @block.scalar
            def _(act):
                def write_hi(m, dsts):
                    act.wait_ge(s_a5, m + 1)
                    for d, rows in dsts:
                        ins = act.activation(d, strip_f[rows, :], ACT.Copy)
                    ins.then_inc(s_h5, 1)

                both = [(ki_hi[0][0:64, :], slice(0, 64)), (ki_hi[1][64:128, :], slice(64, 128))]
                for n in range(3):
                    act.wait_ge(w_used[feed_small.slot(n)], feed_small.used(n, 0) + 1)
                    copy_strip(act, 2 * n, strip_kind(n), (0, 2, 3)[n])
                    if n == 0:
                        act.wait_ge(s_z5, 4)
                        write_hi(0, both)
                    else:
                        write_hi(n, [(lat_hi[:, n - 1, :], slice(0, P))])
                act.wait_ge(w_used[3], feed_small.used(3, 0) + 1)
                for h in range(2):
                    act.activation(val_hi[:, 4 * h:4 * h + 4, 0:P],
                                   ps[:, 6 + h, :].rearrange("p (b n) -> p b n", b=4), ACT.Copy).then_inc(s_v5h, 1)
                act.wait_ge(w_used[0], feed_small.used(4, 0) + 1)
                for h in range(2):
                    src = ps[:, h, 0:320].rearrange("p (b n) -> p b n", b=4)
                    act.activation(w_idx[:, 4 * h:4 * h + 4, :], src[:, :, 64:80], ACT.Copy,
                                   scale=IDX_SCALE).then_inc(s_w5, 1)
                    act.activation(val_hi[:, 4 * h:4 * h + 4, P:LATENT], src[:, :, 0:64], ACT.Copy).then_inc(s_v5h, 1)
                with act.Fori(0, feed_qidx.iters) as i:
                    for r in range(4):
                        m = 3 + 4 * i + r
                        act.wait_ge(w_used[r], feed_qidx.used(r, i) + 1)
                        copy_strip(act, 2 * ((r + 1) % 4), "idx", m + 1)
                        act.wait_ge(s_a5, m + 1)
                        act.activation(qi_hi[:, 4 * i + r, :], strip_f[:, :], ACT.Copy).then_inc(s_h5, 1)
                act.wait_ge(s_l5, 12)
                with act.Fori(0, KT) as p:
                    for t in range(2 * len(picky)):
                        n = span[picky[t % len(picky)]]
                        act.wait_ge(s_iq, 2 * len(picky) * p + t + 1)
                        act.wait_ge(s_ia, since(2 * len(picky) * p, t - 1))
                        act.activation(relu[t % 2][:, 0:n], banks(2 * (t % 4))[:, 0:n], ACT.Relu).then_inc(s_ir, 1)

            @block.vector
            def _(dve):
                for h in range(2):
                    other = slice(64, 128) if h == 0 else slice(0, 64)
                    dve.memset(ki_hi[h][other, :], 0.0).then_inc(s_z5, 1)
                    dve.memset(ki_lo[h][other, :], 0.0).then_inc(s_z5, 1)
                dve.memset(score[:, :], 0.0).then_inc(s_i0, 1)
                dve.wait_ge(s_tl5, 64)

                def rotate(m, kind, rotated, tabs):
                    rows = {"idx": P, "lat": ROPE, "plain": 0}[kind]
                    dve.wait_ge(s_f5, m + 1)
                    if not rows:
                        dve.tensor_copy(tiny[:, 0:1], strip_f[:, 0:1]).then_inc(s_a5, 1)
                        return
                    f, w = strip_f[0:rows, :], strip_w[0:rows, :]
                    dve.tensor_tensor(f, f, tabs[0][0:rows, :], ALU.mult).then_inc(s_c5, 1)
                    dve.tensor_tensor(w, w, tabs[1][0:rows, :], ALU.mult).then_inc(s_s5, 1)
                    dve.wait_ge(s_c5, rotated + 1)
                    dve.wait_ge(s_s5, rotated + 1)
                    dve.tensor_tensor(f, f, w, ALU.add).then_inc(s_a5, 1)

                rotate(0, "idx", 0, rope_i)
                dve.wait_ge(s_h5, 1)
                dve.wait_ge(s_a5, 1)
                dve.tensor_tensor(ki_lo[0][0:64, :], strip_f[0:64, :], ki_hi[0][0:64, :], ALU.subtract).then_inc(s_l5, 1)
                dve.tensor_tensor(ki_lo[1][64:128, :], strip_f[64:128, :], ki_hi[1][64:128, :],
                                  ALU.subtract).then_inc(s_l5, 1)
                for n in (1, 2):
                    rotate(n, "lat" if n == 1 else "plain", n, rope_q)
                    dve.wait_ge(s_h5, n + 1)
                    dve.wait_ge(s_a5, n + 1)
                    dve.tensor_tensor(lat_lo[:, n - 1, :], strip_f[:, :], lat_hi[:, n - 1, :],
                                      ALU.subtract).then_inc(s_l5, 1)
                for h in range(2):
                    dve.wait_ge(s_v5h, h + 1)
                    dve.tensor_tensor(val_lo[:, 4 * h:4 * h + 4, 0:P],
                                      ps[:, 6 + h, :].rearrange("p (b n) -> p b n", b=4),
                                      val_hi[:, 4 * h:4 * h + 4, 0:P], ALU.subtract).then_inc(s_v5l, 1)
                for h in range(2):
                    dve.wait_ge(s_v5h, h + 3)
                    dve.tensor_tensor(val_lo[:, 4 * h:4 * h + 4, P:LATENT],
                                      ps[:, h, 0:320].rearrange("p (b n) -> p b n", b=4)[:, :, 0:64],
                                      val_hi[:, 4 * h:4 * h + 4, P:LATENT], ALU.subtract).then_inc(s_v5l, 1)
                with dve.Fori(0, feed_qidx.iters) as i:
                    for r in range(4):
                        m = 3 + 4 * i + r
                        rotate(m, "idx", m - 1, rope_i)
                        dve.wait_ge(s_h5, m + 1)
                        dve.tensor_tensor(qi_lo[:, 4 * i + r, :], strip_f[:, :], qi_hi[:, 4 * i + r, :],
                                          ALU.subtract).then_inc(s_l5, 1)
                dve.wait_ge(s_i0, 1)
                dve.wait_ge(s_w5, 2)
                with dve.Fori(0, KT) as p:
                    for t in range(2 * len(picky)):
                        hh, i = t // len(picky), picky[t % len(picky)]
                        cell = score[:, sc_at[i]:sc_at[i] + span[i]]
                        dve.wait_ge(s_ir, 2 * len(picky) * p + t + 1)
                        dve.wait_ge(s_ia, since(2 * len(picky) * p, t - len(picky) + 1))
                        dve.scalar_tensor_tensor(cell, relu[t % 2][:, 0:span[i]],
                                                 w_idx[:, i, bass.ds(2 * p + hh, 1)], cell,
                                                 ALU.mult, ALU.add).then_inc(s_ia, 1)

        q_dram = nc.dram_tensor("q_split", (2 * N_DSA, P, 2, SEQ), BF16, kind="Internal").ap()
        room = Room(after_score)
        best = room("best", [P, len(picky), 8], F32)
        qs_f = [room(f"qs_f{b}", [P, SEQ], F32) for b in range(4)]
        qs_w = [room(f"qs_w{b}", [ROPE, SEQ], F32) for b in range(2)]
        q_out = [room(f"q_out{b}", [P, 2, SEQ], BF16) for b in range(4)]
        s_cp, s_cw6, s_co, s_si, s_ro, s_qh, s_ql = [sem(n) for n in
            ("q_copied", "q_swapped", "q_cos", "q_sin", "q_rotated", "q_hi_written", "q_lo_written")]
        s_qst = [sem(f"q_stored{r}") for r in range(4)]
        s_top, s_rep, s_hide = sem("best_found"), sem("best_taken"), sem("hide_written")

        with nc.Block() as block:
            @block.sync
            def _(sp):
                def store(i):
                    for r in range(4):
                        sp.wait_ge(s_ql, 4 * i + r + 1)
                        sp.dma_start(q_dram[4 * i + r], q_out[r][:, :, :]).then_inc(s_qst[r], 16)

                with sp.Fori(1, feed_q.iters) as i:
                    for n in range(4):
                        load_piece(sp, feed_q, n, i)
                    store(i - 1)
                store(feed_q.iters - 1)
                load_first(sp, feed_o1)
                for r in range(4):
                    sp.wait_ge(s_qst[r], 16 * feed_q.iters)

            @block.tensor
            def _(pe):
                with pe.Fori(0, feed_q.iters) as i:
                    for r in range(4):
                        pe.wait_ge(s_cp, 4 * i)
                        products(pe, feed_q, r, i, 2 * r, xt_hi, xt_lo, 0, KT, True, True)

            @block.scalar
            def _(act):
                with act.Fori(0, feed_q.iters) as i:
                    for r in range(4):
                        act.wait_ge(w_loaded[r], 16 * (feed_q.use(r, i) + 1))
                        act.wait_ge(w_used[r], feed_q.used(r, i))
                        act.activation(w_hi[r][:, :], w_stage[r][:, :], ACT.Copy).then_inc(w_cast[r], 1)
                    for r in range(4):
                        act.wait_ge(w_used[r], feed_q.used(r, i) + 1)
                        act.wait_ge(s_ql, 4 * i)
                        if r % 2 == 0:
                            act.activation(qs_w[r // 2][32:64, :], banks(2 * r)[0:32, :], ACT.Copy)
                            act.activation(qs_w[r // 2][0:32, :], banks(2 * r)[32:64, :], ACT.Copy).then_inc(s_cw6, 1)
                        act.activation(qs_f[r][:, :], banks(2 * r), ACT.Copy).then_inc(s_cp, 1)
                        if r % 2 == 0:
                            act.wait_ge(s_ro, 2 * i + r // 2 + 1)
                        else:
                            act.wait_ge(s_cp, 4 * i + r + 1)
                        if r == 0:
                            for rr in range(4):
                                act.wait_ge(s_qst[rr], 16 * i)
                        act.activation(q_out[r][:, 0, :], qs_f[r][:, :], ACT.Copy).then_inc(s_qh, 1)

            @block.gpsimd
            def _(pool):
                with pool.Fori(0, feed_q.iters) as i:
                    for r in range(4):
                        pool.wait_ge(w_loaded[r], 16 * (feed_q.use(r, i) + 1))
                        pool.wait_ge(w_used[r], feed_q.used(r, i))
                        pool.wait_ge(w_cast[r], feed_q.use(r, i) + 1)
                        pool.tensor_tensor(w_lo[r][:, :], w_stage[r][:, :], w_hi[r][:, :], ALU.subtract).then_inc(w_split[r], 1)
                    for r in range(4):
                        if r % 2 == 0:
                            f, w = qs_f[r][0:ROPE, :], qs_w[r // 2][:, :]
                            m = 2 * i + r // 2
                            pool.wait_ge(s_cw6, m + 1)
                            pool.tensor_tensor(w, w, rope_q[1][:, :], ALU.mult).then_inc(s_si, 1)
                            pool.wait_ge(s_cp, 4 * i + r + 1)
                            pool.tensor_tensor(f, f, rope_q[0][:, :], ALU.mult).then_inc(s_co, 1)
                            pool.wait_ge(s_si, m + 1)
                            pool.wait_ge(s_co, m + 1)
                            pool.tensor_tensor(f, f, w, ALU.add).then_inc(s_ro, 1)
                        pool.wait_ge(s_qh, 4 * i + r + 1)
                        pool.tensor_tensor(q_out[r][:, 1, :], qs_f[r][:, :], q_out[r][:, 0, :],
                                           ALU.subtract).then_inc(s_ql, 1)

            @block.vector
            def _(dve):
                for i in picky:
                    end = sc_at[i] + span[i]
                    dve.memset(score[0:CHUNK, end - CHUNK:end], HIDDEN_SCORE).then_inc(s_rep, 1)
                with dve.Fori(0, TOPK // 8) as n:
                    wait_apart(dve, (s_rep, len(picky)), (s_rep, len(picky) * (n + 1)))
                    for c, i in enumerate(picky):
                        dve.max(best[:, c, :], score[:, sc_at[i]:sc_at[i] + span[i]]).then_inc(s_top, 1)
                    wait_apart(dve, (s_top, len(picky)), (s_top, len(picky) * (n + 1)))
                    for c, i in enumerate(picky):
                        cell = score[:, sc_at[i]:sc_at[i] + span[i]]
                        dve.match_replace(cell, best[:, c, :], cell, TAKEN_SCORE).then_inc(s_rep, 1)
                dve.wait_ge(s_rep, len(picky) * (TOPK // 8 + 1))
                for i in range(TB):
                    cell = hide[:, at_of[i]:at_of[i] + span[i]]
                    if i in picky:
                        dve.tensor_scalar(cell, score[:, sc_at[i]:sc_at[i] + span[i]], -2e38, MASKED, ALU.is_gt,
                                          ALU.mult).then_inc(s_hide, 1)
                    else:
                        dve.memset(cell, 0.0).then_inc(s_hide, 1)
                        dve.wait_ge(s_hide, i + 1)
                for i in range(TB):
                    if i not in picky:
                        end = at_of[i] + span[i]
                        dve.memset(hide[0:CHUNK, end - CHUNK:end], MASKED).then_inc(s_hide, 1)

        room = Room(arena + 8 * KB + 2 * TB * LATENT * 2 + (sum(span) * 2 + 31) // 32 * 32)
        at_prob = room.at
        prob7 = [room(f"prob7_{b}", [P, SEQ], F32) for b in range(4)]
        masked = [room(f"masked{b}", [P, SEQ], F32) for b in range(2)]
        q_now = [room(f"q_now{h}", [P, 2, 2, SEQ], BF16) for h in range(2)]
        pt7_hi = [room("pt7_hi0", [P, TB, 512], BF16), room("pt7_hi1", [P, TB // 2, 512], BF16)]
        pt7_lo = [room("pt7_lo0", [P, TB, 512], BF16), room("pt7_lo1", [P, TB // 2, 512], BF16)]
        ctx_hi, ctx_lo = [room(n, [P, 2, 512], BF16) for n in ("ctx_hi", "ctx_lo")]
        uv_hi, uv_lo = [room(n, [P, 2, N_DSA, 64], BF16) for n in ("uv_hi", "uv_lo")]
        uvn_hi, uvn_lo = [room(n, [P, 2, 2, 64], BF16) for n in ("uvn_hi", "uvn_lo")]
        uv_f = sb("uv_f", [P, 2, N_DSA, 64], F32, at_prob)

        s_uvl, s_uvh, s_uvs, s_uvn = sem("uv_loaded"), sem("uv_hi_written"), sem("uv_lo_written"), sem("uv_current")
        s_q7 = [sem(f"q_now_loaded{h}") for h in range(2)]
        t_qk, t_mx, t_nm, t_ex, t_ri, t_w = [sem(n) for n in
            ("lat_scores", "lat_masked_max", "lat_neg_max", "lat_exp", "lat_inverse", "lat_weights")]
        t_pv, t_ch, t_cl = sem("lat_context"), sem("lat_context_hi"), sem("lat_context_lo")

        def group_of(slot, lag):
            done = slot - lag
            if 0 <= done < STEPS and group_end(done) is not None:
                return 2 * (done // 8) + group_end(done)
            return None

        up_slot = [10, 15, 18, 22]

        def up_in(slot):
            return up_slot.index(slot) if slot in up_slot else None

        turns7 = []
        for slot in range(STEPS + 7):
            if up_in(slot) is not None:
                turns7.append(("up", up_in(slot)))
            if 0 <= slot - TR_LAG < STEPS:
                turns7 += [key for key, _, _ in batch_list(slot - TR_LAG)]
        turning7 = Turning("att1", turns7, prob7, pt7_hi, pt7_lo, t_w, t_pv)

        def up_views(group, pair):
            hh, g = group // 2, group % 2
            rows, cols = slice(hh * 64, hh * 64 + 64), slice((1 - g) * 512, (1 - g) * 512 + 512)
            return xt_hi[rows, pair, cols], xt_lo[rows, pair, cols], ps[rows, turning7.bank(("up", group)), :]

        def context_views(ct):
            rows, bank = (slice(0, P), 7) if ct == 0 else (slice(0, LATENT - P), 4)
            return ctx_hi[rows, ct, :], ctx_lo[rows, ct, :], ps[rows, bank, :]

        with nc.Block() as block:
            @block.sync
            def _(sp):
                def load_q(h, pair):
                    sp.dma_start(q_now[h][:, :, :, :],
                                 q_dram[bass.ds(4 * pair + 2 * h, 2)].rearrange("s p l t -> p s l t")
                                 ).then_inc(s_q7[h], 16)

                sp.dma_start(uv_f[:, :, :, :], t_in["l1_uv"]).then_inc(s_uvl, 16)
                load_q(0, 0)
                load_q(1, 0)
                with sp.Fori(1, N_PAIRS) as pair:
                    for h in range(2):
                        sp.wait_ge(t_qk, STEPS * (pair - 1) + 8 * (h + 1))
                        load_q(h, pair)

            @block.gpsimd
            def _(pool):
                pool.wait_ge(s_uvs, 1)
                with pool.Fori(0, N_PAIRS) as pair:
                    pool.wait_ge(turning7.made, turning7.count * pair)
                    for dst, src in ((uvn_hi, uv_hi), (uvn_lo, uv_lo)):
                        pool.tensor_copy(dst[:, :, :, :], src[:, :, bass.ds(2 * pair, 2), :]).then_inc(s_uvn, 1)

            @block.tensor
            def _(pe):
                with pe.Fori(0, N_PAIRS) as pair:
                    for slot in range(STEPS + 8):
                        t = slot
                        if t < STEPS:
                            i, hh = query_block(t), t // 8
                            n = span[i]
                            if t % 8 == 0:
                                pe.wait_ge(s_q7[hh], 16 * (pair + 1))
                            pe.wait_ge(t_mx, since(STEPS * pair, t - 1))
                            qs = slice(i * P, (i + 1) * P)
                            for c in range(0, n, 512):
                                w = min(512, n - c)
                                for kt in range(2):
                                    qh, ql = q_now[hh][:, kt, 0, qs], q_now[hh][:, kt, 1, qs]
                                    kh, kl = lat_hi[:, kt, c:c + w], lat_lo[:, kt, c:c + w]
                                    for m, (a, b) in enumerate(((qh, kh), (qh, kl), (ql, kh))):
                                        mm = pe.matmul(ps[:, 2 * (t % 2) + c // 512, 0:w], a, b,
                                                       start=(kt == 0 and m == 0), stop=(kt == 1 and m == 2))
                            mm.then_inc(t_qk, 1)
                        group = up_in(slot)
                        if group is not None:
                            hh = group // 2
                            if group == 0:
                                pe.wait_ge(s_uvn, 2 * (pair + 1))
                            pe.wait_ge(t_cl, 2 * (4 * pair + group + 1))
                            n = turning7.order[("up", group)]
                            pe.wait_ge(turning7.lo, since(turning7.count * pair, n - 1))
                            _, _, dst = up_views(group, pair)
                            for ct in range(2):
                                rows = slice(0, P) if ct == 0 else slice(0, LATENT - P)
                                uh, ul = uvn_hi[rows, ct, hh, :], uvn_lo[rows, ct, hh, :]
                                xh, xl = ctx_hi[rows, ct, :], ctx_lo[rows, ct, :]
                                for m, (a, b) in enumerate(((uh, xh), (uh, xl), (ul, xh))):
                                    mm = pe.matmul(dst, a, b, start=(ct == 0 and m == 0), stop=(ct == 1 and m == 2))
                            mm.then_inc(turning7.made, 1)
                        group = group_of(slot, 5)
                        if group is not None:
                            g, done = group % 2, slot - 5
                            pe.wait_ge(turning7.lo, turning7.count * pair + turning7.through(done))
                            pe.wait_ge(t_cl, 2 * (4 * pair + group))
                            jend = 8 if g == 0 else 4
                            for ct in range(2):
                                cols = slice(0, P) if ct == 0 else slice(P, LATENT)
                                _, _, dst = context_views(ct)
                                for j in range(jend):
                                    qs = max(0, j - 4) * P if g == 0 else j * P
                                    for m, (v, pt) in enumerate(((val_hi, pt7_hi), (val_hi, pt7_lo), (val_lo, pt7_hi))):
                                        mm = pe.matmul(dst[:, qs:512], v[:, j, cols], pt[g][:, j, qs:512],
                                                       start=(j == 0 and m == 0), stop=(j == jend - 1 and m == 2),
                                                       skip_group_check=True)
                            mm.then_inc(t_pv, 1)
                        if 0 <= slot - TR_LAG < STEPS:
                            turning7.turn(pe, slot - TR_LAG, pair)

            @block.scalar
            def _(act):
                act.wait_ge(s_uvl, 16)
                act.activation(uv_hi[:, :, :, :].rearrange("p a h n -> p (a h n)"),
                               uv_f[:, :, :, :].rearrange("p a h n -> p (a h n)"), ACT.Copy).then_inc(s_uvh, 1)
                act.wait_ge(s_uvs, 1)
                with act.Fori(0, N_PAIRS) as pair:
                    for slot in range(STEPS + 9):
                        t = slot
                        if t < STEPS:
                            n = span[query_block(t)]
                            act.wait_ge(t_nm, STEPS * pair + t + 1)
                            act.wait_ge(turning7.made, turning7.prob_free(pair, t))
                            act.activation(prob7[t % 4][:, 0:n], masked[t % 2][:, 0:n], ACT.Exp, scale=DSA_SCALE,
                                           bias=neg_max[:, t % 4:t % 4 + 1],
                                           accum_out=row_sum[:, t % 4:t % 4 + 1]).then_inc(t_ex, 1)
                        group = up_in(slot - 1)
                        if group is not None:
                            hi, _, src = up_views(group, pair)
                            act.wait_ge(turning7.made, turning7.count * pair + turning7.order[("up", group)] + 1)
                            act.activation(hi, src, ACT.Copy).then_inc(turning7.hi, 1)
                        if 0 <= slot - EV_LAG < STEPS:
                            turning7.write_hi(act, slot - EV_LAG, pair)
                        group = group_of(slot, 6)
                        if group is not None:
                            act.wait_ge(t_pv, 4 * pair + group + 1)
                            act.wait_ge(turning7.made, turning7.count * pair
                                        + (turning7.order[("up", group - 1)] + 1 if group else 0))
                            for ct in range(2):
                                hi, _, src = context_views(ct)
                                act.activation(hi, src, ACT.Copy).then_inc(t_ch, 1)

            @block.vector
            def _(dve):
                dve.wait_ge(s_uvh, 1)
                dve.tensor_tensor(uv_lo[:, :, :, :].rearrange("p a h n -> p (a h n)"),
                                  uv_f[:, :, :, :].rearrange("p a h n -> p (a h n)"),
                                  uv_hi[:, :, :, :].rearrange("p a h n -> p (a h n)"), ALU.subtract).then_inc(s_uvs, 1)
                with dve.Fori(0, N_PAIRS) as pair:
                    for slot in range(STEPS + 9):
                        t, w = slot, slot - 1
                        if t < STEPS:
                            i = query_block(t)
                            n = span[i]
                            wait_apart(dve, (t_qk, 1), (t_qk, STEPS * pair + t + 1),
                                       (t_ex, since(STEPS * pair, t - 1)))
                            dve.tensor_tensor_reduce(masked[t % 2][:, 0:n], banks(2 * (t % 2))[:, 0:n],
                                                     hide[:, at_of[i]:at_of[i] + n], 1.0, 3.0 * MASKED, ALU.add,
                                                     ALU.max, row_max[:, t % 4:t % 4 + 1]).then_inc(t_mx, 1)
                        if 0 <= w < STEPS:
                            dve.wait_ge(t_ex, STEPS * pair + w + 1)
                            dve.reciprocal(row_inv[:, w % 4:w % 4 + 1], row_sum[:, w % 4:w % 4 + 1]).then_inc(t_ri, 1)
                        if t < STEPS:
                            dve.wait_ge(t_mx, STEPS * pair + t + 1)
                            dve.tensor_scalar(neg_max[:, t % 4:t % 4 + 1], row_max[:, t % 4:t % 4 + 1], -DSA_SCALE,
                                              None, ALU.mult).then_inc(t_nm, 1)
                        if 0 <= w < STEPS:
                            n = span[query_block(w)]
                            dve.wait_ge(t_ri, STEPS * pair + w + 1)
                            dve.tensor_scalar(prob7[w % 4][:, 0:n], prob7[w % 4][:, 0:n], row_inv[:, w % 4:w % 4 + 1],
                                              None, ALU.mult).then_inc(t_w, 1)
                        group = up_in(slot - 1)
                        if group is not None:
                            hi, lo, src = up_views(group, pair)
                            dve.wait_ge(turning7.hi, turning7.count * pair + turning7.order[("up", group)] + 1)
                            dve.tensor_tensor(lo, src, hi, ALU.subtract).then_inc(turning7.lo, 1)
                        if 0 <= slot - EV_LAG < STEPS:
                            turning7.write_lo(dve, slot - EV_LAG, pair)
                        group = group_of(slot, 6)
                        if group is not None:
                            for ct in range(2):
                                hi, lo, src = context_views(ct)
                                dve.wait_ge(t_ch, 2 * (4 * pair + group) + ct + 1)
                                dve.tensor_tensor(lo, src, hi, ALU.subtract).then_inc(t_cl, 1)

        back_and_norm("o1", feed_o1, xt_hi, xt_lo, [(0, KT)], (t_in["l1_ln1_g"], t_in["l1_ln1_b"]),
                      arena, feed_up1)
        feed_forward_up("up1", feed_up1, t_in["l1_conv"], feed_down1)
        back_and_norm("dn1", feed_down1, hid_hi, hid_lo, DOWN_CUT, (t_in["l1_ln2_g"], t_in["l1_ln2_b"]),
                      after_hid, None, final=out)



def tiles(w, cols=P):
    k, n = w.shape
    return np.ascontiguousarray(w.reshape(k // P, P, n // cols, cols).transpose(2, 1, 0, 3).reshape(n // cols, P, -1))


def rotary_order():
    return np.array(list(range(0, 8)) + list(range(16, 40)) + list(range(8, 16)) + list(range(40, 64)))


def rope_row_constants():
    rows = np.zeros((P, 4), np.float32)
    for r in range(P):
        half, u = IDX_DIM // 8, r % 32
        if u < half:
            rows[r, 0] = np.float32(THETA) ** np.float32(-u / half)
            rows[r, 1] = -1.0 if r % 64 < 32 else 1.0
        if r < ROPE:
            half = KEY_DIM // 8
            rows[r, 2] = np.float32(THETA) ** np.float32(-(r % 32) / half)
            rows[r, 3] = -1.0 if r < 32 else 1.0
    return rows


def kernel(**inputs):
    import concourse.bacc as bacc
    from concourse.bass_utils import run_bass_kernel_spmd

    a = {k: np.asarray(v) for k, v in inputs.items()}
    c = np.ascontiguousarray
    x = a["x"][0]
    d = {}
    d["x"] = c(x.reshape(TB, P, D_MODEL).transpose(1, 0, 2))
    d["xt"] = c(x.T.reshape(KT, P, SEQ).transpose(1, 0, 2))
    d["positions"] = c(np.broadcast_to(a["positions"], (P, SEQ)))
    d["rope_rows"] = rope_row_constants()
    w = a["l0_w_in"]
    s = tiles(w[:, :3072])
    d["l0_qkv"] = c(s.reshape(2, 3, 4, P, -1).transpose(0, 2, 1, 3, 4).reshape(24, P, -1))
    d["l0_wf"] = c(w[:, 3072:].reshape(KT, P, 8).transpose(1, 0, 2))
    d["l0_bf"] = c(a["l0_b_f"].reshape(8, 1))
    d["l0_o"] = tiles(a["l0_w_o"])
    w = a["l1_w_in"]
    c0 = N_DSA * KEY_DIM
    c2 = c0 + ROPE + LATENT
    c3 = c2 + IDX_HEADS * IDX_DIM
    c4 = c3 + IDX_DIM
    order = rotary_order()
    d["l1_q"] = tiles(w[:, :c0])
    d["l1_qidx"] = tiles(w[:, c2:c3].reshape(D_MODEL, IDX_HEADS, IDX_DIM)[:, :, order].reshape(D_MODEL, -1))
    kidx = w[:, c3:c4][:, order]
    d["l1_kidx"] = tiles(np.concatenate([kidx, kidx], 1))[0]
    d["l1_klat0"], d["l1_klat1"] = tiles(w[:, c0:c2])
    lat = w[:, c0 + ROPE:c2]
    d["l1_v128"] = tiles(lat[:, :P])[0]
    d["l1_v64w"] = tiles(np.concatenate([lat[:, P:], w[:, c4:]], 1), 80)[0]
    uv = np.zeros((2, P, N_DSA, 64), np.float32)
    wuv = a["l1_w_uv"].transpose(1, 0, 2)
    uv[0], uv[1, :LATENT - P] = wuv[:P], wuv[P:]
    d["l1_uv"] = c(uv.transpose(1, 0, 2, 3))
    d["l1_o"] = tiles(a["l1_w_o"])
    for n in range(2):
        up = tiles(a[f"l{n}_w_up"])
        d[f"l{n}_up"] = c(up.reshape(2, FT, P, -1).transpose(1, 0, 2, 3).reshape(2 * FT, P, -1))
        conv = np.concatenate([a[f"l{n}_conv_w"], a[f"l{n}_conv_b"][None]])
        d[f"l{n}_conv"] = c(conv.reshape(4, FT, P).transpose(2, 1, 0).reshape(P, -1))
        d[f"l{n}_down"] = tiles(a[f"l{n}_w_down"])
        for m in (1, 2):
            for q in "gb":
                d[f"l{n}_ln{m}_{q}"] = c(np.broadcast_to(a[f"l{n}_ln{m}_{q}"], (P, D_MODEL)))

    nc = bacc.Bacc("TRN2", target_bir_lowering=False, num_devices=1)
    arrays, t_in = {}, {}
    for name, v in d.items():
        arrays[f"in_{name}"] = v
        t_in[name] = nc.dram_tensor(f"in_{name}", v.shape, mybir.dt.from_np(v.dtype), kind="ExternalInput").ap()
    out = nc.dram_tensor("out", (TB, P, D_MODEL), F32, kind="ExternalOutput").ap()
    program(nc, t_in, out)
    r = run_bass_kernel_spmd(nc, [arrays], core_ids=[0])
    return r.results[0]["out"].reshape(1, SEQ, D_MODEL)
```

```python
import numpy as np
from contextlib import ExitStack

import concourse.bass as bass
from concourse import mybir

F32 = mybir.dt.float32
BF16 = mybir.dt.bfloat16
I32 = mybir.dt.int32
ALU = mybir.AluOpType
ACT = mybir.ActivationFunctionType
AX = mybir.AxisListType

P = 128
D_MODEL = 1024
SEQ = 1024
DEPTH = 2
KT = D_MODEL // P
TB = SEQ // P
HALF = SEQ // 2
CHUNK = 64
HEAD_DIM = 64
N_SB = 8
N_FOX = 8
N_PAIRS = (N_SB + N_FOX) // 2
N_DSA = 16
LATENT = 192
ROPE = 64
KEY_DIM = ROPE + LATENT
IDX_HEADS = 16
IDX_DIM = 64
TOPK = min(256, SEQ // 4)
IDX_SCALE = float(IDX_HEADS * IDX_DIM) ** -0.5
SB_SCALE = float(HEAD_DIM) ** -0.5
DSA_SCALE = float(KEY_DIM) ** -0.5
THETA = 500000.0
D_FF = 2816
FT = D_FF // P
ALPHA = float((2 * DEPTH) ** 0.25)
LN_EPS = 1e-5
MASKED = -1e30
HIDDEN_SCORE = -1e38
TAKEN_SCORE = -3e38
SLOTS = 4
DOWN_CUT = [(0, 6), (6, 12), (12, 17), (17, 22)]
STEPS = 16
TR_LAG = 3
EV_LAG = 4

assert SEQ % P == 0 and D_FF % P == 0 and N_DSA == 2 * N_PAIRS


def query_block(t):
    return TB - 1 - t % TB


def batches_through(t):
    return sum(2 if query_block(s) >= 4 else 1 for s in range(t + 1))


BATCHES = batches_through(STEPS - 1)


def since(first, n):
    return first + max(n, 0)


def lagged(pair, slot, lag):
    return (pair, slot - lag) if slot >= lag else (pair - 1, slot - lag + STEPS)


def wait_if(eng, semaphore, value):
    if not isinstance(value, int) or value > 0:
        eng.wait_ge(semaphore, value)


def wait_apart(eng, always, *waits):
    values = [(s, v if isinstance(v, int) else eng.to_reg(v)) for s, v in waits]
    eng.wait_ge(*always)
    for s, v in values:
        wait_if(eng, s, v)


class Feed:

    def __init__(self, uses, used, dram, pieces, iters, counted=True):
        self.dram, self.pieces, self.iters = dram, pieces, iters
        self.base, self.used_base = dict(uses), dict(used)
        self.order, self.per_iter = [], {s: 0 for s in range(SLOTS)}
        for slot, _ in pieces:
            self.order.append(self.per_iter[slot])
            self.per_iter[slot] += 1
        for s in range(SLOTS):
            uses[s] += iters * self.per_iter[s]
            if counted:
                used[s] += iters * self.per_iter[s]

    def slot(self, n):
        return self.pieces[n][0]

    def use(self, n, i):
        slot = self.slot(n)
        return self.base[slot] + i * self.per_iter[slot] + self.order[n]

    def used(self, n, i):
        slot = self.slot(n)
        return self.used_base[slot] + i * self.per_iter[slot] + self.order[n]


def program(nc, t_in, out):
    with ExitStack() as ctx:
        start = (nc.sbuf_base + 63) // 64 * 64
        KB = 1024
        limit = nc.sbuf_usable_end - start

        def sb(name, shape, dt, at):
            size = int(np.prod(shape[1:])) * (2 if dt == BF16 else 4)
            assert at + size <= limit, (name, at + size, limit)
            return nc.alloc_sbuf_tensor_at(name, shape, dt, offset=start + at)

        class Room:

            def __init__(self, at):
                self.at = at

            def __call__(self, name, shape, dt):
                t = sb(name, shape, dt, self.at)
                self.at += (int(np.prod(shape[1:])) * (2 if dt == BF16 else 4) + 31) // 32 * 32
                return t

        layer_sems = []

        def sem(name):
            layer_sems.append(nc.alloc_semaphore(name))
            return layer_sems[-1]

        def clear_sems():
            nc.clear_and_free_semaphores(layer_sems)
            layer_sems.clear()
            nc.all_engine_barrier(sem_only=True)

        keep = Room(0)
        ident = keep("ident", [P, P], F32)
        ident_b = keep("ident_b", [P, P], BF16)
        mask_strict = keep("mask_strict", [P, P], BF16)
        mask_causal = keep("mask_causal", [P, P], BF16)
        ln_stats = keep("ln_stats", [P, TB, 12], F32)
        ln_mv = keep("ln_mv", [P, TB, 2], F32)
        ln_rstd = keep("ln_rstd", [P, TB], F32)
        row_max = keep("row_max", [P, 4], F32)
        neg_max = keep("neg_max", [P, 4], F32)
        row_sum = keep("row_sum", [P, 4], F32)
        row_inv = keep("row_inv", [P, 4], F32)
        tiny = keep("tiny", [P, 8], F32)
        ones = keep("ones", [P, 1], F32)
        assert keep.at <= 3 * KB
        wroom = Room(3 * KB)
        w_stage = [wroom(f"w_stage{s}", [P, KT * P], F32) for s in range(SLOTS)]
        w_hi = [wroom(f"w_hi{s}", [P, KT * P], BF16) for s in range(SLOTS)]
        w_lo = [wroom(f"w_lo{s}", [P, KT * P], BF16) for s in range(SLOTS)]
        xt_hi = wroom("xt_hi", [P, KT, SEQ], BF16)
        xt_lo = wroom("xt_lo", [P, KT, SEQ], BF16)
        res_at = wroom.at
        x_res = wroom("x_res", [P, TB, D_MODEL], F32)
        arena = wroom.at

        ps = ctx.enter_context(nc.psum_tensor("ps", [P, 8, 512], F32))

        def banks(b):
            return ps[:, b:b + 2, :].rearrange("p a n -> p (a n)")

        w_loaded = [sem(f"w_loaded{s}") for s in range(SLOTS)]
        w_cast = [sem(f"w_cast{s}") for s in range(SLOTS)]
        w_split = [sem(f"w_split{s}") for s in range(SLOTS)]
        w_used = [sem(f"w_used{s}") for s in range(SLOTS)]
        layer_sems.clear()
        uses = {s: 0 for s in range(SLOTS)}
        used = {s: 0 for s in range(SLOTS)}

        feed_qkv = Feed(uses, used, lambda n, i: t_in["l0_qkv"][3 * i + n], [(0, 1024), (1, 1024), (2, 1024)],
                        N_PAIRS, counted=False)

        def strips(name, per_body, iters):
            return Feed(uses, used, lambda n, i: t_in[name][per_body * i + n],
                        [(n, KT * P) for n in range(per_body)], iters)

        def down(name):
            def dram(n, i):
                a, b = DOWN_CUT[n % 4]
                return t_in[name][2 * i + n // 4][:, a * P:b * P]
            return Feed(uses, used, dram,
                        [(n % 4, (DOWN_CUT[n % 4][1] - DOWN_CUT[n % 4][0]) * P) for n in range(8)], KT // 2)

        feed_o0 = strips("l0_o", 4, 2)
        feed_up0 = strips("l0_up", 4, FT // 2)
        feed_down0 = down("l0_down")
        small_cols = [1024, 1024, 1024, 1024, KT * 80]
        small_names = ["l1_kidx", "l1_klat0", "l1_klat1", "l1_v128", "l1_v64w"]
        feed_small = Feed(uses, used, lambda n, i: t_in[small_names[n]],
                          [(s, c) for s, c in zip([0, 1, 2, 3, 0], small_cols)], 1)
        feed_qidx = strips("l1_qidx", 4, 2)
        feed_q = strips("l1_q", 4, 8)
        feed_o1 = strips("l1_o", 4, 2)
        feed_up1 = strips("l1_up", 4, FT // 2)
        feed_down1 = down("l1_down")

        def load_piece(sp, feed, n, i):
            slot, cols = feed.pieces[n]
            sp.wait_ge(w_split[slot], feed.use(n, i))
            sp.dma_start(w_stage[slot][:, 0:cols], feed.dram(n, i)).then_inc(w_loaded[slot], 16)

        def load_first(sp, feed):
            for n in range(len(feed.pieces)):
                if feed.order[n] == 0:
                    load_piece(sp, feed, n, 0)

        def load_rest(sp, feed):
            for n in range(len(feed.pieces)):
                if feed.order[n] > 0:
                    load_piece(sp, feed, n, 0)
            if feed.iters > 1:
                with sp.Fori(1, feed.iters) as i:
                    for n in range(len(feed.pieces)):
                        load_piece(sp, feed, n, i)

        def split_piece(pool, feed, n, i):
            slot, cols = feed.pieces[n]
            pool.wait_ge(w_loaded[slot], 16 * (feed.use(n, i) + 1))
            pool.wait_ge(w_used[slot], feed.used(n, i))
            pool.tensor_tensor(w_hi[slot][:, 0:cols], w_stage[slot][:, 0:cols], ones[:, 0:1].to_broadcast([P, cols]),
                               ALU.mult).then_inc(w_cast[slot], 1)
            pool.wait_ge(w_cast[slot], feed.use(n, i) + 1)
            pool.tensor_tensor(w_lo[slot][:, 0:cols], w_stage[slot][:, 0:cols], w_hi[slot][:, 0:cols],
                               ALU.subtract).then_inc(w_split[slot], 1)

        def split_all(pool, feed):
            if feed.iters == 1:
                for n in range(len(feed.pieces)):
                    split_piece(pool, feed, n, 0)
            else:
                with pool.Fori(0, feed.iters) as i:
                    for n in range(len(feed.pieces)):
                        split_piece(pool, feed, n, i)

        def products(pe, feed, n, i, bank, act_hi, act_lo, k0, k1, first, last):
            slot = feed.slot(n)
            pe.wait_ge(w_split[slot], feed.use(n, i) + 1)
            for k in range(k0, k1):
                wh = w_hi[slot][:, (k - k0) * P:(k - k0 + 1) * P]
                wl = w_lo[slot][:, (k - k0) * P:(k - k0 + 1) * P]
                for m, (w, a) in enumerate(((wh, act_hi), (wh, act_lo), (wl, act_hi))):
                    for h in range(2):
                        mm = pe.matmul(ps[:, bank + h, :], w, a[:, k, h * HALF:(h + 1) * HALF],
                                       start=(first and k == k0 and m == 0),
                                       stop=(last and k == k1 - 1 and m == 2))
            mm.then_inc(w_used[slot], 1)

        room = Room(arena)
        xt_f = room("xt_f", [P, KT, SEQ], F32)
        pos_i = room("pos_i", [P, SEQ], I32)
        pos_f = room("pos_f", [P, SEQ], F32)
        angle = room("angle", [P, SEQ], F32)
        turns = room("turns", [P, SEQ], F32)
        rope_c = room("rope_c", [P, SEQ], F32)
        rope_s = room("rope_s", [P, SEQ], F32)
        rope_rows = room("rope_rows", [P, 4], F32)
        wf_f = room("wf_f", [P, KT, 8], F32)
        wf_hi = room("wf_hi", [P, KT, 8], BF16)
        wf_lo = room("wf_lo", [P, KT, 8], BF16)
        gate_b = room("gate_b", [8, 1], F32)
        low = Room(res_at)
        cum_rows = low("cum_rows", [96, SEQ], BF16)
        cum_pick = low("cum_pick", [96, N_FOX, P], BF16)
        gate_x = low("gate_x", [8, SEQ], F32)
        gate_a = low("gate_a", [8, SEQ], F32)
        gate_m = low("gate_m", [8, SEQ], F32)
        gate_c = low("gate_c", [8, SEQ], F32)
        gate_p = low("gate_p", [8, SEQ], BF16)
        tables = nc.dram_tensor("rope_tables", (4, P, SEQ), F32, kind="Internal").ap()
        s_pos, s_wf = sem("pos_loaded"), sem("wf_loaded")
        s_xt = [sem(f"xt_loaded{k}") for k in range(KT)]
        s_xh, s_xl = sem("xt_hi_written"), sem("xt_lo_written")
        s_const = sem("const_step")
        s_wfh, s_wfl = sem("wf_hi_written"), sem("wf_lo_written")
        s_tab, s_sin, s_tabst = sem("table_step"), sem("table_sin"), sem("table_stored")
        s_gmm, s_gact, s_gdve = sem("gate_product"), sem("gate_act"), sem("gate_dve")
        inv_2pi = float(np.float32(1 / (2 * np.pi)))
        pi_a = 6.28125
        rest = 2 * np.pi - pi_a
        pi_b = float(np.floor(rest * 2 ** 17) / 2 ** 17)
        pi_c = float(np.float32(rest - pi_b))
        magic = 1.5 * 2 ** 23
        pi_max = 3.1415925

        with nc.Block() as block:
            @block.sync
            def _(sp):
                sp.dma_start(pos_i[:, :], t_in["positions"]).then_inc(s_pos, 16)
                sp.dma_start(rope_rows[:, :], t_in["rope_rows"]).then_inc(s_pos, 16)
                for k in range(0, KT, 2):
                    sp.dma_start(xt_f[:, k, :], t_in["xt"][:, k, :]).then_inc(s_xt[k], 16)
                load_first(sp, feed_qkv)
                for t in range(2):
                    for c in range(2):
                        sp.wait_ge(s_tab, 11 * t + (10 if c == 0 else 11))
                        sp.dma_start(tables[2 * t + c], (rope_c if c == 0 else rope_s)[:, :]).then_inc(s_tabst, 16)
                sp.wait_ge(s_tabst, 64)

            @block.scalar
            def _(act):
                act.dma_start(wf_f[:, :, :], t_in["l0_wf"]).then_inc(s_wf, 16)
                act.dma_start(gate_b[:, :], t_in["l0_bf"]).then_inc(s_wf, 16)
                for k in range(1, KT, 2):
                    act.dma_start(xt_f[:, k, :], t_in["xt"][:, k, :]).then_inc(s_xt[k], 16)
                for t in range(2):
                    act.wait_ge(s_tab, 11 * t + 8)
                    if t:
                        act.wait_ge(s_tabst, 32)
                    act.activation(rope_s[:, :], angle[:, :], ACT.Sin).then_inc(s_sin, 1)
                    act.activation(rope_c[:, :], angle[:, :], ACT.Sin, scale=0.5).then_inc(s_sin, 1)
                for k in range(KT):
                    act.wait_ge(s_xt[k], 16)
                    act.activation(xt_hi[:, k, :], xt_f[:, k, :], ACT.Copy).then_inc(s_xh, 1)
                act.preload_act_table_set("natural_log_exp_and_others")
                act.wait_ge(s_gmm, 1)
                act.wait_ge(s_wf, 32)
                act.activation(gate_x[:, :], banks(0)[0:8, :], ACT.Identity, bias=gate_b[:, 0:1]).then_inc(s_gact, 1)
                act.wait_ge(s_gact, 1)
                act.activation(gate_a[:, :], gate_x[:, :], ACT.Abs).then_inc(s_gact, 1)
                act.wait_ge(s_gact, 2)
                act.activation(gate_a[:, :], gate_a[:, :], ACT.Exp, scale=-1.0).then_inc(s_gact, 1)
                act.wait_ge(s_gact, 3)
                act.activation(gate_a[:, :], gate_a[:, :], ACT.Ln, bias=1.0).then_inc(s_gact, 1)

            @block.gpsimd
            def _(pool):
                steps = 0

                def done(ins):
                    nonlocal steps
                    steps += 1
                    ins.then_inc(s_const, 1)

                done(pool.memset(ident[:, :], 0.0))
                done(pool.memset(ident_b[:, :], 0.0))
                done(pool.memset(mask_strict[:, :], 0.0))
                done(pool.memset(mask_causal[:, :], 0.0))
                done(pool.memset(cum_pick[:, :, :], 0.0))
                done(pool.memset(cum_rows[:, :], 0.0))
                done(pool.memset(ones[:, :], 1.0))
                pool.wait_ge(s_const, 7)
                for m in (ident, ident_b):
                    done(pool.affine_select(out=m[:, :], in_=m[:, :], compare_op=ALU.not_equal, fill=1.0,
                                            base=0, pattern=[[-1, P]], channel_multiplier=1))
                done(pool.affine_select(out=mask_strict[:, :], in_=mask_strict[:, :], compare_op=ALU.is_gt,
                                        fill=MASKED, base=0, pattern=[[-1, P]], channel_multiplier=1))
                done(pool.affine_select(out=mask_causal[:, :], in_=mask_causal[:, :], compare_op=ALU.is_ge,
                                        fill=MASKED, base=0, pattern=[[-1, P]], channel_multiplier=1))
                for r in range(3):
                    done(pool.affine_select(out=cum_pick[:, :, :], in_=cum_pick[:, :, :],
                                            compare_op=ALU.not_equal, fill=-1.0 / SB_SCALE, base=-32 * r,
                                            pattern=[[-1, N_FOX], [0, P]], channel_multiplier=1))
                    pool.wait_ge(s_const, steps)
                pool.wait_ge(s_wf, 32)
                pool.tensor_copy(wf_hi[:, :, :], wf_f[:, :, :]).then_inc(s_wfh, 1)
                pool.wait_ge(s_wfh, 1)
                pool.tensor_tensor(wf_lo[:, :, :], wf_f[:, :, :], wf_hi[:, :, :], ALU.subtract).then_inc(s_wfl, 1)
                split_piece(pool, feed_qkv, 0, 0)
                split_piece(pool, feed_qkv, 1, 0)
                split_piece(pool, feed_qkv, 2, 0)

            @block.tensor
            def _(pe):
                pe.wait_ge(s_wfl, 1)
                for k in range(KT):
                    pe.wait_ge(s_xl, k + 1)
                    for h in range(2):
                        for m, (w, a) in enumerate(((wf_hi, xt_hi), (wf_hi, xt_lo), (wf_lo, xt_hi))):
                            mm = pe.matmul(ps[0:8, h, :], w[:, k, :], a[:, k, h * HALF:(h + 1) * HALF],
                                           start=(k == 0 and m == 0), stop=(k == KT - 1 and m == 2))
                mm.then_inc(s_gmm, 1)

            @block.vector
            def _(dve):
                dve.wait_ge(s_pos, 32)
                step = 0

                def then(ins):
                    nonlocal step
                    step += 1
                    ins.then_inc(s_tab, 1)
                    dve.wait_ge(s_tab, step)

                for t in range(2):
                    if t == 0:
                        then(dve.tensor_copy(pos_f[:, :], pos_i[:, :]))
                    else:
                        then(dve.tensor_copy(tiny[:, 0:1], rope_rows[:, 0:1]))
                    then(dve.tensor_scalar(angle[:, :], pos_f[:, :], rope_rows[:, 2 * t:2 * t + 1], None, ALU.mult))
                    then(dve.tensor_scalar(turns[:, :], angle[:, :], inv_2pi, magic, ALU.mult, ALU.add))
                    then(dve.tensor_scalar(turns[:, :], turns[:, :], -magic, None, ALU.add))
                    for c in (pi_a, pi_b, pi_c):
                        then(dve.scalar_tensor_tensor(angle[:, :], turns[:, :], -c, angle[:, :], ALU.mult, ALU.add))
                    then(dve.tensor_scalar(angle[:, :], angle[:, :], pi_max, -pi_max, ALU.min, ALU.max))
                    dve.wait_ge(s_sin, 2 * t + 2)
                    then(dve.tensor_tensor(rope_c[:, :], rope_c[:, :], rope_c[:, :], ALU.mult))
                    then(dve.tensor_scalar(rope_c[:, :], rope_c[:, :], -2.0, 1.0, ALU.mult, ALU.add))
                    then(dve.tensor_scalar(rope_s[:, :], rope_s[:, :], rope_rows[:, 2 * t + 1:2 * t + 2], None, ALU.mult))
                for k in range(KT):
                    dve.wait_ge(s_xh, k + 1)
                    dve.tensor_tensor(xt_lo[:, k, :], xt_f[:, k, :], xt_hi[:, k, :], ALU.subtract).then_inc(s_xl, 1)
                gstep = 0

                def gthen(ins):
                    nonlocal gstep
                    gstep += 1
                    ins.then_inc(s_gdve, 1)
                    dve.wait_ge(s_gdve, gstep)

                dve.wait_ge(s_gact, 1)
                gthen(dve.tensor_scalar(gate_m[:, :], gate_x[:, :], 0.0, None, ALU.min))
                dve.wait_ge(s_gact, 4)
                gthen(dve.tensor_tensor_scan(gate_c[:, :], gate_m[:, :], gate_a[:, :], 0.0, ALU.add, ALU.subtract))
                dve.wait_ge(s_const, 6)
                for r in range(3):
                    gthen(dve.tensor_copy(gate_p[:, :], gate_c[:, :]))
                    gthen(dve.tensor_copy(cum_rows[32 * r:32 * r + 8, :], gate_p[:, :]))
                    if r < 2:
                        gthen(dve.tensor_tensor(gate_c[:, :], gate_c[:, :], gate_p[:, :], ALU.subtract))

        low = Room(res_at + 4 * KB)
        pick_now = low("pick_now", [96, 2, P], BF16)
        score_z = [low(f"score_z{b}", [P, SEQ], F32) for b in range(2)]
        soft_a = [low(f"soft_a{b}", [P, SEQ], F32) for b in range(2)]
        prob = [low(f"prob{b}", [P, SEQ], F32) for b in range(2)]
        assert low.at <= arena
        room = Room(arena)
        mix_hi = room("mix_hi", [P, KT, SEQ], BF16)
        mix_lo = room("mix_lo", [P, KT, SEQ], BF16)
        prob += [room(f"prob{b}", [P, SEQ], F32) for b in range(2, 4)]
        score_z += [room(f"score_z{b}", [P, SEQ], F32) for b in range(2, 4)]
        q_hi, q_lo, k_hi, k_lo = [room(n, [P, SEQ], BF16) for n in ("q_hi", "q_lo", "k_hi", "k_lo")]
        nq_hi, nq_lo, nk_hi, nk_lo = [room(n, [P, SEQ], BF16) for n in ("nq_hi", "nq_lo", "nk_hi", "nk_lo")]
        v_hi, v_lo, nv_hi, nv_lo = [room(n, [P, TB, P], BF16) for n in ("v_hi", "v_lo", "nv_hi", "nv_lo")]
        pt_hi = [room("pt_hi0", [P, TB, 512], BF16), room("pt_hi1", [P, TB // 2, 512], BF16)]
        pt_lo = [room("pt_lo0", [P, TB, 512], BF16), room("pt_lo1", [P, TB // 2, 512], BF16)]

        s_qk = sem("scores_ready")
        s_sfree = sem("score_bank_read")
        s_r, s_ab, s_e, s_ln, s_sc, s_sub = [sem(n) for n in
            ("relu_ready", "abs_ready", "exp_ready", "log1p_ready", "suffix_ready", "exponent_ready")]
        s_mx, s_nm, s_ri = sem("max_ready"), sem("neg_max_ready"), sem("inverse_ready")
        s_wsb, s_wfox = sem("sb_weights_ready"), sem("fox_weights_ready")
        s_pv, s_oh, s_ol = sem("pv_ready"), sem("mix_hi_written"), sem("mix_lo_written")
        s_pj, s_pjh, s_pjl = sem("projected"), sem("proj_hi_written"), sem("proj_lo_written")
        s_cur, s_curv, s_pick = sem("qk_current"), sem("v_current"), sem("pick_current")

        half_slots = [(0, 1), (2, 3, 4), (5, 6, 7), (8, 9), (10, 11, 12), (13, 14, 15)]

        def proj_half(pe, e, pair, units):
            n = e // 2
            for u in units:
                if u == 0:
                    if e % 2 == 0:
                        pe.wait_ge(w_split[n], feed_qkv.use(n, pair) + 1)
                    wait_if(pe, s_pjl, 6 * pair + e)
                if e < 4:
                    h = e % 2
                    wh, wl = w_hi[n][:, u * P:(u + 1) * P], w_lo[n][:, u * P:(u + 1) * P]
                    for m, (w, a) in enumerate(((wh, xt_hi), (wh, xt_lo), (wl, xt_hi))):
                        mm = pe.matmul(ps[:, 4, :], w, a[:, u, h * HALF:(h + 1) * HALF],
                                       start=(u == 0 and m == 0), stop=(u == KT - 1 and m == 2))
                else:
                    b = 4 * (e - 4) + u // 2
                    for k in range(u % 2 * 4, u % 2 * 4 + 4):
                        for m, (a, w) in enumerate(((xt_hi, w_hi), (xt_lo, w_hi), (xt_hi, w_lo))):
                            mm = pe.matmul(ps[:, 4, b % 4 * P:(b % 4 + 1) * P], a[:, k, b * P:(b + 1) * P],
                                           w[n][:, k * P:(k + 1) * P],
                                           start=(k == 0 and m == 0), stop=(k == KT - 1 and m == 2))
                if u == 7:
                    mm.then_inc(s_pj, 1)

        def proj_slot(pe, slot, pair):
            for e, slots in enumerate(half_slots):
                if slot in slots:
                    at, of = slots.index(slot), len(slots)
                    proj_half(pe, e, pair, range((8 * at + of - 1) // of, (8 * at + 8 + of - 1) // of))

        def proj_ends(slot, pair, project, first):
            if slot == 0 and not first:
                return [(5, pair)]
            return [(e, pair + 1) for e, slots in enumerate(half_slots) if project and slots[-1] + 1 == slot]

        def proj_dst(e):
            if e < 4:
                hi, lo = ((nq_hi, nq_lo), (nk_hi, nk_lo))[e // 2]
                cols = slice(e % 2 * HALF, (e % 2 + 1) * HALF)
                return hi[:, cols], lo[:, cols], ps[:, 4, :]
            hv = e - 4
            return (nv_hi[:, 4 * hv:4 * hv + 4, :], nv_lo[:, 4 * hv:4 * hv + 4, :],
                    ps[:, 4, :].rearrange("p (b n) -> p b n", b=4))

        def proj_evac_hi(act, e, pair):
            hi, _, src = proj_dst(e)
            act.wait_ge(s_pj, 6 * pair + e + 1)
            if e == 0:
                wait_if(act, s_cur, 8 * pair)
            if e == 4:
                wait_if(act, s_curv, 4 * pair)
            act.activation(hi, src, ACT.Copy).then_inc(s_pjh, 1)

        def proj_evac_lo(dve, e, pair):
            hi, lo, src = proj_dst(e)
            dve.wait_ge(s_pjh, 6 * pair + e + 1)
            dve.tensor_tensor(lo, src, hi, ALU.subtract).then_inc(s_pjl, 1)

        def make_current_qk(dve, hh, pair):
            wait_if(dve, s_qk, STEPS * (pair - 1) + 8 * (hh + 1))
            dve.wait_ge(s_pjl, 6 * pair + 4)
            rows = slice(hh * HEAD_DIM, (hh + 1) * HEAD_DIM)
            for dst, src in ((q_hi, nq_hi), (q_lo, nq_lo), (k_hi, nk_hi), (k_lo, nk_lo)):
                dve.tensor_copy(dst[rows, :], src[rows, :]).then_inc(s_cur, 1)

        def make_current_v(dve, hh, pair):
            wait_if(dve, s_pv, 4 * (pair - 1) + 2 * (hh + 1))
            dve.wait_ge(s_pjl, 6 * pair + 6)
            cols = slice(hh * HEAD_DIM, (hh + 1) * HEAD_DIM)
            for dst, src in ((v_hi, nv_hi), (v_lo, nv_lo)):
                dve.tensor_copy(dst[:, :, cols], src[:, :, cols]).then_inc(s_curv, 1)

        def batch_list(t):
            i, at = query_block(t), batches_through(t) - (2 if query_block(t) >= 4 else 1)
            if i < 4:
                return [(at, 0, i + 1)]
            return [(at, 0, 4), (at + 1, 4, i - 3)]

        def group_end(t):
            return t % 8 // 4 if t % 4 == 3 else None

        class Turning:

            def __init__(self, tag, prob, pt_hi, pt_lo, group_done):
                self.prob, self.pt_hi, self.pt_lo, self.group_done = prob, pt_hi, pt_lo, group_done
                self.made = sem(f"{tag}_turned")
                self.hi = sem(f"{tag}_turned_hi")
                self.lo = sem(f"{tag}_turned_lo")
                assert BATCHES % 2 == 0

            def turn(self, pe, pair, t, weights, ready):
                pe.wait_ge(weights, ready)
                for n, j0, m in batch_list(t):
                    wait_if(pe, self.lo, BATCHES * pair + n - 1)
                    for j in range(m):
                        mm = pe.transpose(ps[:, 5 + n % 2, j * P:(j + 1) * P],
                                          self.prob[t % 4][:, (j0 + j) * P:(j0 + j + 1) * P], ident[:, :])
                    mm.then_inc(self.made, 1)

            def views(self, t, n, j0, m):
                g, qs = t % 8 // 4, query_block(t) % 4 * P
                src = ps[:, 5 + n % 2, 0:m * P].rearrange("p (b n) -> p b n", b=m)
                return self.pt_hi[g][:, j0:j0 + m, qs:qs + P], self.pt_lo[g][:, j0:j0 + m, qs:qs + P], src

            def write_hi(self, act, pair, t):
                for n, j0, m in batch_list(t):
                    hi, _, src = self.views(t, n, j0, m)
                    if t % 4 == 0 and j0 == 0:
                        wait_if(act, self.group_done, 4 * pair + t // 4 - 1)
                    act.wait_ge(self.made, BATCHES * pair + n + 1)
                    act.activation(hi, src, ACT.Copy).then_inc(self.hi, 1)

            def write_lo(self, dve, pair, t):
                for n, j0, m in batch_list(t):
                    hi, lo, src = self.views(t, n, j0, m)
                    dve.wait_ge(self.hi, BATCHES * pair + n + 1)
                    dve.tensor_tensor(lo, src, hi, ALU.subtract).then_inc(self.lo, 1)

            def prob_free(self, pair, t):
                p, before = lagged(pair, t, 4)
                return BATCHES * p + batches_through(before)

        turning = Turning("att0", prob, pt_hi, pt_lo, s_pv)

        def pair_slots(kind):
            return range(STEPS if kind else 6)

        def group_in(slot, lag, pair, kind, prev):
            p, t = lagged(pair, slot, lag)
            if not (kind if slot >= lag else prev) or group_end(t) is None:
                return None
            return p, 2 * (t // 8) + group_end(t)

        def pair_tensor(pe, pair, kind, prev, project):
            for slot in pair_slots(kind):
                if kind:
                    t, i, hh = slot, query_block(slot), slot // 8
                    n = (i + 1) * P
                    rows = slice(hh * HEAD_DIM, (hh + 1) * HEAD_DIM)
                    if t % 8 == 0:
                        pe.wait_ge(s_cur, 8 * pair + 4 * (hh + 1))
                        if kind == "fox":
                            pe.wait_ge(s_pick, 2 * (pair - N_SB // 2) + hh + 1)
                    wait_if(pe, s_sfree, STEPS * pair + t - 1)
                    for c in range(0, n, 512):
                        w = min(512, n - c)
                        bank = ps[:, 2 * (t % 2) + c // 512, :]
                        ends = c + w == n
                        qs = slice(i * P, (i + 1) * P)
                        parts = [(q_hi[rows, qs], k_hi[rows, c:c + w]), (q_lo[rows, qs], k_hi[rows, c:c + w]),
                                 (q_hi[rows, qs], k_lo[rows, c:c + w])]
                        for m, (a, b) in enumerate(parts):
                            mm = pe.matmul(bank[:, 0:w], a, b, start=(m == 0), stop=(m == 2 and kind == "sb" and not ends))
                        if kind == "fox":
                            mm = pe.matmul(bank[:, 0:w], pick_now[:, hh, :], cum_rows[:, c:c + w],
                                           start=False, stop=not ends)
                        if ends:
                            mask = mask_strict if kind == "sb" else mask_causal
                            mm = pe.matmul(bank[:, w - P:w], ident_b[:, :], mask[:, :], start=False, stop=True)
                    mm.then_inc(s_qk, 1)
                    if project:
                        proj_slot(pe, slot, pair + 1)
                found = group_in(slot, 5, pair, kind, prev)
                if found:
                    p, group = found
                    hh, g = group // 2, group % 2
                    if g == 0:
                        pe.wait_ge(s_curv, 4 * p + 2 * (hh + 1))
                    pe.wait_ge(turning.lo, BATCHES * p + batches_through(4 * group + 3))
                    wait_if(pe, s_ol, 4 * p + group)
                    jend = 8 if g == 0 else 4
                    for j in range(jend):
                        qs = max(0, j - 4) * P if g == 0 else j * P
                        parts = ((v_hi, pt_hi), (v_lo, pt_hi), (v_hi, pt_lo))
                        for m, (v, pt) in enumerate(parts):
                            mm = pe.matmul(ps[hh * 64:hh * 64 + 64, 7, qs:512], v[:, j, hh * 64:hh * 64 + 64],
                                           pt[g][:, j, qs:512], start=(j == 0 and m == 0),
                                           stop=(j == jend - 1 and m == 2), skip_group_check=True)
                    mm.then_inc(s_pv, 1)
                p, t = lagged(pair, slot, TR_LAG)
                kind_then = kind if slot >= TR_LAG else prev
                if kind_then == "sb":
                    turning.turn(pe, p, t, s_wsb, STEPS * p + t + 1)
                elif kind_then == "fox":
                    turning.turn(pe, p, t, s_wfox, STEPS * (p - N_SB // 2) + t + 1)

        def mix_views(group, pair):
            hh, g = group // 2, group % 2
            rows, cols = slice(hh * 64, hh * 64 + 64), slice((1 - g) * 512, (1 - g) * 512 + 512)
            return mix_hi[rows, pair, cols], mix_lo[rows, pair, cols], ps[rows, 7, :]

        def pair_scalar(act, pair, kind, prev, project):
            for slot in pair_slots(kind):
                t, n = slot, (query_block(slot) + 1) * P
                for e, p in proj_ends(slot, pair, project, prev is None) if kind else ():
                    proj_evac_hi(act, e, p)
                if kind if slot >= EV_LAG else prev:
                    turning.write_hi(act, *lagged(pair, slot, EV_LAG))
                found = group_in(slot, 6, pair, kind, prev)
                if found:
                    p, group = found
                    hi, _, src = mix_views(group, p)
                    act.wait_ge(s_pv, 4 * p + group + 1)
                    act.activation(hi, src, ACT.Copy).then_inc(s_oh, 1)
                if kind == "sb":
                    act.wait_ge(s_qk, STEPS * pair + t + 1)
                    wait_if(act, s_sub, STEPS * pair + t - 3)
                    act.activation(score_z[t % 4][:, 0:n], banks(2 * (t % 2))[:, 0:n], ACT.Copy,
                                   scale=SB_SCALE).then_inc(s_sfree, 1)
                if kind == "fox":
                    act.wait_ge(s_nm, STEPS * (pair - N_SB // 2) + t + 1)
                    act.wait_ge(turning.made, turning.prob_free(pair, t))
                    act.activation(prob[t % 4][:, 0:n], banks(2 * (t % 2))[:, 0:n], ACT.Exp, scale=SB_SCALE,
                                   bias=neg_max[:, t % 4:t % 4 + 1],
                                   accum_out=row_sum[:, t % 4:t % 4 + 1]).then_inc(s_sfree, 1)
                one_back = (kind if slot >= 1 else prev) == "sb"
                p1, t1 = lagged(pair, slot, 1)
                soft = soft_a[t1 % 2][:, 0:(query_block(t1) + 1) * P]
                if one_back:
                    act.wait_ge(s_ab, STEPS * p1 + t1 + 1)
                    act.activation(soft, soft, ACT.Exp, scale=-1.0).then_inc(s_e, 1)
                if (kind if slot >= 2 else prev) == "sb":
                    p2, t2 = lagged(pair, slot, 2)
                    w = prob[t2 % 4][:, 0:(query_block(t2) + 1) * P]
                    act.wait_ge(s_sub, STEPS * p2 + t2 + 1)
                    act.activation(w, w, ACT.Exp).then_inc(s_wsb, 1)
                if one_back:
                    act.wait_ge(s_e, STEPS * p1 + t1 + 1)
                    act.activation(soft, soft, ACT.Ln, bias=1.0).then_inc(s_ln, 1)

        def pair_vector(dve, pair, kind, prev, project):
            own = pair - N_SB // 2
            for slot in pair_slots(kind):
                t, n = slot, (query_block(slot) + 1) * P
                for e, p in proj_ends(slot, pair, project, prev is None) if kind else ():
                    proj_evac_lo(dve, e, p)
                if kind if slot >= EV_LAG else prev:
                    turning.write_lo(dve, *lagged(pair, slot, EV_LAG))
                found = group_in(slot, 6, pair, kind, prev)
                if found:
                    p, group = found
                    hi, lo, src = mix_views(group, p)
                    dve.wait_ge(s_oh, 4 * p + group + 1)
                    dve.tensor_tensor(lo, src, hi, ALU.subtract).then_inc(s_ol, 1)
                p1, t1 = lagged(pair, slot, 1)
                n1 = (query_block(t1) + 1) * P
                kind1 = kind if slot >= 1 else prev
                if kind == "sb":
                    z = score_z[t % 4][:, 0:n]
                    dve.wait_ge(s_sfree, STEPS * pair + t + 1)
                    wait_if(dve, s_sc, STEPS * pair + t - 1)
                    dve.scalar_tensor_tensor(soft_a[t % 2][:, 0:n], z, -1.0, z, ALU.mult,
                                             ALU.max).then_inc(s_ab, 1)
                    wait_if(dve, turning.made, turning.prob_free(pair, t))
                    dve.tensor_scalar(prob[t % 4][:, 0:n], z, 0.0, None, ALU.max).then_inc(s_r, 1)
                if kind == "fox":
                    dve.wait_ge(s_qk, STEPS * pair + t + 1)
                    dve.tensor_reduce(row_max[:, t % 4:t % 4 + 1], banks(2 * (t % 2))[:, 0:n], AX.X,
                                      ALU.max).then_inc(s_mx, 1)
                    dve.wait_ge(s_mx, STEPS * own + t + 1)
                    dve.tensor_scalar(neg_max[:, t % 4:t % 4 + 1], row_max[:, t % 4:t % 4 + 1], -SB_SCALE, None,
                                      ALU.mult).then_inc(s_nm, 1)
                if kind1 == "fox":
                    dve.wait_ge(s_sfree, STEPS * p1 + t1 + 1)
                    dve.reciprocal(row_inv[:, t1 % 4:t1 % 4 + 1], row_sum[:, t1 % 4:t1 % 4 + 1]).then_inc(s_ri, 1)
                    dve.wait_ge(s_ri, STEPS * (p1 - N_SB // 2) + t1 + 1)
                    dve.tensor_scalar(prob[t1 % 4][:, 0:n1], prob[t1 % 4][:, 0:n1], row_inv[:, t1 % 4:t1 % 4 + 1],
                                      None, ALU.mult).then_inc(s_wfox, 1)
                if kind1 == "sb":
                    dve.wait_ge(s_r, STEPS * p1 + t1 + 1)
                    dve.wait_ge(s_ln, STEPS * p1 + t1 + 1)
                    back = slice(n1 - 1, None, -1)
                    dve.tensor_tensor_scan(prob[t1 % 4][:, back], prob[t1 % 4][:, back], soft_a[t1 % 2][:, back],
                                           0.0, ALU.add, ALU.add).then_inc(s_sc, 1)
                if kind and prev:
                    if slot == 0:
                        make_current_qk(dve, 1, pair)
                    elif slot == 1:
                        make_current_v(dve, 0, pair)
                    elif slot == 5:
                        make_current_v(dve, 1, pair)
                if project and slot == 11:
                    make_current_qk(dve, 0, pair + 1)

        def split_qkv_hi(pool, n, pair):
            pool.wait_ge(w_loaded[n], 16 * (feed_qkv.use(n, pair) + 1))
            pool.wait_ge(s_pj, 6 * (pair - 1) + 2 * (n + 1))
            pool.tensor_tensor(w_hi[n][:, :], w_stage[n][:, :], ones[:, 0:1].to_broadcast([P, KT * P]),
                               ALU.mult).then_inc(w_cast[n], 1)

        def split_qkv_lo(pool, n, pair):
            pool.wait_ge(w_cast[n], feed_qkv.use(n, pair) + 1)
            pool.tensor_tensor(w_lo[n][:, :], w_stage[n][:, :], w_hi[n][:, :], ALU.subtract).then_inc(w_split[n], 1)

        def pair_gpsimd_sb(pool, pair):
            for t in range(STEPS):
                n = (query_block(t) + 1) * P
                pool.wait_ge(s_sc, STEPS * pair + t + 1)
                pool.tensor_tensor(prob[t % 4][:, 0:n], score_z[t % 4][:, 0:n], prob[t % 4][:, 0:n],
                                   ALU.subtract).then_inc(s_sub, 1)
                if t == 2:
                    split_qkv_hi(pool, 2, pair + 1)
                elif t == 3:
                    split_qkv_lo(pool, 2, pair + 1)
                elif t in (6, 11):
                    split_qkv_hi(pool, t // 11, pair + 2)
                elif t in (7, 12):
                    split_qkv_lo(pool, t // 12, pair + 2)

        def pick_head(pool, pair, hh):
            if not isinstance(pair, int) or pair > N_SB // 2:
                pool.wait_ge(s_qk, STEPS * (pair - 1) + 8 * (hh + 1))
            pool.tensor_copy(pick_now[:, hh:hh + 1, :],
                             cum_pick[:, bass.ds(2 * (pair - N_SB // 2) + hh, 1), :]).then_inc(s_pick, 1)

        def all_pairs(eng, each):
            first_fox = N_SB // 2
            each(eng, 0, "sb", None, True)
            with eng.Fori(1, first_fox) as pair:
                each(eng, pair, "sb", "sb", True)
            each(eng, first_fox, "fox", "sb", True)
            with eng.Fori(first_fox + 1, N_PAIRS - 1) as pair:
                each(eng, pair, "fox", "fox", True)
            each(eng, N_PAIRS - 1, "fox", "fox", False)
            each(eng, N_PAIRS, None, "fox", False)

        with nc.Block() as block:
            @block.sync
            def _(sp):
                load_rest(sp, feed_qkv)
                load_first(sp, feed_o0)

            @block.gpsimd
            def _(pool):
                for n in range(2):
                    split_qkv_hi(pool, n, 1)
                    split_qkv_lo(pool, n, 1)
                for hh in range(2):
                    pick_head(pool, N_SB // 2, hh)
                with pool.Fori(0, N_SB // 2) as pair:
                    pair_gpsimd_sb(pool, pair)
                with pool.Fori(N_SB // 2, N_PAIRS - 2) as pair:
                    split_qkv_hi(pool, 2, pair + 1)
                    split_qkv_lo(pool, 2, pair + 1)
                    for n in range(2):
                        split_qkv_hi(pool, n, pair + 2)
                        split_qkv_lo(pool, n, pair + 2)
                        pick_head(pool, pair + 1, n)
                split_qkv_hi(pool, 2, N_PAIRS - 1)
                split_qkv_lo(pool, 2, N_PAIRS - 1)
                for hh in range(2):
                    pick_head(pool, N_PAIRS - 1, hh)

            @block.tensor
            def _(pe):
                for e in range(6):
                    proj_half(pe, e, 0, range(8))
                all_pairs(pe, pair_tensor)

            @block.scalar
            def _(act):
                act.preload_act_table_set("natural_log_exp_and_others")
                for e in range(6):
                    proj_evac_hi(act, e, 0)
                all_pairs(act, pair_scalar)

            @block.vector
            def _(dve):
                for e in range(4):
                    proj_evac_lo(dve, e, 0)
                for hh in range(2):
                    make_current_qk(dve, hh, 0)
                for e in range(4, 6):
                    proj_evac_lo(dve, e, 0)
                for hh in range(2):
                    make_current_v(dve, hh, 0)
                all_pairs(dve, pair_vector)

        def back_and_norm(tag, feed, act_hi, act_lo, cuts, names, free_at, next_feed, load_x=None, final=None):
            pps = len(cuts)
            body = len(feed.pieces) // pps
            room = Room(free_at)
            yt = [room(f"yt{b}_{tag}", [P, SEQ], F32) for b in range(2)]
            g_rows = room(f"g_rows_{tag}", [P, D_MODEL], F32)
            b_rows = room(f"b_rows_{tag}", [P, D_MODEL], F32)
            s_gb, s_x = sem(f"{tag}_gb_loaded"), sem(f"{tag}_x_loaded")
            s_yt, s_yT, s_acc = sem(f"{tag}_yt_written"), sem(f"{tag}_yt_transposed"), sem(f"{tag}_accumulated")
            s_st, s_mv, s_sd, s_rs = [sem(f"{tag}_{n}") for n in ("stats", "moments", "deviation", "rstd")]
            s_n, s_g, s_b = sem(f"{tag}_normed"), sem(f"{tag}_scaled"), sem(f"{tag}_shifted")
            s_nt, s_nh, s_nl = sem(f"{tag}_norm_transposed"), sem(f"{tag}_norm_hi"), sem(f"{tag}_norm_lo")
            s_out = sem(f"{tag}_stored")

            def col_slice(strip):
                return bass.ds(strip * P, P)

            with nc.Block() as block:
                @block.sync
                def _(sp):
                    if load_x is not None:
                        sp.dma_start(x_res[:, :, :], load_x).then_inc(s_x, 16)
                    sp.dma_start(g_rows[:, :], names[0]).then_inc(s_gb, 16)
                    sp.dma_start(b_rows[:, :], names[1]).then_inc(s_gb, 16)
                    load_rest(sp, feed)
                    if next_feed is not None:
                        load_first(sp, next_feed)
                    if final is not None:
                        for b in range(TB):
                            sp.wait_ge(s_b, b + 1)
                            sp.dma_start(final[b], x_res[:, b, :]).then_inc(s_out, 16)
                        sp.wait_ge(s_out, 16 * TB)

                @block.gpsimd
                def _(pool):
                    split_all(pool, feed)
                    pool.wait_ge(s_gb, 32)
                    for b in range(TB):
                        pool.wait_ge(s_g, b + 1)
                        pool.tensor_tensor(x_res[:, b, :], x_res[:, b, :], b_rows[:, :], ALU.add).then_inc(s_b, 1)

                @block.tensor
                def _(pe):
                    def turn(i, r):
                        strip = body * i + r
                        pe.wait_ge(s_yt, strip + 1)
                        pe.wait_ge(s_acc, 2 * since(body * i, r - 1))
                        for b in range(TB):
                            mm = pe.transpose(ps[:, 4 + 2 * (r % 2) + b // 4, b % 4 * P:(b % 4 + 1) * P],
                                              yt[r % 2][:, b * P:(b + 1) * P], ident[:, :])
                        mm.then_inc(s_yT, 1)

                    with pe.Fori(0, feed.iters) as i:
                        for r in range(body):
                            pe.wait_ge(s_yt, since(body * i, r - 1))
                            for c, (a, b) in enumerate(cuts):
                                products(pe, feed, r * pps + c, i, 2 * (r % 2), act_hi, act_lo, a, b,
                                         c == 0, c == pps - 1)
                            if r:
                                turn(i, r - 1)
                        turn(i, body - 1)
                    if final is None:
                        for b in range(TB):
                            pe.wait_ge(s_b, b + 1)
                            pe.wait_ge(s_nl, max(2 * (b - 1), 0))
                            for k in range(KT):
                                mm = pe.transpose(ps[:, 2 * (b % 2) + k // 4, k % 4 * P:(k % 4 + 1) * P],
                                                  x_res[:, b, k * P:(k + 1) * P], ident[:, :])
                            mm.then_inc(s_nt, 1)

                @block.scalar
                def _(act):
                    with act.Fori(0, feed.iters) as i:
                        for r in range(body):
                            n = r * pps + pps - 1
                            act.wait_ge(w_used[feed.slot(n)], feed.used(n, i) + 1)
                            act.wait_ge(s_yT, since(body * i, r - 1))
                            act.activation(yt[r % 2][:, :], banks(2 * (r % 2)), ACT.Copy).then_inc(s_yt, 1)
                    act.wait_ge(s_mv, TB + 1)
                    act.activation(ln_rstd[:, :], ln_rstd[:, :], ACT.Sqrt).then_inc(s_sd, 1)
                    if final is None:
                        for b in range(TB):
                            act.wait_ge(s_nt, b + 1)
                            for h in range(2):
                                act.activation(xt_hi[:, 4 * h:4 * h + 4, b * P:(b + 1) * P],
                                               ps[:, 2 * (b % 2) + h, :].rearrange("p (k n) -> p k n", k=4),
                                               ACT.Copy).then_inc(s_nh, 1)

                @block.vector
                def _(dve):
                    if load_x is not None:
                        dve.wait_ge(s_x, 16)
                    with dve.Fori(0, feed.iters) as i:
                        for r in range(body):
                            dve.wait_ge(s_yT, body * i + r + 1)
                            for h in range(2):
                                cell = x_res[:, 4 * h:4 * h + 4, col_slice(body * i + r)]
                                dve.scalar_tensor_tensor(
                                    cell, cell, ALPHA,
                                    ps[:, 4 + 2 * (r % 2) + h, :].rearrange("p (b n) -> p b n", b=4),
                                    ALU.mult, ALU.add).then_inc(s_acc, 1)
                    dve.wait_ge(s_acc, 2 * body * feed.iters)
                    for b in range(TB):
                        for h in range(2):
                            dve.bn_stats(ln_stats[:, b, 6 * h:6 * h + 6], x_res[:, b, h * 512:(h + 1) * 512]).then_inc(s_st, 1)
                    for b in range(TB):
                        dve.wait_ge(s_st, 2 * (b + 1))
                        dve.bn_aggr(ln_mv[:, b, :], ln_stats[:, b, :]).then_inc(s_mv, 1)
                    dve.wait_ge(s_mv, TB)
                    dve.tensor_scalar(ln_rstd[:, :], ln_mv[:, :, 1], LN_EPS, None, ALU.add).then_inc(s_mv, 1)
                    dve.wait_ge(s_sd, 1)
                    dve.reciprocal(ln_rstd[:, :], ln_rstd[:, :]).then_inc(s_rs, 1)
                    dve.wait_ge(s_rs, 1)
                    dve.wait_ge(s_gb, 32)

                    def norm(b):
                        dve.tensor_scalar(x_res[:, b, :], x_res[:, b, :], ln_mv[:, b, 0:1], ln_rstd[:, b:b + 1],
                                          ALU.subtract, ALU.mult).then_inc(s_n, 1)

                    def lows(b):
                        for h in range(2):
                            dve.wait_ge(s_nh, 2 * b + h + 1)
                            dve.tensor_tensor(xt_lo[:, 4 * h:4 * h + 4, b * P:(b + 1) * P],
                                              ps[:, 2 * (b % 2) + h, :].rearrange("p (k n) -> p k n", k=4),
                                              xt_hi[:, 4 * h:4 * h + 4, b * P:(b + 1) * P],
                                              ALU.subtract).then_inc(s_nl, 1)

                    norm(0)
                    for b in range(TB):
                        if b + 1 < TB:
                            norm(b + 1)
                        dve.wait_ge(s_n, b + 1)
                        dve.tensor_tensor(x_res[:, b, :], x_res[:, b, :], g_rows[:, :], ALU.mult).then_inc(s_g, 1)
                        if final is None and b >= 2:
                            lows(b - 2)
                    if final is None:
                        lows(TB - 2)
                        lows(TB - 1)

        hroom = Room(arena)
        hid_hi = hroom("hid_hi", [P, FT, SEQ], BF16)
        hid_lo = hroom("hid_lo", [P, FT, SEQ], BF16)
        after_hid = hroom.at

        def feed_forward_up(tag, feed, conv_rows, next_feed):
            room = Room(after_hid)
            gate = [room(f"gate{a}_{tag}", [P, SEQ + 2], F32) for a in range(2)]
            conv = [room(f"conv{a}_{tag}", [P, SEQ], F32) for a in range(2)]
            conv_w = sb(f"conv_w_{tag}", [P, FT * 4], F32, 2560)
            assert keep.at <= 2560
            s_cw, s_zero = sem(f"{tag}_conv_w"), sem(f"{tag}_gate_pad")
            s_gt, s_cv, s_ge, s_hm, s_hh, s_hl = [sem(f"{tag}_{n}") for n in
                ("gate_copied", "conv_step", "gelu", "hidden", "hidden_hi", "hidden_lo")]

            with nc.Block() as block:
                @block.sync
                def _(sp):
                    sp.dma_start(conv_w[:, :], conv_rows).then_inc(s_cw, 16)
                    load_rest(sp, feed)
                    load_first(sp, next_feed)

                @block.gpsimd
                def _(pool):
                    for a in range(2):
                        pool.memset(gate[a][:, 0:2], 0.0).then_inc(s_zero, 1)
                    split_all(pool, feed)

                @block.tensor
                def _(pe):
                    with pe.Fori(0, feed.iters) as i:
                        for a in range(2):
                            pe.wait_ge(s_gt, 2 * i)
                            products(pe, feed, 2 * a, i, 4 * a, xt_hi, xt_lo, 0, KT, True, True)
                            pe.wait_ge(s_hm, 2 * i)
                            products(pe, feed, 2 * a + 1, i, 4 * a + 2, xt_hi, xt_lo, 0, KT, True, True)

                @block.scalar
                def _(act):
                    with act.Fori(0, feed.iters) as i:
                        for a in range(2):
                            act.wait_ge(w_used[2 * a], feed.used(2 * a, i) + 1)
                            act.wait_ge(s_cv, 3 * (2 * i))
                            act.activation(gate[a][:, 2:SEQ + 2], banks(4 * a), ACT.Copy).then_inc(s_gt, 1)
                            act.wait_ge(s_cv, 3 * (2 * i + a + 1))
                            act.activation(conv[a][:, :], conv[a][:, :], ACT.Gelu_apprx_tanh).then_inc(s_ge, 1)
                            act.wait_ge(s_hm, 2 * i + a + 1)
                            act.activation(hid_hi[:, 2 * i + a, :], conv[a][:, :], ACT.Copy).then_inc(s_hh, 1)

                @block.vector
                def _(dve):
                    dve.wait_ge(s_cw, 16)
                    dve.wait_ge(s_zero, 2)
                    with dve.Fori(0, feed.iters) as i:
                        for a in range(2):
                            m = 2 * i + a

                            def tap(j):
                                return conv_w[:, bass.ds(4 * m + j, 1)]

                            dve.wait_ge(s_gt, m + 1)
                            dve.wait_ge(s_hl, 2 * i)
                            dve.tensor_scalar(conv[a][:, :], gate[a][:, 0:SEQ], tap(0), tap(3), ALU.mult,
                                              ALU.add).then_inc(s_cv, 1)
                            dve.wait_ge(s_cv, 3 * m + 1)
                            dve.scalar_tensor_tensor(conv[a][:, :], gate[a][:, 1:SEQ + 1], tap(1), conv[a][:, :],
                                                     ALU.mult, ALU.add).then_inc(s_cv, 1)
                            dve.wait_ge(s_cv, 3 * m + 2)
                            dve.scalar_tensor_tensor(conv[a][:, :], gate[a][:, 2:SEQ + 2], tap(2), conv[a][:, :],
                                                     ALU.mult, ALU.add).then_inc(s_cv, 1)
                            dve.wait_ge(s_ge, m + 1)
                            dve.wait_ge(w_used[2 * a + 1], feed.used(2 * a + 1, i) + 1)
                            dve.tensor_tensor(conv[a][:, :], conv[a][:, :], banks(4 * a + 2), ALU.mult).then_inc(s_hm, 1)
                            dve.wait_ge(s_hh, m + 1)
                            dve.tensor_tensor(hid_lo[:, m, :], conv[a][:, :], hid_hi[:, m, :],
                                              ALU.subtract).then_inc(s_hl, 1)

        back_and_norm("o0", feed_o0, mix_hi, mix_lo, [(0, KT)], (t_in["l0_ln1_g"], t_in["l0_ln1_b"]),
                      arena + 32 * KB, feed_up0, load_x=t_in["x"])
        feed_forward_up("up0", feed_up0, t_in["l0_conv"], feed_down0)
        back_and_norm("dn0", feed_down0, hid_hi, hid_lo, DOWN_CUT, (t_in["l0_ln2_g"], t_in["l0_ln2_b"]),
                      after_hid, feed_small)

        clear_sems()

        span = [(i + 1) * P for i in range(TB)]
        at_of = [sum(span[:i]) for i in range(TB)]
        picky = [i for i in range(TB) if (i + 1) * P > TOPK]
        sc_at = {i: at_of[i] - at_of[picky[0]] for i in picky}
        room = Room(arena)
        lat_hi, lat_lo = [room(n, [P, 2, SEQ], BF16) for n in ("lat_hi", "lat_lo")]
        val_hi, val_lo = [room(n, [P, TB, LATENT], BF16) for n in ("val_hi", "val_lo")]
        hide = room("hide", [P, sum(span)], BF16)
        score = room("score", [P, sum(span[i] for i in picky)], F32)
        rope_q = [room(n, [ROPE, SEQ], F32) for n in ("rope_q_cos", "rope_q_sin")]
        after_score = room.at
        rope_i = [room(n, [P, SEQ], F32) for n in ("rope_i_cos", "rope_i_sin")]
        w_idx = room("w_idx", [P, TB, IDX_HEADS], F32)
        qi_hi, qi_lo = [room(n, [P, KT, SEQ], BF16) for n in ("qi_hi", "qi_lo")]
        ki_hi = [room(f"ki_hi{h}", [P, SEQ], BF16) for h in range(2)]
        ki_lo = [room(f"ki_lo{h}", [P, SEQ], BF16) for h in range(2)]
        strip_f = room("strip_f", [P, SEQ], F32)
        strip_w = room("strip_w", [P, SEQ], F32)
        relu = [strip_f, strip_w]

        s_tl5 = sem("tables_loaded")
        s_f5, s_c5, s_s5, s_a5, s_h5, s_l5 = [sem(n) for n in
            ("strip_copied", "strip_cos", "strip_sin", "strip_rotated", "strip_hi", "strip_lo")]
        s_v5h, s_v5l, s_w5, s_z5 = sem("val_hi_written"), sem("val_lo_written"), sem("w_idx_written"), sem("zeros_written")
        s_iq, s_ir, s_ia, s_i0 = sem("idx_product"), sem("idx_relu"), sem("idx_added"), sem("score_zeroed")

        def copy_strip(act, bank, kind, wait_prev):
            act.wait_ge(s_l5, wait_prev)
            src = banks(bank)
            swaps = {"idx": (0, 32, 64, 96), "lat": (0, 32), "plain": ()}[kind]
            for a in swaps:
                b = a + 32 if a % 64 == 0 else a - 32
                act.activation(strip_w[b:b + 32, :], src[a:a + 32, :], ACT.Copy)
            act.activation(strip_f[:, :], src, ACT.Copy).then_inc(s_f5, 1)

        with nc.Block() as block:
            def strip_kind(m):
                return "idx" if m == 0 or m >= 3 else ("lat" if m == 1 else "plain")

            @block.sync
            def _(sp):
                for t, tab in ((0, rope_i), (2, rope_q)):
                    for c in range(2):
                        rows = P if t == 0 else ROPE
                        sp.dma_start(tab[c][0:rows, :], tables[t + c][0:rows, :]).then_inc(s_tl5, 16)
                load_rest(sp, feed_small)
                load_first(sp, feed_qidx)
                load_rest(sp, feed_qidx)
                load_first(sp, feed_q)

            @block.gpsimd
            def _(pool):
                split_all(pool, feed_small)
                split_all(pool, feed_qidx)

            def v_strip(pe, n, cols, bank):
                slot = feed_small.slot(n)
                pe.wait_ge(w_split[slot], feed_small.use(n, 0) + 1)
                for b in range(TB):
                    for k in range(KT):
                        for m, (a, w) in enumerate(((xt_hi, w_hi), (xt_lo, w_hi), (xt_hi, w_lo))):
                            mm = pe.matmul(ps[:, bank + b // 4, b % 4 * cols:(b % 4 + 1) * cols],
                                           a[:, k, b * P:(b + 1) * P], w[slot][:, k * cols:(k + 1) * cols],
                                           start=(k == 0 and m == 0), stop=(k == KT - 1 and m == 2))
                mm.then_inc(w_used[slot], 1)

            @block.tensor
            def _(pe):
                for n in range(3):
                    products(pe, feed_small, n, 0, 2 * n, xt_hi, xt_lo, 0, KT, True, True)
                v_strip(pe, 3, P, 6)
                pe.wait_ge(s_f5, 1)
                v_strip(pe, 4, 80, 0)
                pe.wait_ge(s_f5, 3)
                with pe.Fori(0, feed_qidx.iters) as i:
                    for r in range(4):
                        pe.wait_ge(s_f5, 4 * i + r)
                        if r == 2:
                            pe.wait_ge(s_v5l, 2)
                        if r == 3:
                            pe.wait_ge(s_v5l, 4)
                            pe.wait_ge(s_w5, 2)
                        products(pe, feed_qidx, r, i, 2 * ((r + 1) % 4), xt_hi, xt_lo, 0, KT, True, True)
                pe.wait_ge(s_l5, 11 + 1)
                with pe.Fori(0, KT) as p:
                    for t in range(2 * len(picky)):
                        hh, i = t // len(picky), picky[t % len(picky)]
                        n = span[i]
                        pe.wait_ge(s_ir, since(2 * len(picky) * p, t - 3))
                        for c in range(0, n, 512):
                            w = min(512, n - c)
                            for m, (a, b) in enumerate(((qi_hi, ki_hi), (qi_lo, ki_hi), (qi_hi, ki_lo))):
                                mm = pe.matmul(ps[:, 2 * (t % 4) + c // 512, 0:w], a[:, p, i * P:(i + 1) * P],
                                               b[hh][:, c:c + w], start=(m == 0), stop=(m == 2))
                        mm.then_inc(s_iq, 1)

            @block.scalar
            def _(act):
                def write_hi(m, dsts):
                    act.wait_ge(s_a5, m + 1)
                    for d, rows in dsts:
                        ins = act.activation(d, strip_f[rows, :], ACT.Copy)
                    ins.then_inc(s_h5, 1)

                both = [(ki_hi[0][0:64, :], slice(0, 64)), (ki_hi[1][64:128, :], slice(64, 128))]
                for n in range(3):
                    act.wait_ge(w_used[feed_small.slot(n)], feed_small.used(n, 0) + 1)
                    copy_strip(act, 2 * n, strip_kind(n), (0, 2, 3)[n])
                    if n == 0:
                        act.wait_ge(s_z5, 4)
                        write_hi(0, both)
                    else:
                        write_hi(n, [(lat_hi[:, n - 1, :], slice(0, P))])
                act.wait_ge(w_used[3], feed_small.used(3, 0) + 1)
                for h in range(2):
                    act.activation(val_hi[:, 4 * h:4 * h + 4, 0:P],
                                   ps[:, 6 + h, :].rearrange("p (b n) -> p b n", b=4), ACT.Copy).then_inc(s_v5h, 1)
                act.wait_ge(w_used[0], feed_small.used(4, 0) + 1)
                for h in range(2):
                    src = ps[:, h, 0:320].rearrange("p (b n) -> p b n", b=4)
                    act.activation(w_idx[:, 4 * h:4 * h + 4, :], src[:, :, 64:80], ACT.Copy,
                                   scale=IDX_SCALE).then_inc(s_w5, 1)
                    act.activation(val_hi[:, 4 * h:4 * h + 4, P:LATENT], src[:, :, 0:64], ACT.Copy).then_inc(s_v5h, 1)
                with act.Fori(0, feed_qidx.iters) as i:
                    for r in range(4):
                        m = 3 + 4 * i + r
                        act.wait_ge(w_used[r], feed_qidx.used(r, i) + 1)
                        copy_strip(act, 2 * ((r + 1) % 4), "idx", m + 1)
                        act.wait_ge(s_a5, m + 1)
                        act.activation(qi_hi[:, 4 * i + r, :], strip_f[:, :], ACT.Copy).then_inc(s_h5, 1)
                act.wait_ge(s_l5, 12)
                with act.Fori(0, KT) as p:
                    for t in range(2 * len(picky)):
                        n = span[picky[t % len(picky)]]
                        act.wait_ge(s_iq, 2 * len(picky) * p + t + 1)
                        act.wait_ge(s_ia, since(2 * len(picky) * p, t - 1))
                        act.activation(relu[t % 2][:, 0:n], banks(2 * (t % 4))[:, 0:n], ACT.Relu).then_inc(s_ir, 1)

            @block.vector
            def _(dve):
                for h in range(2):
                    other = slice(64, 128) if h == 0 else slice(0, 64)
                    dve.memset(ki_hi[h][other, :], 0.0).then_inc(s_z5, 1)
                    dve.memset(ki_lo[h][other, :], 0.0).then_inc(s_z5, 1)
                dve.memset(score[:, :], 0.0).then_inc(s_i0, 1)
                dve.wait_ge(s_tl5, 64)

                def rotate(m, kind, rotated, tabs):
                    rows = {"idx": P, "lat": ROPE, "plain": 0}[kind]
                    dve.wait_ge(s_f5, m + 1)
                    if not rows:
                        dve.tensor_copy(tiny[:, 0:1], strip_f[:, 0:1]).then_inc(s_a5, 1)
                        return
                    f, w = strip_f[0:rows, :], strip_w[0:rows, :]
                    dve.tensor_tensor(f, f, tabs[0][0:rows, :], ALU.mult).then_inc(s_c5, 1)
                    dve.tensor_tensor(w, w, tabs[1][0:rows, :], ALU.mult).then_inc(s_s5, 1)
                    dve.wait_ge(s_c5, rotated + 1)
                    dve.wait_ge(s_s5, rotated + 1)
                    dve.tensor_tensor(f, f, w, ALU.add).then_inc(s_a5, 1)

                rotate(0, "idx", 0, rope_i)
                dve.wait_ge(s_h5, 1)
                dve.wait_ge(s_a5, 1)
                dve.tensor_tensor(ki_lo[0][0:64, :], strip_f[0:64, :], ki_hi[0][0:64, :], ALU.subtract).then_inc(s_l5, 1)
                dve.tensor_tensor(ki_lo[1][64:128, :], strip_f[64:128, :], ki_hi[1][64:128, :],
                                  ALU.subtract).then_inc(s_l5, 1)
                for n in (1, 2):
                    rotate(n, "lat" if n == 1 else "plain", n, rope_q)
                    dve.wait_ge(s_h5, n + 1)
                    dve.wait_ge(s_a5, n + 1)
                    dve.tensor_tensor(lat_lo[:, n - 1, :], strip_f[:, :], lat_hi[:, n - 1, :],
                                      ALU.subtract).then_inc(s_l5, 1)
                for h in range(2):
                    dve.wait_ge(s_v5h, h + 1)
                    dve.tensor_tensor(val_lo[:, 4 * h:4 * h + 4, 0:P],
                                      ps[:, 6 + h, :].rearrange("p (b n) -> p b n", b=4),
                                      val_hi[:, 4 * h:4 * h + 4, 0:P], ALU.subtract).then_inc(s_v5l, 1)
                for h in range(2):
                    dve.wait_ge(s_v5h, h + 3)
                    dve.tensor_tensor(val_lo[:, 4 * h:4 * h + 4, P:LATENT],
                                      ps[:, h, 0:320].rearrange("p (b n) -> p b n", b=4)[:, :, 0:64],
                                      val_hi[:, 4 * h:4 * h + 4, P:LATENT], ALU.subtract).then_inc(s_v5l, 1)
                with dve.Fori(0, feed_qidx.iters) as i:
                    for r in range(4):
                        m = 3 + 4 * i + r
                        rotate(m, "idx", m - 1, rope_i)
                        dve.wait_ge(s_h5, m + 1)
                        dve.tensor_tensor(qi_lo[:, 4 * i + r, :], strip_f[:, :], qi_hi[:, 4 * i + r, :],
                                          ALU.subtract).then_inc(s_l5, 1)
                dve.wait_ge(s_i0, 1)
                dve.wait_ge(s_w5, 2)
                with dve.Fori(0, KT) as p:
                    for t in range(2 * len(picky)):
                        hh, i = t // len(picky), picky[t % len(picky)]
                        cell = score[:, sc_at[i]:sc_at[i] + span[i]]
                        dve.wait_ge(s_ir, 2 * len(picky) * p + t + 1)
                        dve.wait_ge(s_ia, since(2 * len(picky) * p, t - len(picky) + 1))
                        dve.scalar_tensor_tensor(cell, relu[t % 2][:, 0:span[i]],
                                                 w_idx[:, i, bass.ds(2 * p + hh, 1)], cell,
                                                 ALU.mult, ALU.add).then_inc(s_ia, 1)

        q_dram = nc.dram_tensor("q_split", (2 * N_DSA, P, 2, SEQ), BF16, kind="Internal").ap()
        room = Room(after_score)
        best = room("best", [P, len(picky), 8], F32)
        qs_f = [room(f"qs_f{b}", [P, SEQ], F32) for b in range(4)]
        qs_w = [room(f"qs_w{b}", [ROPE, SEQ], F32) for b in range(2)]
        q_out = [room(f"q_out{b}", [P, 2, SEQ], BF16) for b in range(4)]
        s_cp, s_cw6, s_co, s_si, s_ro, s_qh, s_ql = [sem(n) for n in
            ("q_copied", "q_swapped", "q_cos", "q_sin", "q_rotated", "q_hi_written", "q_lo_written")]
        s_qst = [sem(f"q_stored{r}") for r in range(4)]
        s_top, s_rep, s_hide = sem("best_found"), sem("best_taken"), sem("hide_written")

        with nc.Block() as block:
            @block.sync
            def _(sp):
                def store(i):
                    for r in range(4):
                        sp.wait_ge(s_ql, 4 * i + r + 1)
                        sp.dma_start(q_dram[4 * i + r], q_out[r][:, :, :]).then_inc(s_qst[r], 16)

                with sp.Fori(1, feed_q.iters) as i:
                    for n in range(4):
                        load_piece(sp, feed_q, n, i)
                    store(i - 1)
                store(feed_q.iters - 1)
                load_first(sp, feed_o1)
                for r in range(4):
                    sp.wait_ge(s_qst[r], 16 * feed_q.iters)

            @block.tensor
            def _(pe):
                with pe.Fori(0, feed_q.iters) as i:
                    for r in range(4):
                        pe.wait_ge(s_cp, 4 * i)
                        products(pe, feed_q, r, i, 2 * r, xt_hi, xt_lo, 0, KT, True, True)

            @block.scalar
            def _(act):
                with act.Fori(0, feed_q.iters) as i:
                    for r in range(4):
                        act.wait_ge(w_loaded[r], 16 * (feed_q.use(r, i) + 1))
                        act.wait_ge(w_used[r], feed_q.used(r, i))
                        act.activation(w_hi[r][:, :], w_stage[r][:, :], ACT.Copy).then_inc(w_cast[r], 1)
                    for r in range(4):
                        act.wait_ge(w_used[r], feed_q.used(r, i) + 1)
                        act.wait_ge(s_ql, 4 * i)
                        if r % 2 == 0:
                            act.activation(qs_w[r // 2][32:64, :], banks(2 * r)[0:32, :], ACT.Copy)
                            act.activation(qs_w[r // 2][0:32, :], banks(2 * r)[32:64, :], ACT.Copy).then_inc(s_cw6, 1)
                        act.activation(qs_f[r][:, :], banks(2 * r), ACT.Copy).then_inc(s_cp, 1)
                        if r % 2 == 0:
                            act.wait_ge(s_ro, 2 * i + r // 2 + 1)
                        else:
                            act.wait_ge(s_cp, 4 * i + r + 1)
                        if r == 0:
                            for rr in range(4):
                                act.wait_ge(s_qst[rr], 16 * i)
                        act.activation(q_out[r][:, 0, :], qs_f[r][:, :], ACT.Copy).then_inc(s_qh, 1)

            @block.gpsimd
            def _(pool):
                with pool.Fori(0, feed_q.iters) as i:
                    for r in range(4):
                        pool.wait_ge(w_loaded[r], 16 * (feed_q.use(r, i) + 1))
                        pool.wait_ge(w_used[r], feed_q.used(r, i))
                        pool.wait_ge(w_cast[r], feed_q.use(r, i) + 1)
                        pool.tensor_tensor(w_lo[r][:, :], w_stage[r][:, :], w_hi[r][:, :], ALU.subtract).then_inc(w_split[r], 1)
                    for r in range(4):
                        if r % 2 == 0:
                            f, w = qs_f[r][0:ROPE, :], qs_w[r // 2][:, :]
                            m = 2 * i + r // 2
                            pool.wait_ge(s_cw6, m + 1)
                            pool.tensor_tensor(w, w, rope_q[1][:, :], ALU.mult).then_inc(s_si, 1)
                            pool.wait_ge(s_cp, 4 * i + r + 1)
                            pool.tensor_tensor(f, f, rope_q[0][:, :], ALU.mult).then_inc(s_co, 1)
                            pool.wait_ge(s_si, m + 1)
                            pool.wait_ge(s_co, m + 1)
                            pool.tensor_tensor(f, f, w, ALU.add).then_inc(s_ro, 1)
                        pool.wait_ge(s_qh, 4 * i + r + 1)
                        pool.tensor_tensor(q_out[r][:, 1, :], qs_f[r][:, :], q_out[r][:, 0, :],
                                           ALU.subtract).then_inc(s_ql, 1)

            @block.vector
            def _(dve):
                for i in picky:
                    end = sc_at[i] + span[i]
                    dve.memset(score[0:CHUNK, end - CHUNK:end], HIDDEN_SCORE).then_inc(s_rep, 1)
                with dve.Fori(0, TOPK // 8) as n:
                    wait_apart(dve, (s_rep, len(picky)), (s_rep, len(picky) * (n + 1)))
                    for c, i in enumerate(picky):
                        dve.max(best[:, c, :], score[:, sc_at[i]:sc_at[i] + span[i]]).then_inc(s_top, 1)
                    wait_apart(dve, (s_top, len(picky)), (s_top, len(picky) * (n + 1)))
                    for c, i in enumerate(picky):
                        cell = score[:, sc_at[i]:sc_at[i] + span[i]]
                        dve.match_replace(cell, best[:, c, :], cell, TAKEN_SCORE).then_inc(s_rep, 1)
                dve.wait_ge(s_rep, len(picky) * (TOPK // 8 + 1))
                for i in range(TB):
                    cell = hide[:, at_of[i]:at_of[i] + span[i]]
                    if i in picky:
                        dve.tensor_scalar(cell, score[:, sc_at[i]:sc_at[i] + span[i]], -2e38, MASKED, ALU.is_gt,
                                          ALU.mult).then_inc(s_hide, 1)
                    else:
                        dve.memset(cell, 0.0).then_inc(s_hide, 1)
                        dve.wait_ge(s_hide, i + 1)
                for i in range(TB):
                    if i not in picky:
                        end = at_of[i] + span[i]
                        dve.memset(hide[0:CHUNK, end - CHUNK:end], MASKED).then_inc(s_hide, 1)

        room = Room(arena + 8 * KB + 2 * TB * LATENT * 2 + (sum(span) * 2 + 31) // 32 * 32)
        at_prob = room.at
        prob7 = [room(f"prob7_{b}", [P, SEQ], F32) for b in range(4)]
        masked = [room(f"masked{b}", [P, SEQ], F32) for b in range(2)]
        q_now = [room(f"q_now{h}", [P, 2, 2, SEQ], BF16) for h in range(2)]
        pt7_hi = [room("pt7_hi0", [P, TB, 512], BF16), room("pt7_hi1", [P, TB // 2, 512], BF16)]
        pt7_lo = [room("pt7_lo0", [P, TB, 512], BF16), room("pt7_lo1", [P, TB // 2, 512], BF16)]
        ctx_hi, ctx_lo = [room(n, [P, 2, 512], BF16) for n in ("ctx_hi", "ctx_lo")]
        uv_hi, uv_lo = [room(n, [P, 2, N_DSA, 64], BF16) for n in ("uv_hi", "uv_lo")]
        uvn_hi, uvn_lo = [room(n, [P, 2, 2, 64], BF16) for n in ("uvn_hi", "uvn_lo")]
        uv_f = sb("uv_f", [P, 2, N_DSA, 64], F32, at_prob)

        s_uvl, s_uvh, s_uvs, s_uvn = sem("uv_loaded"), sem("uv_hi_written"), sem("uv_lo_written"), sem("uv_current")
        s_q7 = [sem(f"q_now_loaded{h}") for h in range(2)]
        t_qk, t_mx, t_nm, t_ex, t_ri, t_w = [sem(n) for n in
            ("lat_scores", "lat_masked_max", "lat_neg_max", "lat_exp", "lat_inverse", "lat_weights")]
        t_pv, t_ch, t_cl = sem("lat_context"), sem("lat_context_hi"), sem("lat_context_lo")

        turning7 = Turning("att1", prob7, pt7_hi, pt7_lo, t_pv)
        s_up, s_uph, s_upl = sem("up_projected"), sem("up_hi_written"), sem("up_lo_written")

        def up_views(group, pair):
            hh, g = group // 2, group % 2
            rows, cols = slice(hh * 64, hh * 64 + 64), slice((1 - g) * 512, (1 - g) * 512 + 512)
            return xt_hi[rows, pair, cols], xt_lo[rows, pair, cols], ps[rows, 4, :]

        def context_views(ct):
            rows, bank = (slice(0, P), 7) if ct == 0 else (slice(0, LATENT - P), 4)
            return ctx_hi[rows, ct, :], ctx_lo[rows, ct, :], ps[rows, bank, :]

        def latent_slots(going):
            return range(STEPS if going else 8)

        def latent_tensor(pe, pair, going, before):
            for slot in latent_slots(going):
                if going:
                    t, i, hh = slot, query_block(slot), slot // 8
                    n = span[i]
                    if t % 8 == 0:
                        pe.wait_ge(s_q7[hh], 16 * (pair + 1))
                    wait_if(pe, t_mx, STEPS * pair + t - 1)
                    qs = slice(i * P, (i + 1) * P)
                    for c in range(0, n, 512):
                        w = min(512, n - c)
                        for kt in range(2):
                            qh, ql = q_now[hh][:, kt, 0, qs], q_now[hh][:, kt, 1, qs]
                            kh, kl = lat_hi[:, kt, c:c + w], lat_lo[:, kt, c:c + w]
                            for m, (a, b) in enumerate(((qh, kh), (qh, kl), (ql, kh))):
                                mm = pe.matmul(ps[:, 2 * (t % 2) + c // 512, 0:w], a, b,
                                               start=(kt == 0 and m == 0), stop=(kt == 1 and m == 2))
                    mm.then_inc(t_qk, 1)
                found = group_in(slot, 7, pair, going, before)
                if found:
                    p, group = found
                    if group == 0:
                        pe.wait_ge(s_uvn, 2 * (p + 1))
                    pe.wait_ge(t_cl, 2 * (4 * p + group + 1))
                    _, _, dst = up_views(group, p)
                    for ct in range(2):
                        rows = slice(0, P) if ct == 0 else slice(0, LATENT - P)
                        uh, ul = uvn_hi[rows, ct, group // 2, :], uvn_lo[rows, ct, group // 2, :]
                        xh, xl = ctx_hi[rows, ct, :], ctx_lo[rows, ct, :]
                        for m, (a, b) in enumerate(((uh, xh), (uh, xl), (ul, xh))):
                            mm = pe.matmul(dst, a, b, start=(ct == 0 and m == 0), stop=(ct == 1 and m == 2))
                    mm.then_inc(s_up, 1)
                found = group_in(slot, 5, pair, going, before)
                if found:
                    p, group = found
                    g = group % 2
                    pe.wait_ge(turning7.lo, BATCHES * p + batches_through(4 * group + 3))
                    wait_if(pe, t_cl, 2 * (4 * p + group))
                    wait_if(pe, s_upl, 4 * p + group)
                    jend = 8 if g == 0 else 4
                    for ct in range(2):
                        cols = slice(0, P) if ct == 0 else slice(P, LATENT)
                        _, _, dst = context_views(ct)
                        for j in range(jend):
                            qs = max(0, j - 4) * P if g == 0 else j * P
                            for m, (v, pt) in enumerate(((val_hi, pt7_hi), (val_hi, pt7_lo), (val_lo, pt7_hi))):
                                mm = pe.matmul(dst[:, qs:512], v[:, j, cols], pt[g][:, j, qs:512],
                                               start=(j == 0 and m == 0), stop=(j == jend - 1 and m == 2),
                                               skip_group_check=True)
                    mm.then_inc(t_pv, 1)
                if going if slot >= TR_LAG else before:
                    p, t = lagged(pair, slot, TR_LAG)
                    turning7.turn(pe, p, t, t_w, STEPS * p + t + 1)

        def latent_scalar(act, pair, going, before):
            for slot in latent_slots(going):
                if going if slot >= EV_LAG else before:
                    turning7.write_hi(act, *lagged(pair, slot, EV_LAG))
                found = group_in(slot, 8, pair, going, before)
                if found:
                    p, group = found
                    hi, _, src = up_views(group, p)
                    act.wait_ge(s_up, 4 * p + group + 1)
                    act.activation(hi, src, ACT.Copy).then_inc(s_uph, 1)
                found = group_in(slot, 6, pair, going, before)
                if found:
                    p, group = found
                    act.wait_ge(t_pv, 4 * p + group + 1)
                    wait_if(act, s_up, 4 * p + group)
                    for ct in range(2):
                        hi, _, src = context_views(ct)
                        act.activation(hi, src, ACT.Copy).then_inc(t_ch, 1)
                if going:
                    t, n = slot, span[query_block(slot)]
                    act.wait_ge(t_nm, STEPS * pair + t + 1)
                    wait_if(act, turning7.made, turning7.prob_free(pair, t))
                    act.activation(prob7[t % 4][:, 0:n], masked[t % 2][:, 0:n], ACT.Exp, scale=DSA_SCALE,
                                   bias=neg_max[:, t % 4:t % 4 + 1],
                                   accum_out=row_sum[:, t % 4:t % 4 + 1]).then_inc(t_ex, 1)

        def latent_vector(dve, pair, going, before):
            for slot in latent_slots(going):
                if going if slot >= EV_LAG else before:
                    turning7.write_lo(dve, *lagged(pair, slot, EV_LAG))
                found = group_in(slot, 8, pair, going, before)
                if found:
                    p, group = found
                    hi, lo, src = up_views(group, p)
                    dve.wait_ge(s_uph, 4 * p + group + 1)
                    dve.tensor_tensor(lo, src, hi, ALU.subtract).then_inc(s_upl, 1)
                found = group_in(slot, 6, pair, going, before)
                if found:
                    p, group = found
                    for ct in range(2):
                        hi, lo, src = context_views(ct)
                        dve.wait_ge(t_ch, 2 * (4 * p + group) + ct + 1)
                        dve.tensor_tensor(lo, src, hi, ALU.subtract).then_inc(t_cl, 1)
                if going:
                    t, i = slot, query_block(slot)
                    n = span[i]
                    wait_apart(dve, (t_qk, 1), (t_qk, STEPS * pair + t + 1), (t_ex, STEPS * pair + t - 1))
                    dve.tensor_tensor_reduce(masked[t % 2][:, 0:n], banks(2 * (t % 2))[:, 0:n],
                                             hide[:, at_of[i]:at_of[i] + n], 1.0, 3.0 * MASKED, ALU.add,
                                             ALU.max, row_max[:, t % 4:t % 4 + 1]).then_inc(t_mx, 1)
                    dve.wait_ge(t_mx, STEPS * pair + t + 1)
                    dve.tensor_scalar(neg_max[:, t % 4:t % 4 + 1], row_max[:, t % 4:t % 4 + 1], -DSA_SCALE,
                                      None, ALU.mult).then_inc(t_nm, 1)
                if going if slot >= 1 else before:
                    p, t = lagged(pair, slot, 1)
                    n = span[query_block(t)]
                    dve.wait_ge(t_ex, STEPS * p + t + 1)
                    dve.reciprocal(row_inv[:, t % 4:t % 4 + 1], row_sum[:, t % 4:t % 4 + 1]).then_inc(t_ri, 1)
                    dve.wait_ge(t_ri, STEPS * p + t + 1)
                    dve.tensor_scalar(prob7[t % 4][:, 0:n], prob7[t % 4][:, 0:n], row_inv[:, t % 4:t % 4 + 1],
                                      None, ALU.mult).then_inc(t_w, 1)

        def all_latent_pairs(eng, each):
            each(eng, 0, True, False)
            with eng.Fori(1, N_PAIRS) as pair:
                each(eng, pair, True, True)
            each(eng, N_PAIRS, False, True)

        with nc.Block() as block:
            @block.sync
            def _(sp):
                def load_q(h, pair):
                    sp.dma_start(q_now[h][:, :, :, :],
                                 q_dram[bass.ds(4 * pair + 2 * h, 2)].rearrange("s p l t -> p s l t")
                                 ).then_inc(s_q7[h], 16)

                load_q(0, 0)
                sp.dma_start(uv_f[:, :, :, :], t_in["l1_uv"]).then_inc(s_uvl, 16)
                load_q(1, 0)
                with sp.Fori(1, N_PAIRS) as pair:
                    for h in range(2):
                        sp.wait_ge(t_qk, STEPS * (pair - 1) + 8 * (h + 1))
                        load_q(h, pair)

            @block.gpsimd
            def _(pool):
                pool.wait_ge(s_uvs, 1)

                def uv_pair(pair):
                    for dst, src in ((uvn_hi, uv_hi), (uvn_lo, uv_lo)):
                        pool.tensor_copy(dst[:, :, :, :], src[:, :, bass.ds(2 * pair, 2), :]).then_inc(s_uvn, 1)

                uv_pair(0)
                with pool.Fori(1, N_PAIRS) as pair:
                    pool.wait_ge(s_up, 4 * pair)
                    uv_pair(pair)

            @block.tensor
            def _(pe):
                all_latent_pairs(pe, latent_tensor)

            @block.scalar
            def _(act):
                act.wait_ge(s_uvl, 16)
                act.activation(uv_hi[:, :, :, :].rearrange("p a h n -> p (a h n)"),
                               uv_f[:, :, :, :].rearrange("p a h n -> p (a h n)"), ACT.Copy).then_inc(s_uvh, 1)
                act.wait_ge(s_uvs, 1)
                all_latent_pairs(act, latent_scalar)

            @block.vector
            def _(dve):
                dve.wait_ge(s_uvh, 1)
                dve.tensor_tensor(uv_lo[:, :, :, :].rearrange("p a h n -> p (a h n)"),
                                  uv_f[:, :, :, :].rearrange("p a h n -> p (a h n)"),
                                  uv_hi[:, :, :, :].rearrange("p a h n -> p (a h n)"), ALU.subtract).then_inc(s_uvs, 1)
                all_latent_pairs(dve, latent_vector)

        back_and_norm("o1", feed_o1, xt_hi, xt_lo, [(0, KT)], (t_in["l1_ln1_g"], t_in["l1_ln1_b"]),
                      arena, feed_up1)
        feed_forward_up("up1", feed_up1, t_in["l1_conv"], feed_down1)
        back_and_norm("dn1", feed_down1, hid_hi, hid_lo, DOWN_CUT, (t_in["l1_ln2_g"], t_in["l1_ln2_b"]),
                      after_hid, None, final=out)



def tiles(w, cols=P):
    k, n = w.shape
    return np.ascontiguousarray(w.reshape(k // P, P, n // cols, cols).transpose(2, 1, 0, 3).reshape(n // cols, P, -1))


def rotary_order():
    return np.array(list(range(0, 8)) + list(range(16, 40)) + list(range(8, 16)) + list(range(40, 64)))


def rope_row_constants():
    rows = np.zeros((P, 4), np.float32)
    for r in range(P):
        half, u = IDX_DIM // 8, r % 32
        if u < half:
            rows[r, 0] = np.float32(THETA) ** np.float32(-u / half)
            rows[r, 1] = -1.0 if r % 64 < 32 else 1.0
        if r < ROPE:
            half = KEY_DIM // 8
            rows[r, 2] = np.float32(THETA) ** np.float32(-(r % 32) / half)
            rows[r, 3] = -1.0 if r < 32 else 1.0
    return rows


def kernel(**inputs):
    import concourse.bacc as bacc
    from concourse.bass_utils import run_bass_kernel_spmd

    a = {k: np.asarray(v) for k, v in inputs.items()}
    c = np.ascontiguousarray
    x = a["x"][0]
    d = {}
    d["x"] = c(x.reshape(TB, P, D_MODEL).transpose(1, 0, 2))
    d["xt"] = c(x.T.reshape(KT, P, SEQ).transpose(1, 0, 2))
    d["positions"] = c(np.broadcast_to(a["positions"], (P, SEQ)))
    d["rope_rows"] = rope_row_constants()
    w = a["l0_w_in"]
    s = tiles(w[:, :3072])
    d["l0_qkv"] = c(s.reshape(2, 3, 4, P, -1).transpose(0, 2, 1, 3, 4).reshape(24, P, -1))
    d["l0_wf"] = c(w[:, 3072:].reshape(KT, P, 8).transpose(1, 0, 2))
    d["l0_bf"] = c(a["l0_b_f"].reshape(8, 1))
    d["l0_o"] = tiles(a["l0_w_o"])
    w = a["l1_w_in"]
    c0 = N_DSA * KEY_DIM
    c2 = c0 + ROPE + LATENT
    c3 = c2 + IDX_HEADS * IDX_DIM
    c4 = c3 + IDX_DIM
    order = rotary_order()
    d["l1_q"] = tiles(w[:, :c0])
    d["l1_qidx"] = tiles(w[:, c2:c3].reshape(D_MODEL, IDX_HEADS, IDX_DIM)[:, :, order].reshape(D_MODEL, -1))
    kidx = w[:, c3:c4][:, order]
    d["l1_kidx"] = tiles(np.concatenate([kidx, kidx], 1))[0]
    d["l1_klat0"], d["l1_klat1"] = tiles(w[:, c0:c2])
    lat = w[:, c0 + ROPE:c2]
    d["l1_v128"] = tiles(lat[:, :P])[0]
    d["l1_v64w"] = tiles(np.concatenate([lat[:, P:], w[:, c4:]], 1), 80)[0]
    uv = np.zeros((2, P, N_DSA, 64), np.float32)
    wuv = a["l1_w_uv"].transpose(1, 0, 2)
    uv[0], uv[1, :LATENT - P] = wuv[:P], wuv[P:]
    d["l1_uv"] = c(uv.transpose(1, 0, 2, 3))
    d["l1_o"] = tiles(a["l1_w_o"])
    for n in range(2):
        up = tiles(a[f"l{n}_w_up"])
        d[f"l{n}_up"] = c(up.reshape(2, FT, P, -1).transpose(1, 0, 2, 3).reshape(2 * FT, P, -1))
        conv = np.concatenate([a[f"l{n}_conv_w"], a[f"l{n}_conv_b"][None]])
        d[f"l{n}_conv"] = c(conv.reshape(4, FT, P).transpose(2, 1, 0).reshape(P, -1))
        d[f"l{n}_down"] = tiles(a[f"l{n}_w_down"])
        for m in (1, 2):
            for q in "gb":
                d[f"l{n}_ln{m}_{q}"] = c(np.broadcast_to(a[f"l{n}_ln{m}_{q}"], (P, D_MODEL)))

    nc = bacc.Bacc("TRN2", target_bir_lowering=False, num_devices=1)
    arrays, t_in = {}, {}
    for name, v in d.items():
        arrays[f"in_{name}"] = v
        t_in[name] = nc.dram_tensor(f"in_{name}", v.shape, mybir.dt.from_np(v.dtype), kind="ExternalInput").ap()
    out = nc.dram_tensor("out", (TB, P, D_MODEL), F32, kind="ExternalOutput").ap()
    program(nc, t_in, out)
    r = run_bass_kernel_spmd(nc, [arrays], core_ids=[0])
    return r.results[0]["out"].reshape(1, SEQ, D_MODEL)
```

```python
import numpy as np
from contextlib import ExitStack

import concourse.bass as bass
from concourse import mybir

F32 = mybir.dt.float32
BF16 = mybir.dt.bfloat16
I32 = mybir.dt.int32
ALU = mybir.AluOpType
ACT = mybir.ActivationFunctionType
AX = mybir.AxisListType

P = 128
D_MODEL = 1024
SEQ = 1024
DEPTH = 2
KT = D_MODEL // P
TB = SEQ // P
HALF = SEQ // 2
CHUNK = 64
HEAD_DIM = 64
N_SB = 8
N_FOX = 8
N_PAIRS = (N_SB + N_FOX) // 2
N_DSA = 16
LATENT = 192
ROPE = 64
KEY_DIM = ROPE + LATENT
IDX_HEADS = 16
IDX_DIM = 64
TOPK = min(256, SEQ // 4)
IDX_SCALE = float(IDX_HEADS * IDX_DIM) ** -0.5
SB_SCALE = float(HEAD_DIM) ** -0.5
DSA_SCALE = float(KEY_DIM) ** -0.5
THETA = 500000.0
D_FF = 2816
FT = D_FF // P
ALPHA = float((2 * DEPTH) ** 0.25)
LN_EPS = 1e-5
MASKED = -1e30
HIDDEN_SCORE = -1e38
TAKEN_SCORE = -3e38
SLOTS = 4
DOWN_CUT = [(0, 6), (6, 12), (12, 17), (17, 22)]
STEPS = 16
TURN_LAG = {"sb": 3, "fox": 4, "latent": 4}

assert SEQ % P == 0 and D_FF % P == 0 and N_DSA == 2 * N_PAIRS


def query_block(t):
    return TB - 1 - t % TB


def batches_through(t):
    return sum(2 if query_block(s) >= 4 else 1 for s in range(t + 1))


BATCHES = batches_through(STEPS - 1)


def since(first, n):
    return first + max(n, 0)


def before(pair, step, back):
    return (pair, step - back) if step >= back else (pair - 1, step - back + STEPS)


def trailing(pair, slot, kind, prev, lag, after_turn=None):
    def behind(k):
        return lag if after_turn is None else TURN_LAG[k] + after_turn

    if kind and slot >= behind(kind):
        return kind, pair, slot - behind(kind)
    if prev and slot < behind(prev):
        return prev, pair - 1, slot - behind(prev) + STEPS
    return None, 0, 0


def wait_if(eng, semaphore, value):
    if not isinstance(value, int) or value > 0:
        eng.wait_ge(semaphore, value)


def wait_apart(eng, always, *waits):
    values = [(s, v if isinstance(v, int) else eng.to_reg(v)) for s, v in waits]
    eng.wait_ge(*always)
    for s, v in values:
        wait_if(eng, s, v)


class Feed:

    def __init__(self, uses, used, dram, pieces, iters, counted=True):
        self.dram, self.pieces, self.iters = dram, pieces, iters
        self.base, self.used_base = dict(uses), dict(used)
        self.order, self.per_iter = [], {s: 0 for s in range(SLOTS)}
        for slot, _ in pieces:
            self.order.append(self.per_iter[slot])
            self.per_iter[slot] += 1
        for s in range(SLOTS):
            uses[s] += iters * self.per_iter[s]
            if counted:
                used[s] += iters * self.per_iter[s]

    def slot(self, n):
        return self.pieces[n][0]

    def use(self, n, i):
        slot = self.slot(n)
        return self.base[slot] + i * self.per_iter[slot] + self.order[n]

    def used(self, n, i):
        slot = self.slot(n)
        return self.used_base[slot] + i * self.per_iter[slot] + self.order[n]


def program(nc, t_in, out):
    with ExitStack() as ctx:
        start = (nc.sbuf_base + 63) // 64 * 64
        KB = 1024
        limit = nc.sbuf_usable_end - start

        def sb(name, shape, dt, at):
            size = int(np.prod(shape[1:])) * (2 if dt == BF16 else 4)
            assert at + size <= limit, (name, at + size, limit)
            return nc.alloc_sbuf_tensor_at(name, shape, dt, offset=start + at)

        class Room:

            def __init__(self, at):
                self.at = at

            def __call__(self, name, shape, dt):
                t = sb(name, shape, dt, self.at)
                self.at += (int(np.prod(shape[1:])) * (2 if dt == BF16 else 4) + 31) // 32 * 32
                return t

        layer_sems = []

        def sem(name):
            layer_sems.append(nc.alloc_semaphore(name))
            return layer_sems[-1]

        def clear_sems():
            nc.clear_and_free_semaphores(layer_sems)
            layer_sems.clear()
            nc.all_engine_barrier(sem_only=True)

        keep = Room(0)
        ident = keep("ident", [P, P], F32)
        ident_b = keep("ident_b", [P, P], BF16)
        mask_strict = keep("mask_strict", [P, P], BF16)
        mask_causal = keep("mask_causal", [P, P], BF16)
        ln_mv = keep("ln_mv", [P, TB, 2], F32)
        ln_rstd = keep("ln_rstd", [P, TB], F32)
        ln_shift = keep("ln_shift", [P, TB], F32)
        row_max = keep("row_max", [P, 4], F32)
        neg_max = keep("neg_max", [P, 4], F32)
        row_sum = keep("row_sum", [P, 4], F32)
        row_inv = keep("row_inv", [P, 4], F32)
        tiny = keep("tiny", [P, 8], F32)
        ones = keep("ones", [P, 1], F32)
        assert keep.at <= 3 * KB
        wroom = Room(3 * KB)
        w_stage = [wroom(f"w_stage{s}", [P, KT * P], F32) for s in range(SLOTS)]
        w_hi = [wroom(f"w_hi{s}", [P, KT * P], BF16) for s in range(SLOTS)]
        w_lo = [wroom(f"w_lo{s}", [P, KT * P], BF16) for s in range(SLOTS)]
        xt_hi = wroom("xt_hi", [P, KT, SEQ], BF16)
        xt_lo = wroom("xt_lo", [P, KT, SEQ], BF16)
        res_at = wroom.at
        x_res = wroom("x_res", [P, TB, D_MODEL], F32)
        arena = wroom.at

        ps = ctx.enter_context(nc.psum_tensor("ps", [P, 8, 512], F32))

        def banks(b):
            return ps[:, b:b + 2, :].rearrange("p a n -> p (a n)")

        w_loaded = [sem(f"w_loaded{s}") for s in range(SLOTS)]
        w_cast = [sem(f"w_cast{s}") for s in range(SLOTS)]
        w_split = [sem(f"w_split{s}") for s in range(SLOTS)]
        w_used = [sem(f"w_used{s}") for s in range(SLOTS)]
        layer_sems.clear()
        uses = {s: 0 for s in range(SLOTS)}
        used = {s: 0 for s in range(SLOTS)}

        feed_qkv = Feed(uses, used, lambda n, i: t_in["l0_qkv"][3 * i + n], [(0, 1024), (1, 1024), (2, 1024)],
                        N_PAIRS, counted=False)

        def strips(name, per_body, iters):
            return Feed(uses, used, lambda n, i: t_in[name][per_body * i + n],
                        [(n, KT * P) for n in range(per_body)], iters)

        def down(name):
            def dram(n, i):
                a, b = DOWN_CUT[n % 4]
                return t_in[name][2 * i + n // 4][:, a * P:b * P]
            return Feed(uses, used, dram,
                        [(n % 4, (DOWN_CUT[n % 4][1] - DOWN_CUT[n % 4][0]) * P) for n in range(8)], KT // 2)

        feed_o0 = strips("l0_o", 4, 2)
        feed_up0 = strips("l0_up", 4, FT // 2)
        feed_down0 = down("l0_down")
        small_cols = [1024, 1024, 1024, 1024, KT * 80]
        small_names = ["l1_kidx", "l1_klat0", "l1_klat1", "l1_v128", "l1_v64w"]
        feed_small = Feed(uses, used, lambda n, i: t_in[small_names[n]],
                          [(s, c) for s, c in zip([0, 1, 2, 3, 0], small_cols)], 1)
        feed_qidx = strips("l1_qidx", 4, 2)
        feed_q = strips("l1_q", 4, 8)
        feed_o1 = strips("l1_o", 4, 2)
        feed_up1 = strips("l1_up", 4, FT // 2)
        feed_down1 = down("l1_down")

        def load_piece(sp, feed, n, i):
            slot, cols = feed.pieces[n]
            sp.wait_ge(w_split[slot], feed.use(n, i))
            sp.dma_start(w_stage[slot][:, 0:cols], feed.dram(n, i)).then_inc(w_loaded[slot], 16)

        def load_first(sp, feed):
            for n in range(len(feed.pieces)):
                if feed.order[n] == 0:
                    load_piece(sp, feed, n, 0)

        def load_rest(sp, feed):
            for n in range(len(feed.pieces)):
                if feed.order[n] > 0:
                    load_piece(sp, feed, n, 0)
            if feed.iters > 1:
                with sp.Fori(1, feed.iters) as i:
                    for n in range(len(feed.pieces)):
                        load_piece(sp, feed, n, i)

        def split_piece(pool, feed, n, i):
            slot, cols = feed.pieces[n]
            pool.wait_ge(w_loaded[slot], 16 * (feed.use(n, i) + 1))
            pool.wait_ge(w_used[slot], feed.used(n, i))
            pool.tensor_tensor(w_hi[slot][:, 0:cols], w_stage[slot][:, 0:cols], ones[:, 0:1].to_broadcast([P, cols]),
                               ALU.mult).then_inc(w_cast[slot], 1)
            pool.wait_ge(w_cast[slot], feed.use(n, i) + 1)
            pool.tensor_tensor(w_lo[slot][:, 0:cols], w_stage[slot][:, 0:cols], w_hi[slot][:, 0:cols],
                               ALU.subtract).then_inc(w_split[slot], 1)

        def split_first(pool, feed, ns=range(SLOTS)):
            for n in range(len(feed.pieces)):
                if feed.order[n] == 0 and feed.slot(n) in ns:
                    split_piece(pool, feed, n, 0)

        def split_rest(pool, feed):
            for n in range(len(feed.pieces)):
                if feed.order[n] > 0:
                    split_piece(pool, feed, n, 0)
            if feed.iters > 1:
                with pool.Fori(1, feed.iters) as i:
                    for n in range(len(feed.pieces)):
                        split_piece(pool, feed, n, i)

        def products(pe, feed, n, i, bank, act_hi, act_lo, k0, k1, first, last):
            slot = feed.slot(n)
            pe.wait_ge(w_split[slot], feed.use(n, i) + 1)
            for k in range(k0, k1):
                wh = w_hi[slot][:, (k - k0) * P:(k - k0 + 1) * P]
                wl = w_lo[slot][:, (k - k0) * P:(k - k0 + 1) * P]
                for m, (w, a) in enumerate(((wh, act_hi), (wh, act_lo), (wl, act_hi))):
                    for h in range(2):
                        mm = pe.matmul(ps[:, bank + h, :], w, a[:, k, h * HALF:(h + 1) * HALF],
                                       start=(first and k == k0 and m == 0),
                                       stop=(last and k == k1 - 1 and m == 2))
            mm.then_inc(w_used[slot], 1)

        def product_tile(pe, feed, act_hi, act_lo, k):
            slot = feed.slot(0)
            wh, wl = w_hi[slot][:, k * P:(k + 1) * P], w_lo[slot][:, k * P:(k + 1) * P]
            for m, (w, a) in enumerate(((wh, act_hi), (wh, act_lo), (wl, act_hi))):
                for h in range(2):
                    mm = pe.matmul(ps[:, h, :], w, a[:, k, h * HALF:(h + 1) * HALF],
                                   start=(k == 0 and m == 0), stop=(k == KT - 1 and m == 2))
            return mm

        def start_product(pe, slot, feed, act_hi, act_lo, tiles_ready, banks_read):
            if 1 <= slot < KT:
                if slot == 1:
                    pe.wait_ge(w_split[feed.slot(0)], feed.use(0, 0) + 1)
                    pe.wait_ge(*tiles_ready)
                    pe.wait_ge(*banks_read)
                product_tile(pe, feed, act_hi, act_lo, slot - 1)

        def product_part(pe, feed, n, h, ks):
            slot, bank = feed.slot(n), 2 * n
            for k in ks:
                wh, wl = w_hi[slot][:, k * P:(k + 1) * P], w_lo[slot][:, k * P:(k + 1) * P]
                for m, (w, a) in enumerate(((wh, xt_hi), (wh, xt_lo), (wl, xt_hi))):
                    mm = pe.matmul(ps[:, bank + h, :], w, a[:, k, h * HALF:(h + 1) * HALF],
                                   start=(k == 0 and m == 0), stop=(k == KT - 1 and m == 2))
            return mm

        def phase(sync, gpsimd, tensor, scalar, vector):
            return dict(sync=sync, gpsimd=gpsimd, tensor=tensor, scalar=scalar, vector=vector)

        def run_phases(*phases):
            with nc.Block() as block:
                @block.sync
                def _(sp):
                    for p in phases:
                        p["sync"](sp)

                @block.gpsimd
                def _(pool):
                    for p in phases:
                        p["gpsimd"](pool)

                @block.tensor
                def _(pe):
                    for p in phases:
                        p["tensor"](pe)

                @block.scalar
                def _(act):
                    for p in phases:
                        p["scalar"](act)

                @block.vector
                def _(dve):
                    for p in phases:
                        p["vector"](dve)

        room = Room(arena)
        xt_f = room("xt_f", [P, KT, SEQ], F32)
        rope_rows = room("rope_rows", [P, 4], F32)
        wf_f = room("wf_f", [P, KT, 8], F32)
        wf_hi = room("wf_hi", [P, KT, 8], BF16)
        wf_lo = room("wf_lo", [P, KT, 8], BF16)
        gate_b = room("gate_b", [8, 1], F32)
        low = Room(res_at)
        cum_rows = low("cum_rows", [96, SEQ], BF16)
        cum_pick = low("cum_pick", [96, N_FOX, P], BF16)
        gate_x = room("gate_x", [8, SEQ], F32)
        gate_a = room("gate_a", [8, SEQ], F32)
        gate_m = room("gate_m", [8, SEQ], F32)
        gate_c = room("gate_c", [8, SEQ], F32)
        gate_p = room("gate_p", [8, SEQ], BF16)
        tables = nc.dram_tensor("rope_tables", (4, P, SEQ), F32, kind="Internal").ap()
        s_pos, s_wf = sem("pos_loaded"), sem("wf_loaded")
        s_xt = [sem(f"xt_loaded{k}") for k in range(KT)]
        s_xh, s_xl = sem("xt_hi_written"), sem("xt_lo_written")
        s_const = sem("const_step")
        s_wfh, s_wfl = sem("wf_hi_written"), sem("wf_lo_written")
        s_tab, s_sin, s_tabst = sem("table_step"), sem("table_sin"), sem("table_stored")
        s_gmm, s_gact, s_gdve = sem("gate_product"), sem("gate_act"), sem("gate_dve")
        CONST_STEPS, GATE_STEPS = 14, 10
        inv_2pi = float(np.float32(1 / (2 * np.pi)))
        pi_a = 6.28125
        rest = 2 * np.pi - pi_a
        pi_b = float(np.floor(rest * 2 ** 17) / 2 ** 17)
        pi_c = float(np.float32(rest - pi_b))
        magic = 1.5 * 2 ** 23
        pi_max = 3.1415925

        def start_sync(sp):
            for k in range(0, KT, 2):
                sp.dma_start(xt_f[:, k, :], t_in["xt"][:, k, :]).then_inc(s_xt[k], 16)
            sp.dma_start(pos_i[:, :], t_in["positions"]).then_inc(s_pos, 16)
            sp.dma_start(rope_rows[:, :], t_in["rope_rows"]).then_inc(s_pos, 16)
            load_first(sp, feed_qkv)

        def start_scalar(act):
            act.dma_start(wf_f[:, :, :], t_in["l0_wf"]).then_inc(s_wf, 16)
            act.dma_start(gate_b[:, :], t_in["l0_bf"]).then_inc(s_wf, 16)
            for k in range(1, KT, 2):
                act.dma_start(xt_f[:, k, :], t_in["xt"][:, k, :]).then_inc(s_xt[k], 16)
            for k in range(KT):
                act.wait_ge(s_xt[k], 16)
                act.activation(xt_hi[:, k, :], xt_f[:, k, :], ACT.Copy).then_inc(s_xh, 1)
            act.preload_act_table_set("natural_log_exp_and_others")
            act.wait_ge(s_gmm, 1)
            act.wait_ge(s_wf, 32)
            act.activation(gate_x[:, :], banks(0)[0:8, :], ACT.Identity, bias=gate_b[:, 0:1]).then_inc(s_gact, 1)
            act.wait_ge(s_gact, 1)
            act.activation(gate_a[:, :], gate_x[:, :], ACT.Abs).then_inc(s_gact, 1)
            act.wait_ge(s_gact, 2)
            act.activation(gate_a[:, :], gate_a[:, :], ACT.Exp, scale=-1.0).then_inc(s_gact, 1)
            act.wait_ge(s_gact, 3)
            act.activation(gate_a[:, :], gate_a[:, :], ACT.Ln, bias=1.0).then_inc(s_gact, 1)

        def start_gpsimd(pool):
            steps = 0

            def done(ins):
                nonlocal steps
                steps += 1
                ins.then_inc(s_const, 1)

            done(pool.memset(ident[:, :], 0.0))
            done(pool.memset(ident_b[:, :], 0.0))
            done(pool.memset(mask_strict[:, :], 0.0))
            done(pool.memset(mask_causal[:, :], 0.0))
            done(pool.memset(cum_pick[:, :, :], 0.0))
            done(pool.memset(cum_rows[:, :], 0.0))
            done(pool.memset(ones[:, :], 1.0))
            pool.wait_ge(s_const, 7)
            for m in (ident, ident_b):
                done(pool.affine_select(out=m[:, :], in_=m[:, :], compare_op=ALU.not_equal, fill=1.0,
                                        base=0, pattern=[[-1, P]], channel_multiplier=1))
            done(pool.affine_select(out=mask_strict[:, :], in_=mask_strict[:, :], compare_op=ALU.is_gt,
                                    fill=MASKED, base=0, pattern=[[-1, P]], channel_multiplier=1))
            done(pool.affine_select(out=mask_causal[:, :], in_=mask_causal[:, :], compare_op=ALU.is_ge,
                                    fill=MASKED, base=0, pattern=[[-1, P]], channel_multiplier=1))
            for r in range(3):
                done(pool.affine_select(out=cum_pick[:, :, :], in_=cum_pick[:, :, :],
                                        compare_op=ALU.not_equal, fill=-1.0 / SB_SCALE, base=-32 * r,
                                        pattern=[[-1, N_FOX], [0, P]], channel_multiplier=1))
                pool.wait_ge(s_const, steps)
            pool.wait_ge(s_wf, 32)
            pool.tensor_copy(wf_hi[:, :, :], wf_f[:, :, :]).then_inc(s_wfh, 1)
            pool.wait_ge(s_wfh, 1)
            pool.tensor_tensor(wf_lo[:, :, :], wf_f[:, :, :], wf_hi[:, :, :], ALU.subtract).then_inc(s_wfl, 1)
            split_piece(pool, feed_qkv, 0, 0)
            split_piece(pool, feed_qkv, 1, 0)
            split_piece(pool, feed_qkv, 2, 0)

        def start_tensor(pe):
            pe.wait_ge(s_wfl, 1)
            for k in range(KT):
                pe.wait_ge(s_xl, k + 1)
                for h in range(2):
                    for m, (w, a) in enumerate(((wf_hi, xt_hi), (wf_hi, xt_lo), (wf_lo, xt_hi))):
                        mm = pe.matmul(ps[0:8, h, :], w[:, k, :], a[:, k, h * HALF:(h + 1) * HALF],
                                       start=(k == 0 and m == 0), stop=(k == KT - 1 and m == 2))
            mm.then_inc(s_gmm, 1)

        def start_vector(dve):
            for k in range(KT):
                dve.wait_ge(s_xh, k + 1)
                dve.tensor_tensor(xt_lo[:, k, :], xt_f[:, k, :], xt_hi[:, k, :], ALU.subtract).then_inc(s_xl, 1)
            rotary_angles(dve, 0)
            gstep = 0

            def gthen(ins):
                nonlocal gstep
                gstep += 1
                ins.then_inc(s_gdve, 1)
                dve.wait_ge(s_gdve, gstep)

            dve.wait_ge(s_gact, 1)
            gthen(dve.tensor_scalar(gate_m[:, :], gate_x[:, :], 0.0, None, ALU.min))
            dve.wait_ge(s_gact, 4)
            gthen(dve.tensor_tensor_scan(gate_c[:, :], gate_m[:, :], gate_a[:, :], 0.0, ALU.add, ALU.subtract))
            dve.wait_ge(s_const, 6)
            for r in range(3):
                gthen(dve.tensor_copy(gate_p[:, :], gate_c[:, :]))
                gthen(dve.tensor_copy(cum_rows[32 * r:32 * r + 8, :], gate_p[:, :]))
                if r < 2:
                    gthen(dve.tensor_tensor(gate_c[:, :], gate_c[:, :], gate_p[:, :], ALU.subtract))

        low = Room(res_at + 4 * KB)
        pick_now = low("pick_now", [96, 2, P], BF16)
        z_at = [low.at, low.at + 4 * KB]
        score_z = [low(f"score_z{b}", [P, SEQ], F32) for b in range(2)]
        soft_a = [low(f"soft_a{b}", [P, SEQ], F32) for b in range(2)]
        prob = [low(f"prob{b}", [P, SEQ], F32) for b in range(2)]
        assert low.at <= arena
        room = Room(arena)
        mix_hi = room("mix_hi", [P, KT, SEQ], BF16)
        mix_lo = room("mix_lo", [P, KT, SEQ], BF16)
        prob += [room(f"prob{b}", [P, SEQ], F32) for b in range(2, 4)]
        z_at += [room.at, room.at + 4 * KB]
        score_z += [room(f"score_z{b}", [P, SEQ], F32) for b in range(2, 4)]
        q_both, k_twice = [[room(f"{n}{hh}", [P, SEQ], BF16) for hh in range(2)] for n in ("q_both", "k_twice")]
        k_lo = room("k_lo", [P, SEQ], BF16)
        nq_hi, nq_lo, nk_hi, nk_lo = [room(n, [P, SEQ], BF16) for n in ("nq_hi", "nq_lo", "nk_hi", "nk_lo")]
        v_hi, v_lo, nv_hi, nv_lo = [room(n, [P, TB, P], BF16) for n in ("v_hi", "v_lo", "nv_hi", "nv_lo")]
        scratch = Room(room.at)
        pos_i = scratch("pos_i", [P, SEQ], I32)
        pos_f, angle, turns, rope_c, rope_s = [scratch(n, [P, SEQ], F32) for n in
            ("pos_f", "angle", "turns", "rope_c", "rope_s")]
        pt_hi = [room("pt_hi0", [P, TB, 512], BF16), room("pt_hi1", [P, TB // 2, 512], BF16)]
        pt_lo = [room("pt_lo0", [P, TB, 512], BF16), room("pt_lo1", [P, TB // 2, 512], BF16)]

        s_qk = sem("scores_ready")
        s_sfree = sem("score_bank_read")
        s_r, s_ab, s_e, s_ln, s_sc, s_sub = [sem(n) for n in
            ("relu_ready", "abs_ready", "exp_ready", "log1p_ready", "suffix_ready", "exponent_ready")]
        s_mx, s_nm, s_ri = sem("max_ready"), sem("neg_max_ready"), sem("inverse_ready")
        s_ph = sem("prob_hi_written")
        s_wsb, s_wfox = sem("sb_weights_ready"), sem("fox_weights_ready")
        s_pv, s_oh, s_ol = sem("pv_ready"), sem("mix_hi_written"), sem("mix_lo_written")
        s_pj, s_pjh, s_pjl = sem("projected"), sem("proj_hi_written"), sem("proj_lo_written")
        s_cur, s_curv, s_pick = sem("qk_current"), sem("v_current"), sem("pick_current")

        half_slots = [(0, 1), (2, 3, 4), (5, 6, 7), (8, 9), (10, 11, 12), (13, 14, 15)]

        def proj_bank(e, pair):
            return 2 + e if isinstance(pair, int) and pair == 0 else 4

        def proj_half(pe, e, pair, units):
            n, bank = e // 2, proj_bank(e, pair)
            first = isinstance(pair, int) and pair == 0
            for u in units:
                if u == 0:
                    if e % 2 == 0:
                        pe.wait_ge(w_split[n], feed_qkv.use(n, pair) + 1)
                    if not first:
                        pe.wait_ge(s_pjl, 6 * pair + e)
                if e < 4:
                    h = e % 2
                    wh, wl = w_hi[n][:, u * P:(u + 1) * P], w_lo[n][:, u * P:(u + 1) * P]
                    for m, (w, a) in enumerate(((wh, xt_hi), (wh, xt_lo), (wl, xt_hi))):
                        mm = pe.matmul(ps[:, bank, :], w, a[:, u, h * HALF:(h + 1) * HALF],
                                       start=(u == 0 and m == 0), stop=(u == KT - 1 and m == 2))
                else:
                    b = 4 * (e - 4) + u // 2
                    for k in range(u % 2 * 4, u % 2 * 4 + 4):
                        for m, (a, w) in enumerate(((xt_hi, w_hi), (xt_lo, w_hi), (xt_hi, w_lo))):
                            mm = pe.matmul(ps[:, bank, b % 4 * P:(b % 4 + 1) * P], a[:, k, b * P:(b + 1) * P],
                                           w[n][:, k * P:(k + 1) * P],
                                           start=(k == 0 and m == 0), stop=(k == KT - 1 and m == 2))
                if u == 7:
                    mm.then_inc(s_pj, 1)

        def proj_slot(pe, slot, pair):
            for e, slots in enumerate(half_slots):
                if slot in slots:
                    at, of = slots.index(slot), len(slots)
                    proj_half(pe, e, pair, range((8 * at + of - 1) // of, (8 * at + 8 + of - 1) // of))

        def proj_ends(slot, pair, project, first):
            if slot == 0 and not first:
                return [(5, pair)]
            return [(e, pair + 1) for e, slots in enumerate(half_slots) if project and slots[-1] + 1 == slot]

        def proj_dst(e, pair):
            if e < 4:
                hi, lo = ((nq_hi, nq_lo), (nk_hi, nk_lo))[e // 2]
                cols = slice(e % 2 * HALF, (e % 2 + 1) * HALF)
                return hi[:, cols], lo[:, cols], ps[:, proj_bank(e, pair), :]
            hv = e - 4
            return (nv_hi[:, 4 * hv:4 * hv + 4, :], nv_lo[:, 4 * hv:4 * hv + 4, :],
                    ps[:, proj_bank(e, pair), :].rearrange("p (b n) -> p b n", b=4))

        def proj_evac_hi(act, e, pair):
            hi, _, src = proj_dst(e, pair)
            act.wait_ge(s_pj, 6 * pair + e + 1)
            if e == 0:
                wait_if(act, s_cur, 10 * pair)
            if e == 4:
                wait_if(act, s_curv, 4 * pair)
            act.activation(hi, src, ACT.Copy).then_inc(s_pjh, 1)

        def proj_evac_lo(dve, e, pair):
            hi, lo, src = proj_dst(e, pair)
            dve.wait_ge(s_pjh, 6 * pair + e + 1)
            dve.tensor_tensor(lo, src, hi, ALU.subtract).then_inc(s_pjl, 1)

        def make_current_qk(dve, hh, pair):
            wait_if(dve, s_qk, STEPS * (pair - 1) + 8 * (hh + 1))
            dve.wait_ge(s_pjl, 6 * pair + 4)
            rows = slice(hh * HEAD_DIM, (hh + 1) * HEAD_DIM)
            other = slice((1 - hh) * HEAD_DIM, (2 - hh) * HEAD_DIM)
            for dst, to, src in ((q_both[hh], rows, nq_hi), (q_both[hh], other, nq_lo), (k_twice[hh], rows, nk_hi),
                                 (k_twice[hh], other, nk_hi), (k_lo, rows, nk_lo)):
                dve.tensor_copy(dst[to, :], src[rows, :]).then_inc(s_cur, 1)

        def make_current_v(dve, hh, pair):
            wait_if(dve, s_pv, 4 * (pair - 1) + 2 * (hh + 1))
            dve.wait_ge(s_pjl, 6 * pair + 6)
            cols = slice(hh * HEAD_DIM, (hh + 1) * HEAD_DIM)
            for dst, src in ((v_hi, nv_hi), (v_lo, nv_lo)):
                dve.tensor_copy(dst[:, :, cols], src[:, :, cols]).then_inc(s_curv, 1)

        def batch_list(t):
            i, at = query_block(t), batches_through(t) - (2 if query_block(t) >= 4 else 1)
            if i < 4:
                return [(at, 0, i + 1)]
            return [(at, 0, 4), (at + 1, 4, i - 3)]

        def group_end(t):
            return t % 8 // 4 if t % 4 == 3 else None

        class Turning:

            def __init__(self, tag, prob, parts, pt_hi, pt_lo, group_done):
                self.prob, self.parts = prob, parts
                self.pt_hi, self.pt_lo, self.group_done = pt_hi, pt_lo, group_done
                self.made = sem(f"{tag}_turned")
                self.hi = sem(f"{tag}_turned_hi")
                self.lo = sem(f"{tag}_turned_lo")
                assert BATCHES % 2 == 0

            def turn(self, pe, pair, t, weights, ready, in_parts):
                pe.wait_ge(weights, ready)
                for n, j0, m in batch_list(t):
                    wait_if(pe, self.lo, BATCHES * pair + n - 1)
                    for j in range(m):
                        dst, cols = ps[:, 5 + n % 2, j * P:(j + 1) * P], slice((j0 + j) * P, (j0 + j + 1) * P)
                        if in_parts:
                            for a, part in enumerate(self.parts[t % 4]):
                                mm = pe.matmul(dst, part[:, cols], ident_b[:, :], start=(a == 0), stop=(a == 1))
                        else:
                            mm = pe.transpose(dst, self.prob[t % 4][:, cols], ident[:, :])
                    mm.then_inc(self.made, 1)

            def views(self, t, n, j0, m):
                g, qs = t % 8 // 4, query_block(t) % 4 * P
                src = ps[:, 5 + n % 2, 0:m * P].rearrange("p (b n) -> p b n", b=m)
                return self.pt_hi[g][:, j0:j0 + m, qs:qs + P], self.pt_lo[g][:, j0:j0 + m, qs:qs + P], src

            def write_hi(self, act, pair, t):
                for n, j0, m in batch_list(t):
                    hi, _, src = self.views(t, n, j0, m)
                    if t % 4 == 0 and j0 == 0:
                        wait_if(act, self.group_done, 4 * pair + t // 4 - 1)
                    act.wait_ge(self.made, BATCHES * pair + n + 1)
                    act.activation(hi, src, ACT.Copy).then_inc(self.hi, 1)

            def write_lo(self, dve, pair, t):
                for n, j0, m in batch_list(t):
                    hi, lo, src = self.views(t, n, j0, m)
                    dve.wait_ge(self.hi, BATCHES * pair + n + 1)
                    dve.tensor_tensor(lo, src, hi, ALU.subtract).then_inc(self.lo, 1)

            def prob_free(self, pair, t):
                p, last = before(pair, t, 4)
                return BATCHES * p + batches_through(last)

        parts0 = [[sb(f"prob_{n}{b}", [P, SEQ], BF16, z_at[b] + 2 * KB * a) for a, n in enumerate(("hi", "lo"))]
                  for b in range(4)]
        turning = Turning("att0", prob, parts0, pt_hi, pt_lo, s_pv)

        def slots_of(kind, prev, last):
            return range(STEPS if kind else TURN_LAG[prev] + last)

        def group_in(slot, after_turn, pair, kind, prev):
            k, p, t = trailing(pair, slot, kind, prev, None, after_turn)
            if not k or group_end(t) is None:
                return None
            return p, 2 * (t // 8) + group_end(t)

        def pair_tensor(pe, pair, kind, prev, project):
            for slot in slots_of(kind, prev, 5):
                if kind:
                    t, i, hh = slot, query_block(slot), slot // 8
                    n = (i + 1) * P
                    rows = slice(hh * HEAD_DIM, (hh + 1) * HEAD_DIM)
                    if t % 8 == 0:
                        pe.wait_ge(s_cur, 10 * pair + 5 * (hh + 1))
                        if kind == "fox":
                            pe.wait_ge(s_pick, 2 * (pair - N_SB // 2) + hh + 1)
                    wait_if(pe, s_sfree, STEPS * pair + t - 1)
                    for c in range(0, n, 512):
                        w = min(512, n - c)
                        bank = ps[:, 2 * (t % 2) + c // 512, :]
                        ends = c + w == n
                        qs = slice(i * P, (i + 1) * P)
                        parts = [(q_both[hh][:, qs], k_twice[hh][:, c:c + w]),
                                 (q_both[hh][rows, qs], k_lo[rows, c:c + w])]
                        for m, (a, b) in enumerate(parts):
                            mm = pe.matmul(bank[:, 0:w], a, b, start=(m == 0), stop=(m == 1 and kind == "sb" and not ends))
                        if kind == "fox":
                            mm = pe.matmul(bank[:, 0:w], pick_now[:, hh, :], cum_rows[:, c:c + w],
                                           start=False, stop=not ends)
                        if ends:
                            mask = mask_strict if kind == "sb" else mask_causal
                            mm = pe.matmul(bank[:, w - P:w], ident_b[:, :], mask[:, :], start=False, stop=True)
                    mm.then_inc(s_qk, 1)
                    if project:
                        proj_slot(pe, slot, pair + 1)
                for part, cuts in enumerate((((0, 3), (0, 1)), ((3, TB), (1, TB // 2)))):
                    found = group_in(slot, 2 + part, pair, kind, prev)
                    if not found:
                        continue
                    p, group = found
                    hh, g = group // 2, group % 2
                    if g == 0 and part == 0:
                        pe.wait_ge(s_curv, 4 * p + 2 * (hh + 1))
                    if part == 0:
                        pe.wait_ge(turning.lo, BATCHES * p + batches_through(4 * group + 3))
                        wait_if(pe, s_ol, 4 * p + group)
                    for j in range(*cuts[g]):
                        qs = max(0, j - 4) * P if g == 0 else j * P
                        ends = j == (TB, TB // 2)[g] - 1
                        for m, (v, pt) in enumerate(((v_hi, pt_hi), (v_lo, pt_hi), (v_hi, pt_lo))):
                            mm = pe.matmul(ps[hh * 64:hh * 64 + 64, 7, qs:512], v[:, j, hh * 64:hh * 64 + 64],
                                           pt[g][:, j, qs:512], start=(j == 0 and m == 0),
                                           stop=(ends and m == 2), skip_group_check=True)
                    if part == 1:
                        mm.then_inc(s_pv, 1)
                if not kind:
                    start_product(pe, slot, feed_o0, mix_hi, mix_lo, (s_ol, 4 * (N_PAIRS - 1)),
                                  (s_sfree, STEPS * N_PAIRS))
                kind_then, p, t = trailing(pair, slot, kind, prev, None, 0)
                if prev is None and kind_then and t == 0:
                    pe.wait_ge(s_pjl, 6)
                if kind_then == "sb":
                    turning.turn(pe, p, t, s_wsb, STEPS * p + t + 1, False)
                elif kind_then == "fox":
                    turning.turn(pe, p, t, s_wfox, STEPS * (p - N_SB // 2) + t + 1, True)

        def mix_views(group, pair):
            hh, g = group // 2, group % 2
            rows, cols = slice(hh * 64, hh * 64 + 64), slice((1 - g) * 512, (1 - g) * 512 + 512)
            return mix_hi[rows, pair, cols], mix_lo[rows, pair, cols], ps[rows, 7, :]

        def pair_scalar(act, pair, kind, prev, project):
            own = pair - N_SB // 2
            for slot in slots_of(kind, prev, 5):
                t, n = slot, (query_block(slot) + 1) * P
                for e, p in proj_ends(slot, pair, project, prev is None) if kind else ():
                    proj_evac_hi(act, e, p)
                turned, p, at = trailing(pair, slot, kind, prev, None, 1)
                if turned:
                    if prev is None and at == 0:
                        act.wait_ge(s_tabst, 64)
                    turning.write_hi(act, p, at)
                found = group_in(slot, 4, pair, kind, prev)
                if found:
                    p, group = found
                    hi, _, src = mix_views(group, p)
                    act.wait_ge(s_pv, 4 * p + group + 1)
                    act.activation(hi, src, ACT.Copy).then_inc(s_oh, 1)
                if kind == "sb":
                    act.wait_ge(s_qk, STEPS * pair + t + 1)
                    wait_if(act, s_sub, STEPS * pair + t - 3)
                    act.activation(score_z[t % 4][:, 0:n], banks(2 * (t % 2))[:, 0:n], ACT.Copy,
                                   scale=SB_SCALE).then_inc(s_sfree, 1)
                two_back, p2, t2 = trailing(pair, slot, kind, prev, 2)
                n2 = (query_block(t2) + 1) * P
                if two_back == "fox":
                    act.wait_ge(s_ri, STEPS * (p2 - N_SB // 2) + t2 + 1)
                    wait_if(act, turning.made, turning.prob_free(p2, t2))
                    act.activation(parts0[t2 % 4][0][:, 0:n2], prob[t2 % 4][:, 0:n2], ACT.Copy,
                                   scale=row_inv[:, t2 % 4:t2 % 4 + 1]).then_inc(s_ph, 1)
                if kind == "fox":
                    act.wait_ge(s_nm, STEPS * (pair - N_SB // 2) + t + 1)
                    if t < 4 and prev == "sb":
                        act.wait_ge(turning.made, turning.prob_free(pair, t))
                    else:
                        p4, t4 = before(own, t, 4)
                        act.wait_ge(s_wfox, STEPS * p4 + t4 + 1)
                    act.activation(prob[t % 4][:, 0:n], banks(2 * (t % 2))[:, 0:n], ACT.Exp, scale=SB_SCALE,
                                   bias=neg_max[:, t % 4:t % 4 + 1],
                                   accum_out=row_sum[:, t % 4:t % 4 + 1]).then_inc(s_sfree, 1)
                one_back, p1, t1 = trailing(pair, slot, kind, prev, 1)
                soft = soft_a[t1 % 2][:, 0:(query_block(t1) + 1) * P]
                if one_back == "sb":
                    act.wait_ge(s_ab, STEPS * p1 + t1 + 1)
                    act.activation(soft, soft, ACT.Exp, scale=-1.0).then_inc(s_e, 1)
                if one_back == "sb":
                    act.wait_ge(s_e, STEPS * p1 + t1 + 1)
                    act.activation(soft, soft, ACT.Ln, bias=1.0).then_inc(s_ln, 1)
                if two_back == "sb":
                    w = prob[t2 % 4][:, 0:n2]
                    act.wait_ge(s_sub, STEPS * p2 + t2 + 1)
                    act.activation(w, w, ACT.Exp).then_inc(s_wsb, 1)

        def pair_vector(dve, pair, kind, prev, project):
            own = pair - N_SB // 2
            for slot in slots_of(kind, prev, 5):
                t, n = slot, (query_block(slot) + 1) * P
                for e, p in proj_ends(slot, pair, project, prev is None) if kind else ():
                    proj_evac_lo(dve, e, p)
                turned, p, at = trailing(pair, slot, kind, prev, None, 1)
                if turned:
                    turning.write_lo(dve, p, at)
                found = group_in(slot, 4, pair, kind, prev)
                if found:
                    p, group = found
                    hi, lo, src = mix_views(group, p)
                    dve.wait_ge(s_oh, 4 * p + group + 1)
                    dve.tensor_tensor(lo, src, hi, ALU.subtract).then_inc(s_ol, 1)
                kind1, p1, t1 = trailing(pair, slot, kind, prev, 1)
                n1 = (query_block(t1) + 1) * P
                if kind == "sb":
                    z = score_z[t % 4][:, 0:n]
                    dve.wait_ge(s_sfree, STEPS * pair + t + 1)
                    wait_if(dve, s_sc, STEPS * pair + t - 1)
                    dve.scalar_tensor_tensor(soft_a[t % 2][:, 0:n], z, -1.0, z, ALU.mult,
                                             ALU.max).then_inc(s_ab, 1)
                    wait_if(dve, turning.made, turning.prob_free(pair, t))
                    dve.tensor_scalar(prob[t % 4][:, 0:n], z, 0.0, None, ALU.max).then_inc(s_r, 1)
                if kind == "fox":
                    dve.wait_ge(s_qk, STEPS * pair + t + 1)
                    dve.tensor_reduce(row_max[:, t % 4:t % 4 + 1], banks(2 * (t % 2))[:, 0:n], AX.X,
                                      ALU.max).then_inc(s_mx, 1)
                    dve.wait_ge(s_mx, STEPS * own + t + 1)
                    dve.tensor_scalar(neg_max[:, t % 4:t % 4 + 1], row_max[:, t % 4:t % 4 + 1], -SB_SCALE, None,
                                      ALU.mult).then_inc(s_nm, 1)
                if kind1 == "fox":
                    dve.wait_ge(s_sfree, STEPS * p1 + t1 + 1)
                    dve.reciprocal(row_inv[:, t1 % 4:t1 % 4 + 1], row_sum[:, t1 % 4:t1 % 4 + 1]).then_inc(s_ri, 1)
                two_back, p2, t2 = trailing(pair, slot, kind, prev, 2)
                n2 = (query_block(t2) + 1) * P
                if two_back == "fox":
                    dve.wait_ge(s_ph, STEPS * (p2 - N_SB // 2) + t2 + 1)
                    dve.scalar_tensor_tensor(parts0[t2 % 4][1][:, 0:n2], prob[t2 % 4][:, 0:n2],
                                             row_inv[:, t2 % 4:t2 % 4 + 1], parts0[t2 % 4][0][:, 0:n2],
                                             ALU.mult, ALU.subtract).then_inc(s_wfox, 1)
                if kind1 == "sb":
                    dve.wait_ge(s_r, STEPS * p1 + t1 + 1)
                    dve.wait_ge(s_ln, STEPS * p1 + t1 + 1)
                    back = slice(n1 - 1, None, -1)
                    dve.tensor_tensor_scan(prob[t1 % 4][:, back], prob[t1 % 4][:, back], soft_a[t1 % 2][:, back],
                                           0.0, ALU.add, ALU.add).then_inc(s_sc, 1)
                if kind and prev:
                    if slot == 0:
                        make_current_qk(dve, 1, pair)
                    elif slot == 1:
                        make_current_v(dve, 0, pair)
                    elif slot == 5:
                        make_current_v(dve, 1, pair)
                if project and slot == 11:
                    make_current_qk(dve, 0, pair + 1)

        def split_qkv_hi(pool, n, pair):
            pool.wait_ge(w_loaded[n], 16 * (feed_qkv.use(n, pair) + 1))
            pool.wait_ge(s_pj, 6 * (pair - 1) + 2 * (n + 1))
            pool.tensor_tensor(w_hi[n][:, :], w_stage[n][:, :], ones[:, 0:1].to_broadcast([P, KT * P]),
                               ALU.mult).then_inc(w_cast[n], 1)

        def split_qkv_lo(pool, n, pair):
            pool.wait_ge(w_cast[n], feed_qkv.use(n, pair) + 1)
            pool.tensor_tensor(w_lo[n][:, :], w_stage[n][:, :], w_hi[n][:, :], ALU.subtract).then_inc(w_split[n], 1)

        def pair_gpsimd_sb(pool, pair):
            for t in range(STEPS):
                n = (query_block(t) + 1) * P
                pool.wait_ge(s_sc, STEPS * pair + t + 1)
                pool.tensor_tensor(prob[t % 4][:, 0:n], score_z[t % 4][:, 0:n], prob[t % 4][:, 0:n],
                                   ALU.subtract).then_inc(s_sub, 1)
                if t == 2:
                    split_qkv_hi(pool, 2, pair + 1)
                elif t == 3:
                    split_qkv_lo(pool, 2, pair + 1)
                elif t in (6, 11):
                    split_qkv_hi(pool, t // 11, pair + 2)
                elif t in (7, 12):
                    split_qkv_lo(pool, t // 12, pair + 2)

        def pick_head(pool, pair, hh):
            if not isinstance(pair, int) or pair > N_SB // 2:
                pool.wait_ge(s_qk, STEPS * (pair - 1) + 8 * (hh + 1))
            pool.tensor_copy(pick_now[:, hh:hh + 1, :],
                             cum_pick[:, bass.ds(2 * (pair - N_SB // 2) + hh, 1), :]).then_inc(s_pick, 1)

        def all_pairs(eng, each):
            first_fox = N_SB // 2
            each(eng, 0, "sb", None, True)
            with eng.Fori(1, first_fox) as pair:
                each(eng, pair, "sb", "sb", True)
            each(eng, first_fox, "fox", "sb", True)
            with eng.Fori(first_fox + 1, N_PAIRS - 1) as pair:
                each(eng, pair, "fox", "fox", True)
            each(eng, N_PAIRS - 1, "fox", "fox", False)
            each(eng, N_PAIRS, None, "fox", False)

        def rotary_angles(dve, t):
            def then(ins, step):
                ins.then_inc(s_tab, 1)
                dve.wait_ge(s_tab, 11 * t + step)

            if t == 0:
                dve.wait_ge(s_pos, 32)
                then(dve.tensor_copy(pos_f[:, :], pos_i[:, :]), 1)
            else:
                then(dve.tensor_copy(tiny[:, 0:1], rope_rows[:, 0:1]), 1)
            then(dve.tensor_scalar(angle[:, :], pos_f[:, :], rope_rows[:, 2 * t:2 * t + 1], None, ALU.mult), 2)
            then(dve.tensor_scalar(turns[:, :], angle[:, :], inv_2pi, magic, ALU.mult, ALU.add), 3)
            then(dve.tensor_scalar(turns[:, :], turns[:, :], -magic, None, ALU.add), 4)
            for n, c in enumerate((pi_a, pi_b, pi_c)):
                then(dve.scalar_tensor_tensor(angle[:, :], turns[:, :], -c, angle[:, :], ALU.mult, ALU.add), 5 + n)
            then(dve.tensor_scalar(angle[:, :], angle[:, :], pi_max, -pi_max, ALU.min, ALU.max), 8)

        def rotary_sines(act, t):
            act.wait_ge(s_tab, 11 * t + 8)
            if t:
                act.wait_ge(s_tabst, 32)
            act.activation(rope_s[:, :], angle[:, :], ACT.Sin).then_inc(s_sin, 1)
            act.activation(rope_c[:, :], angle[:, :], ACT.Sin, scale=0.5).then_inc(s_sin, 1)

        def rotary_finish(dve, t):
            dve.wait_ge(s_sin, 2 * t + 2)
            dve.tensor_tensor(rope_c[:, :], rope_c[:, :], rope_c[:, :], ALU.mult).then_inc(s_tab, 1)
            dve.wait_ge(s_tab, 11 * t + 9)
            dve.tensor_scalar(rope_c[:, :], rope_c[:, :], -2.0, 1.0, ALU.mult, ALU.add).then_inc(s_tab, 1)
            dve.tensor_scalar(rope_s[:, :], rope_s[:, :], rope_rows[:, 2 * t + 1:2 * t + 2], None,
                              ALU.mult).then_inc(s_tab, 1)

        def rotary_store(act, t):
            act.wait_ge(s_tab, 11 * t + 11)
            for c, tab in enumerate((rope_c, rope_s)):
                act.dma_start(tables[2 * t + c], tab[:, :]).then_inc(s_tabst, 16)

        def heads_sync(sp):
            load_rest(sp, feed_qkv)
            load_first(sp, feed_o0)
            sp.wait_ge(s_tabst, 64)

        def heads_gpsimd(pool):
            for n in range(2):
                split_qkv_hi(pool, n, 1)
                split_qkv_lo(pool, n, 1)
            for hh in range(2):
                pick_head(pool, N_SB // 2, hh)
            with pool.Fori(0, N_SB // 2) as pair:
                pair_gpsimd_sb(pool, pair)
            with pool.Fori(N_SB // 2, N_PAIRS - 2) as pair:
                split_qkv_hi(pool, 2, pair + 1)
                split_qkv_lo(pool, 2, pair + 1)
                for n in range(2):
                    split_qkv_hi(pool, n, pair + 2)
                    split_qkv_lo(pool, n, pair + 2)
                    pick_head(pool, pair + 1, n)
            split_qkv_hi(pool, 2, N_PAIRS - 1)
            split_qkv_lo(pool, 2, N_PAIRS - 1)
            for hh in range(2):
                pick_head(pool, N_PAIRS - 1, hh)
            split_first(pool, feed_o0, (3,))
            pool.wait_ge(s_pj, 6 * N_PAIRS)
            split_first(pool, feed_o0, (0, 1, 2))

        def heads_tensor(pe):
            for e in range(6):
                proj_half(pe, e, 0, range(8))
            pe.wait_ge(s_gact, 1)
            pe.wait_ge(s_gdve, GATE_STEPS)
            pe.wait_ge(s_const, CONST_STEPS)
            all_pairs(pe, pair_tensor)

        def heads_scalar(act):
            rotary_sines(act, 0)
            rotary_store(act, 0)
            proj_evac_hi(act, 0, 0)
            proj_evac_hi(act, 1, 0)
            rotary_sines(act, 1)
            act.preload_act_table_set("natural_log_exp_and_others")
            for e in range(2, 6):
                proj_evac_hi(act, e, 0)
            rotary_store(act, 1)
            all_pairs(act, pair_scalar)

        def heads_vector(dve):
            rotary_finish(dve, 0)
            proj_evac_lo(dve, 0, 0)
            proj_evac_lo(dve, 1, 0)
            rotary_angles(dve, 1)
            proj_evac_lo(dve, 2, 0)
            proj_evac_lo(dve, 3, 0)
            for hh in range(2):
                make_current_qk(dve, hh, 0)
            rotary_finish(dve, 1)
            proj_evac_lo(dve, 4, 0)
            proj_evac_lo(dve, 5, 0)
            for hh in range(2):
                make_current_v(dve, hh, 0)
            all_pairs(dve, pair_vector)

        opening = phase(start_sync, start_gpsimd, start_tensor, start_scalar, start_vector)
        heads = phase(heads_sync, heads_gpsimd, heads_tensor, heads_scalar, heads_vector)

        def back_and_norm(tag, feed, act_hi, act_lo, cuts, names, free_at, next_feed, load_x=None, final=None,
                          after=None, meanwhile=None, started=None):
            pps = len(cuts)
            body = len(feed.pieces) // pps
            room = Room(free_at)
            yt = [room(f"yt{b}_{tag}", [P, SEQ], F32) for b in range(2)]
            ln_stats = room(f"ln_stats_{tag}", [P, TB, KT * 6], F32)
            g_rows = room(f"g_rows_{tag}", [P, D_MODEL], F32)
            b_rows = room(f"b_rows_{tag}", [P, D_MODEL], F32)
            s_gb, s_x = sem(f"{tag}_gb_loaded"), sem(f"{tag}_x_loaded")
            s_yt, s_yT, s_acc = sem(f"{tag}_yt_written"), sem(f"{tag}_yt_transposed"), sem(f"{tag}_accumulated")
            s_st, s_mv, s_sd, s_rs = [sem(f"{tag}_{n}") for n in ("stats", "moments", "deviation", "rstd")]
            s_n, s_g, s_b = sem(f"{tag}_normed"), sem(f"{tag}_scaled"), sem(f"{tag}_shifted")
            s_bv = sem(f"{tag}_shifted_by_vector") if final is not None else None
            s_nt, s_nh, s_nl = sem(f"{tag}_norm_transposed"), sem(f"{tag}_norm_hi"), sem(f"{tag}_norm_lo")
            s_out = sem(f"{tag}_stored")

            def col_slice(strip):
                return bass.ds(strip * P, P)

            def sync_program(sp):
                if started:
                    sp.wait_ge(*started)
                if load_x is not None:
                    sp.dma_start(x_res[:, :, :], load_x).then_inc(s_x, 16)
                load_rest(sp, feed)
                if after:
                    sp.wait_ge(after["hidden_lo"], FT)
                sp.dma_start(g_rows[:, :], names[0]).then_inc(s_gb, 16)
                sp.dma_start(b_rows[:, :], names[1]).then_inc(s_gb, 16)
                if next_feed is not None:
                    load_first(sp, next_feed)
                if final is not None:
                    for b in range(TB):
                        sp.wait_ge(s_bv if b % 2 else s_b, b // 2 + 1)
                        sp.dma_start(final[b], x_res[:, b, :]).then_inc(s_out, 16)
                    sp.wait_ge(s_out, 16 * TB)

            def gpsimd_program(pool):
                split_rest(pool, feed)
                if next_feed is not None:
                    split_first(pool, next_feed, (0, 1))
                pool.wait_ge(s_gb, 32)
                for b in range(0, TB, 1 if final is None else 2):
                    pool.wait_ge(s_g, b + 1)
                    pool.tensor_tensor(x_res[:, b, :], x_res[:, b, :], b_rows[:, :], ALU.add).then_inc(s_b, 1)
                if next_feed is not None:
                    split_first(pool, next_feed, (2, 3))

            def tensor_program(pe):
                def turn(i, r):
                    strip = body * i + r
                    pe.wait_ge(s_yt, strip + 1)
                    wait_if(pe, s_acc, 2 * (strip - 1))
                    for b in range(TB):
                        mm = pe.transpose(ps[:, 4 + 2 * (r % 2) + b // 4, b % 4 * P:(b % 4 + 1) * P],
                                          yt[r % 2][:, b * P:(b + 1) * P], ident[:, :])
                    mm.then_inc(s_yT, 1)

                def strip_pair(i, first):
                    for r in range(body):
                        if not first or r >= 2:
                            pe.wait_ge(s_yt, since(body * i, r - 1))
                        for c, (a, b) in enumerate(cuts):
                            if after and first and r == 0:
                                pe.wait_ge(after["hidden_lo"], b)
                                if c == 0:
                                    pe.wait_ge(after["gate_copied"], FT - 1)
                            if started and first and r == 0:
                                pe.wait_ge(*started)
                                product_tile(pe, feed, act_hi, act_lo, KT - 1).then_inc(w_used[feed.slot(0)], 1)
                            else:
                                products(pe, feed, r * pps + c, i, 2 * (r % 2), act_hi, act_lo, a, b,
                                         c == 0, c == pps - 1)
                        if r:
                            turn(i, r - 1)
                    turn(i, body - 1)

                strip_pair(0, True)
                with pe.Fori(1, feed.iters) as i:
                    strip_pair(i, False)
                if final is None:
                    for b in range(TB):
                        pe.wait_ge(s_b, b + 1)
                        pe.wait_ge(s_nl, max(2 * (b - 1), 0))
                        for k in range(KT):
                            mm = pe.transpose(ps[:, 4 + 2 * (b % 2) + k // 4, k % 4 * P:(k % 4 + 1) * P],
                                              x_res[:, b, k * P:(k + 1) * P], ident[:, :])
                        mm.then_inc(s_nt, 1)
                        if meanwhile:
                            meanwhile(pe, b, s_nl)
                    if not meanwhile:
                        pe.wait_ge(s_nl, 2 * TB)

            def scalar_program(act):
                with act.Fori(0, feed.iters) as i:
                    for r in range(body):
                        n = r * pps + pps - 1
                        act.wait_ge(w_used[feed.slot(n)], feed.used(n, i) + 1)
                        act.wait_ge(s_yT, since(body * i, r - 1))
                        act.activation(yt[r % 2][:, :], banks(2 * (r % 2)), ACT.Copy).then_inc(s_yt, 1)
                act.wait_ge(s_mv, TB + 1)
                act.activation(ln_rstd[:, :], ln_rstd[:, :], ACT.Sqrt).then_inc(s_sd, 1)
                act.wait_ge(s_rs, 2)

                def norm(b):
                    act.activation(x_res[:, b, :], x_res[:, b, :], ACT.Identity, scale=ln_rstd[:, b:b + 1],
                                   bias=ln_shift[:, b:b + 1]).then_inc(s_n, 1)

                ahead = 3 if final is None else TB
                for b in range(ahead):
                    norm(b)
                if final is None:
                    for b in range(TB):
                        act.wait_ge(s_nt, b + 1)
                        if b + ahead < TB:
                            norm(b + ahead)
                        for h in range(2):
                            act.activation(xt_hi[:, 4 * h:4 * h + 4, b * P:(b + 1) * P],
                                           ps[:, 4 + 2 * (b % 2) + h, :].rearrange("p (k n) -> p k n", k=4),
                                           ACT.Copy).then_inc(s_nh, 1)

            def vector_program(dve):
                if load_x is not None:
                    dve.wait_ge(s_x, 16)
                with dve.Fori(0, feed.iters) as i:
                    for r in range(body):
                        dve.wait_ge(s_yT, body * i + r + 1)
                        for h in range(2):
                            cell = x_res[:, 4 * h:4 * h + 4, col_slice(body * i + r)]
                            dve.scalar_tensor_tensor(
                                cell, cell, ALPHA,
                                ps[:, 4 + 2 * (r % 2) + h, :].rearrange("p (b n) -> p b n", b=4),
                                ALU.mult, ALU.add).then_inc(s_acc, 1)
                        wait_apart(dve, (s_acc, 2), (s_acc, 2 * (body * i + r + 1)))
                        for b in range(TB):
                            dve.bn_stats(ln_stats[:, b, bass.ds(6 * (body * i + r), 6)],
                                         x_res[:, b, col_slice(body * i + r)]).then_inc(s_st, 1)
                dve.wait_ge(s_st, TB * KT)
                for b in range(TB):
                    dve.bn_aggr(ln_mv[:, b, :], ln_stats[:, b, :]).then_inc(s_mv, 1)
                dve.wait_ge(s_mv, TB)
                dve.tensor_scalar(ln_rstd[:, :], ln_mv[:, :, 1], LN_EPS, None, ALU.add).then_inc(s_mv, 1)
                dve.wait_ge(s_sd, 1)
                dve.reciprocal(ln_rstd[:, :], ln_rstd[:, :]).then_inc(s_rs, 1)
                dve.wait_ge(s_rs, 1)
                dve.scalar_tensor_tensor(ln_shift[:, :], ln_mv[:, :, 0], -1.0, ln_rstd[:, :], ALU.mult,
                                         ALU.mult).then_inc(s_rs, 1)
                dve.wait_ge(s_gb, 32)

                def lows(b):
                    for h in range(2):
                        dve.wait_ge(s_nh, 2 * b + h + 1)
                        dve.tensor_tensor(xt_lo[:, 4 * h:4 * h + 4, b * P:(b + 1) * P],
                                          ps[:, 4 + 2 * (b % 2) + h, :].rearrange("p (k n) -> p k n", k=4),
                                          xt_hi[:, 4 * h:4 * h + 4, b * P:(b + 1) * P],
                                          ALU.subtract).then_inc(s_nl, 1)

                for b in range(TB):
                    dve.wait_ge(s_n, b + 1)
                    dve.tensor_tensor(x_res[:, b, :], x_res[:, b, :], g_rows[:, :], ALU.mult).then_inc(s_g, 1)
                    if final is not None and b % 2:
                        dve.wait_ge(s_g, b + 1)
                        dve.tensor_tensor(x_res[:, b, :], x_res[:, b, :], b_rows[:, :], ALU.add).then_inc(s_bv, 1)
                    if final is None and b >= 2:
                        lows(b - 2)
                if final is None:
                    lows(TB - 2)
                    lows(TB - 1)

            return phase(sync_program, gpsimd_program, tensor_program, scalar_program, vector_program)

        hroom = Room(arena)
        hid_hi = hroom("hid_hi", [P, FT, SEQ], BF16)
        hid_lo = hroom("hid_lo", [P, FT, SEQ], BF16)
        after_hid = hroom.at

        def early_strips(feed):
            parts = {4: (0, range(0, 4)), 5: (0, range(4, 8)), 6: (1, range(0, 4)), 7: (1, range(4, 8))}

            def meanwhile(pe, b, norm_lo):
                if b in parts:
                    n, ks = parts[b]
                    if ks[0] == 0:
                        pe.wait_ge(w_split[feed.slot(n)], feed.use(n, 0) + 1)
                    pe.wait_ge(norm_lo, TB)
                    product_part(pe, feed, n, 0, ks)
                if b == TB - 1:
                    pe.wait_ge(norm_lo, 2 * TB)
                    for n in range(2):
                        product_part(pe, feed, n, 1, range(KT)).then_inc(w_used[feed.slot(n)], 1)
            return meanwhile

        def feed_forward_up(tag, feed, conv_rows, next_feed):
            room = Room(after_hid)
            gate = [room(f"gate{a}_{tag}", [P, SEQ + 2], F32) for a in range(2)]
            conv = [room(f"conv{a}_{tag}", [P, SEQ], F32) for a in range(2)]
            conv_w = sb(f"conv_w_{tag}", [P, FT * 4], F32, 2560)
            assert keep.at <= 2560
            s_cw, s_zero = sem(f"{tag}_conv_w"), sem(f"{tag}_gate_pad")
            s_gt, s_cv, s_ge, s_hm, s_hh, s_hl = [sem(f"{tag}_{n}") for n in
                ("gate_copied", "conv_step", "gelu", "hidden", "hidden_hi", "hidden_lo")]

            def sync_program(sp):
                sp.dma_start(conv_w[:, :], conv_rows).then_inc(s_cw, 16)
                load_rest(sp, feed)
                load_first(sp, next_feed)

            def gpsimd_program(pool):
                for a in range(2):
                    pool.memset(gate[a][:, 0:2], 0.0).then_inc(s_zero, 1)
                split_rest(pool, feed)
                split_first(pool, next_feed)

            def tensor_program(pe):
                products(pe, feed, 2, 0, 4, xt_hi, xt_lo, 0, KT, True, True)
                products(pe, feed, 3, 0, 6, xt_hi, xt_lo, 0, KT, True, True)
                with pe.Fori(1, feed.iters) as i:
                    for a in range(2):
                        pe.wait_ge(s_gt, 2 * i - 1 + a)
                        products(pe, feed, 2 * a, i, 4 * a, xt_hi, xt_lo, 0, KT, True, True)
                        pe.wait_ge(s_hm, 2 * i - 1 + a)
                        products(pe, feed, 2 * a + 1, i, 4 * a + 2, xt_hi, xt_lo, 0, KT, True, True)

            def scalar_program(act):
                with act.Fori(0, feed.iters) as i:
                    for a in range(2):
                        act.wait_ge(w_used[2 * a], feed.used(2 * a, i) + 1)
                        act.wait_ge(s_cv, 3 * (2 * i))
                        act.activation(gate[a][:, 2:SEQ + 2], banks(4 * a), ACT.Copy).then_inc(s_gt, 1)
                        act.wait_ge(s_cv, 3 * (2 * i + a + 1))
                        act.activation(conv[a][:, :], conv[a][:, :], ACT.Gelu_apprx_tanh).then_inc(s_ge, 1)
                        act.wait_ge(s_hm, 2 * i + a + 1)
                        act.activation(hid_hi[:, 2 * i + a, :], conv[a][:, :], ACT.Copy).then_inc(s_hh, 1)

            def vector_program(dve):
                dve.wait_ge(s_cw, 16)
                dve.wait_ge(s_zero, 2)
                with dve.Fori(0, feed.iters) as i:
                    for a in range(2):
                        m = 2 * i + a

                        def tap(j):
                            return conv_w[:, bass.ds(4 * m + j, 1)]

                        dve.wait_ge(s_gt, m + 1)
                        dve.wait_ge(s_hl, 2 * i)
                        dve.tensor_scalar(conv[a][:, :], gate[a][:, 0:SEQ], tap(0), tap(3), ALU.mult,
                                          ALU.add).then_inc(s_cv, 1)
                        dve.wait_ge(s_cv, 3 * m + 1)
                        dve.scalar_tensor_tensor(conv[a][:, :], gate[a][:, 1:SEQ + 1], tap(1), conv[a][:, :],
                                                 ALU.mult, ALU.add).then_inc(s_cv, 1)
                        dve.wait_ge(s_cv, 3 * m + 2)
                        dve.scalar_tensor_tensor(conv[a][:, :], gate[a][:, 2:SEQ + 2], tap(2), conv[a][:, :],
                                                 ALU.mult, ALU.add).then_inc(s_cv, 1)
                        dve.wait_ge(s_ge, m + 1)
                        dve.wait_ge(w_used[2 * a + 1], feed.used(2 * a + 1, i) + 1)
                        dve.tensor_tensor(conv[a][:, :], conv[a][:, :], banks(4 * a + 2), ALU.mult).then_inc(s_hm, 1)
                        dve.wait_ge(s_hh, m + 1)
                        dve.tensor_tensor(hid_lo[:, m, :], conv[a][:, :], hid_hi[:, m, :],
                                          ALU.subtract).then_inc(s_hl, 1)

            programs = phase(sync_program, gpsimd_program, tensor_program, scalar_program, vector_program)
            return programs, dict(hidden_lo=s_hl, gate_copied=s_gt)

        up0, up0_sems = feed_forward_up("up0", feed_up0, t_in["l0_conv"], feed_down0)
        run_phases(
            opening, heads,
            back_and_norm("o0", feed_o0, mix_hi, mix_lo, [(0, KT)], (t_in["l0_ln1_g"], t_in["l0_ln1_b"]),
                          arena + 32 * KB, feed_up0, load_x=t_in["x"], meanwhile=early_strips(feed_up0),
                          started=(s_ol, 4 * N_PAIRS)),
            up0,
            back_and_norm("dn0", feed_down0, hid_hi, hid_lo, DOWN_CUT, (t_in["l0_ln2_g"], t_in["l0_ln2_b"]),
                          after_hid, feed_small, after=up0_sems))

        clear_sems()

        span = [(i + 1) * P for i in range(TB)]
        at_of = [sum(span[:i]) for i in range(TB)]
        picky = [i for i in range(TB) if (i + 1) * P > TOPK]
        sc_at = {i: at_of[i] - at_of[picky[0]] for i in picky}
        room = Room(arena)
        lat_hi, lat_lo = [room(n, [P, 2, SEQ], BF16) for n in ("lat_hi", "lat_lo")]
        val_hi = room("val_hi", [P, TB, LATENT + 64], BF16)
        val_lo = room("val_lo", [P, TB, P], BF16)
        hide = room("hide", [P, sum(span)], BF16)
        score = room("score", [P, sum(span[i] for i in picky)], F32)
        rope_q = [room(n, [ROPE, SEQ], F32) for n in ("rope_q_cos", "rope_q_sin")]
        after_score = room.at
        rope_i = [room(n, [P, SEQ], F32) for n in ("rope_i_cos", "rope_i_sin")]
        w_idx = room("w_idx", [P, TB, IDX_HEADS], F32)
        qi_hi, qi_lo = [room(n, [P, KT, SEQ], BF16) for n in ("qi_hi", "qi_lo")]
        ki_hi = [room(f"ki_hi{h}", [P, SEQ], BF16) for h in range(2)]
        ki_lo = [room(f"ki_lo{h}", [P, SEQ], BF16) for h in range(2)]
        strip_f = room("strip_f", [P, SEQ], F32)
        strip_w = room("strip_w", [P, SEQ], F32)
        relu = [strip_f, strip_w]

        s_tl5 = sem("tables_loaded")
        s_f5, s_c5, s_s5, s_a5, s_h5, s_l5 = [sem(n) for n in
            ("strip_copied", "strip_cos", "strip_sin", "strip_rotated", "strip_hi", "strip_lo")]
        s_v5h, s_v5l, s_w5, s_z5 = sem("val_hi_written"), sem("val_lo_written"), sem("w_idx_written"), sem("zeros_written")
        s_iq, s_ir, s_ia, s_i0 = sem("idx_product"), sem("idx_relu"), sem("idx_added"), sem("score_zeroed")

        idx_steps = 2 * len(picky)

        def idx_bank(t):
            return 2 * ((t + 1) % 4)

        def over_index_strips(eng, each):
            each(0)
            with eng.Fori(1, KT) as p:
                each(p)

        def copy_strip(act, bank, kind, wait_prev):
            act.wait_ge(s_l5, wait_prev)
            src = banks(bank)
            swaps = {"idx": (0, 32, 64, 96), "lat": (0, 32), "plain": ()}[kind]
            for a in swaps:
                b = a + 32 if a % 64 == 0 else a - 32
                act.activation(strip_w[b:b + 32, :], src[a:a + 32, :], ACT.Copy)
            act.activation(strip_f[:, :], src, ACT.Copy).then_inc(s_f5, 1)

        def strip_kind(m):
            return "idx" if m == 0 or m >= 3 else ("lat" if m == 1 else "plain")

        def index_sync(sp):
            for t, tab in ((0, rope_i), (2, rope_q)):
                for c in range(2):
                    rows = P if t == 0 else ROPE
                    sp.dma_start(tab[c][0:rows, :], tables[t + c][0:rows, :]).then_inc(s_tl5, 16)
            load_rest(sp, feed_small)
            load_first(sp, feed_qidx)
            load_rest(sp, feed_qidx)
            load_first(sp, feed_q)

        def index_gpsimd(pool):
            split_rest(pool, feed_small)
            split_first(pool, feed_qidx)
            split_rest(pool, feed_qidx)
            split_first(pool, feed_q)

        def v_strip(pe, n, cols, bank):
            slot = feed_small.slot(n)
            pe.wait_ge(w_split[slot], feed_small.use(n, 0) + 1)
            for b in range(TB):
                for k in range(KT):
                    for m, (a, w) in enumerate(((xt_hi, w_hi), (xt_lo, w_hi), (xt_hi, w_lo))):
                        mm = pe.matmul(ps[:, bank + b // 4, b % 4 * cols:(b % 4 + 1) * cols],
                                       a[:, k, b * P:(b + 1) * P], w[slot][:, k * cols:(k + 1) * cols],
                                       start=(k == 0 and m == 0), stop=(k == KT - 1 and m == 2))
            mm.then_inc(w_used[slot], 1)

        def index_tensor(pe):
            for n in range(3):
                products(pe, feed_small, n, 0, 2 * n, xt_hi, xt_lo, 0, KT, True, True)
            v_strip(pe, 3, P, 6)
            pe.wait_ge(s_f5, 1)
            v_strip(pe, 4, 80, 0)
            pe.wait_ge(s_f5, 3)
            with pe.Fori(0, feed_qidx.iters) as i:
                for r in range(4):
                    pe.wait_ge(s_f5, 4 * i + r)
                    if r == 2:
                        pe.wait_ge(s_v5l, 2)
                    if r == 3:
                        pe.wait_ge(s_v5l, 4)
                        pe.wait_ge(s_w5, 2)
                    products(pe, feed_qidx, r, i, 2 * ((r + 1) % 4), xt_hi, xt_lo, 0, KT, True, True)
            def index_scores(p):
                for t in range(idx_steps):
                    hh, i = t // len(picky), picky[t % len(picky)]
                    n = span[i]
                    if t == 0:
                        pe.wait_ge(s_l5, p + 5)
                    if isinstance(p, int) and t < 4:
                        pe.wait_ge(s_f5, 8 + t)
                    else:
                        pe.wait_ge(s_ir, idx_steps * p + t - 3)
                    for c in range(0, n, 512):
                        w = min(512, n - c)
                        for m, (a, b) in enumerate(((qi_hi, ki_hi), (qi_lo, ki_hi), (qi_hi, ki_lo))):
                            mm = pe.matmul(ps[:, idx_bank(t) + c // 512, 0:w], a[:, p, i * P:(i + 1) * P],
                                           b[hh][:, c:c + w], start=(m == 0), stop=(m == 2))
                    mm.then_inc(s_iq, 1)

            over_index_strips(pe, index_scores)

        def index_scalar(act):
            def write_hi(m, dsts):
                act.wait_ge(s_a5, m + 1)
                for d, rows in dsts:
                    ins = act.activation(d, strip_f[rows, :], ACT.Copy)
                ins.then_inc(s_h5, 1)

            both = [(ki_hi[0][0:64, :], slice(0, 64)), (ki_hi[1][64:128, :], slice(64, 128))]
            for n in range(3):
                act.wait_ge(w_used[feed_small.slot(n)], feed_small.used(n, 0) + 1)
                copy_strip(act, 2 * n, strip_kind(n), (0, 2, 3)[n])
                if n == 0:
                    act.wait_ge(s_z5, 4)
                    write_hi(0, both)
                else:
                    write_hi(n, [(lat_hi[:, n - 1, :], slice(0, P))])
            act.wait_ge(w_used[3], feed_small.used(3, 0) + 1)
            for h in range(2):
                act.activation(val_hi[:, 4 * h:4 * h + 4, 0:P],
                               ps[:, 6 + h, :].rearrange("p (b n) -> p b n", b=4), ACT.Copy).then_inc(s_v5h, 1)
            act.wait_ge(w_used[0], feed_small.used(4, 0) + 1)
            for h in range(2):
                src = ps[:, h, 0:320].rearrange("p (b n) -> p b n", b=4)
                act.activation(w_idx[:, 4 * h:4 * h + 4, :], src[:, :, 64:80], ACT.Copy,
                               scale=IDX_SCALE).then_inc(s_w5, 1)
                act.activation(val_hi[:, 4 * h:4 * h + 4, P:LATENT], src[:, :, 0:64], ACT.Copy).then_inc(s_v5h, 1)
            with act.Fori(0, feed_qidx.iters) as i:
                for r in range(4):
                    m = 3 + 4 * i + r
                    act.wait_ge(w_used[r], feed_qidx.used(r, i) + 1)
                    copy_strip(act, 2 * ((r + 1) % 4), "idx", m + 1)
                    act.wait_ge(s_a5, m + 1)
                    act.activation(qi_hi[:, 4 * i + r, :], strip_f[:, :], ACT.Copy).then_inc(s_h5, 1)
            act.wait_ge(s_l5, 12)

            def index_relu(p):
                for t in range(idx_steps):
                    n = span[picky[t % len(picky)]]
                    act.wait_ge(s_iq, idx_steps * p + t + 1)
                    wait_if(act, s_ia, idx_steps * p + t - 1)
                    act.activation(relu[t % 2][:, 0:n], banks(idx_bank(t))[:, 0:n], ACT.Relu).then_inc(s_ir, 1)

            over_index_strips(act, index_relu)

        def index_vector(dve):
            for h in range(2):
                other = slice(64, 128) if h == 0 else slice(0, 64)
                dve.memset(ki_hi[h][other, :], 0.0).then_inc(s_z5, 1)
                dve.memset(ki_lo[h][other, :], 0.0).then_inc(s_z5, 1)
            dve.memset(score[:, :], 0.0).then_inc(s_i0, 1)
            dve.wait_ge(s_tl5, 64)

            def rotate(m, kind, rotated, tabs):
                rows = {"idx": P, "lat": ROPE, "plain": 0}[kind]
                dve.wait_ge(s_f5, m + 1)
                if not rows:
                    dve.tensor_copy(tiny[:, 0:1], strip_f[:, 0:1]).then_inc(s_a5, 1)
                    return
                f, w = strip_f[0:rows, :], strip_w[0:rows, :]
                dve.tensor_tensor(f, f, tabs[0][0:rows, :], ALU.mult).then_inc(s_c5, 1)
                dve.tensor_tensor(w, w, tabs[1][0:rows, :], ALU.mult).then_inc(s_s5, 1)
                dve.wait_ge(s_c5, rotated + 1)
                dve.wait_ge(s_s5, rotated + 1)
                dve.tensor_tensor(f, f, w, ALU.add).then_inc(s_a5, 1)

            rotate(0, "idx", 0, rope_i)
            dve.wait_ge(s_h5, 1)
            dve.wait_ge(s_a5, 1)
            dve.tensor_tensor(ki_lo[0][0:64, :], strip_f[0:64, :], ki_hi[0][0:64, :], ALU.subtract).then_inc(s_l5, 1)
            dve.tensor_tensor(ki_lo[1][64:128, :], strip_f[64:128, :], ki_hi[1][64:128, :],
                              ALU.subtract).then_inc(s_l5, 1)
            for n in (1, 2):
                rotate(n, "lat" if n == 1 else "plain", n, rope_q)
                dve.wait_ge(s_h5, n + 1)
                dve.wait_ge(s_a5, n + 1)
                dve.tensor_tensor(lat_lo[:, n - 1, :], strip_f[:, :], lat_hi[:, n - 1, :],
                                  ALU.subtract).then_inc(s_l5, 1)
            for h in range(2):
                dve.wait_ge(s_v5h, h + 1)
                dve.tensor_tensor(val_lo[:, 4 * h:4 * h + 4, 0:P],
                                  ps[:, 6 + h, :].rearrange("p (b n) -> p b n", b=4),
                                  val_hi[:, 4 * h:4 * h + 4, 0:P], ALU.subtract).then_inc(s_v5l, 1)
            for h in range(2):
                dve.wait_ge(s_v5h, h + 3)
                dve.tensor_tensor(val_hi[:, 4 * h:4 * h + 4, LATENT:LATENT + 64],
                                  ps[:, h, 0:320].rearrange("p (b n) -> p b n", b=4)[:, :, 0:64],
                                  val_hi[:, 4 * h:4 * h + 4, P:LATENT], ALU.subtract).then_inc(s_v5l, 1)
            with dve.Fori(0, feed_qidx.iters) as i:
                for r in range(4):
                    m = 3 + 4 * i + r
                    rotate(m, "idx", m - 1, rope_i)
                    dve.wait_ge(s_h5, m + 1)
                    dve.tensor_tensor(qi_lo[:, 4 * i + r, :], strip_f[:, :], qi_hi[:, 4 * i + r, :],
                                      ALU.subtract).then_inc(s_l5, 1)
            dve.wait_ge(s_i0, 1)
            dve.wait_ge(s_w5, 2)

            def index_add(p):
                for t in range(idx_steps):
                    hh, i = t // len(picky), picky[t % len(picky)]
                    cell = score[:, sc_at[i]:sc_at[i] + span[i]]
                    dve.wait_ge(s_ir, idx_steps * p + t + 1)
                    wait_if(dve, s_ia, idx_steps * p + t - len(picky) + 1)
                    dve.scalar_tensor_tensor(cell, relu[t % 2][:, 0:span[i]],
                                             w_idx[:, i, bass.ds(2 * p + hh, 1)], cell,
                                             ALU.mult, ALU.add).then_inc(s_ia, 1)

            over_index_strips(dve, index_add)

        q_dram = nc.dram_tensor("q_split", (2 * N_DSA, P, 2, SEQ), BF16, kind="Internal").ap()
        room = Room(after_score)
        q_now_at = (limit - 16 * KB) // 32 * 32
        q_room = Room(q_now_at)
        q_now = [q_room(f"q_now{h}", [P, 2, 2, SEQ], BF16) for h in range(2)]
        best = room("best", [P, len(picky), 8], F32)
        qs_f = [room(f"qs_f{b}", [P, SEQ], F32) for b in range(4)]
        qs_w = [room(f"qs_w{b}", [ROPE, SEQ], F32) for b in range(2)]
        q_out = [room(f"q_out{b}", [P, 2, SEQ], BF16) for b in range(4)]
        s_cp, s_cw6, s_co, s_si, s_ro, s_qh, s_ql = [sem(n) for n in
            ("q_copied", "q_swapped", "q_cos", "q_sin", "q_rotated", "q_hi_written", "q_lo_written")]
        assert room.at <= q_now_at
        s_q7 = [sem(f"q_now_loaded{h}") for h in range(2)]
        s_qst = [sem(f"q_stored{r}") for r in range(4)]
        s_top, s_rep, s_hide = sem("best_found"), sem("best_taken"), sem("hide_written")

        def topk_sync(sp):
            def store(i):
                for r in range(4):
                    sp.wait_ge(s_ql, 4 * i + r + 1)
                    sp.dma_start(q_dram[4 * i + r], q_out[r][:, :, :]).then_inc(s_qst[r], 16)

            for n in range(4):
                load_piece(sp, feed_q, n, 1)
            store(0)
            for r in range(4):
                sp.wait_ge(s_qst[r], 16)
            for h in range(2):
                sp.dma_start(q_now[h][:, :, :, :],
                             q_dram[2 * h:2 * h + 2].rearrange("s p l t -> p s l t")).then_inc(s_q7[h], 16)
            with sp.Fori(2, feed_q.iters) as i:
                for n in range(4):
                    load_piece(sp, feed_q, n, i)
                store(i - 1)
            store(feed_q.iters - 1)
            load_first(sp, feed_o1)

        def over_strips(eng, split, finish):
            with eng.Fori(0, feed_q.iters - 1) as i:
                for r in range(4):
                    finish(r, i)
                    split(r, i + 1)
            for r in range(4):
                finish(r, feed_q.iters - 1)

        def topk_tensor(pe):
            pe.wait_ge(s_ir, idx_steps * KT)
            for r in range(4):
                products(pe, feed_q, r, 0, 2 * r, xt_hi, xt_lo, 0, KT, True, True)
            with pe.Fori(1, feed_q.iters) as i:
                for r in range(4):
                    pe.wait_ge(s_cp, 4 * i + r - 3)
                    products(pe, feed_q, r, i, 2 * r, xt_hi, xt_lo, 0, KT, True, True)

        def topk_scalar(act):
            act.wait_ge(s_ia, idx_steps * KT)
            def split(r, i):
                act.wait_ge(w_loaded[r], 16 * (feed_q.use(r, i) + 1))
                act.wait_ge(w_used[r], feed_q.used(r, i))
                act.activation(w_hi[r][:, :], w_stage[r][:, :], ACT.Copy).then_inc(w_cast[r], 1)

            def finish(r, i):
                act.wait_ge(w_used[r], feed_q.used(r, i) + 1)
                act.wait_ge(s_ql, 4 * i)
                if r % 2 == 0:
                    act.activation(qs_w[r // 2][32:64, :], banks(2 * r)[0:32, :], ACT.Copy)
                    act.activation(qs_w[r // 2][0:32, :], banks(2 * r)[32:64, :], ACT.Copy).then_inc(s_cw6, 1)
                act.activation(qs_f[r][:, :], banks(2 * r), ACT.Copy).then_inc(s_cp, 1)
                if r % 2 == 0:
                    act.wait_ge(s_ro, 2 * i + r // 2 + 1)
                else:
                    act.wait_ge(s_cp, 4 * i + r + 1)
                act.wait_ge(s_qst[r], 16 * i)
                act.activation(q_out[r][:, 0, :], qs_f[r][:, :], ACT.Copy).then_inc(s_qh, 1)

            over_strips(act, split, finish)

        def topk_gpsimd(pool):
            def split(r, i):
                pool.wait_ge(w_loaded[r], 16 * (feed_q.use(r, i) + 1))
                pool.wait_ge(w_used[r], feed_q.used(r, i))
                pool.wait_ge(w_cast[r], feed_q.use(r, i) + 1)
                pool.tensor_tensor(w_lo[r][:, :], w_stage[r][:, :], w_hi[r][:, :], ALU.subtract).then_inc(w_split[r], 1)

            def finish(r, i):
                if r % 2 == 0:
                    f, w = qs_f[r][0:ROPE, :], qs_w[r // 2][:, :]
                    m = 2 * i + r // 2
                    pool.wait_ge(s_cw6, m + 1)
                    pool.tensor_tensor(w, w, rope_q[1][:, :], ALU.mult).then_inc(s_si, 1)
                    pool.wait_ge(s_cp, 4 * i + r + 1)
                    pool.tensor_tensor(f, f, rope_q[0][:, :], ALU.mult).then_inc(s_co, 1)
                    pool.wait_ge(s_si, m + 1)
                    pool.wait_ge(s_co, m + 1)
                    pool.tensor_tensor(f, f, w, ALU.add).then_inc(s_ro, 1)
                pool.wait_ge(s_qh, 4 * i + r + 1)
                pool.tensor_tensor(q_out[r][:, 1, :], qs_f[r][:, :], q_out[r][:, 0, :],
                                   ALU.subtract).then_inc(s_ql, 1)

            over_strips(pool, split, finish)

        def topk_vector(dve):
            dve.wait_ge(s_ia, idx_steps * KT)
            for i in picky:
                end = sc_at[i] + span[i]
                dve.memset(score[0:CHUNK, end - CHUNK:end], HIDDEN_SCORE).then_inc(s_rep, 1)
            with dve.Fori(0, TOPK // 8) as n:
                wait_apart(dve, (s_rep, len(picky)), (s_rep, len(picky) * (n + 1)))
                for c, i in enumerate(picky):
                    dve.max(best[:, c, :], score[:, sc_at[i]:sc_at[i] + span[i]]).then_inc(s_top, 1)
                wait_apart(dve, (s_top, len(picky)), (s_top, len(picky) * (n + 1)))
                for c, i in enumerate(picky):
                    cell = score[:, sc_at[i]:sc_at[i] + span[i]]
                    dve.match_replace(cell, best[:, c, :], cell, TAKEN_SCORE).then_inc(s_rep, 1)
            dve.wait_ge(s_rep, len(picky) * (TOPK // 8 + 1))
            for i in range(TB):
                cell = hide[:, at_of[i]:at_of[i] + span[i]]
                if i in picky:
                    dve.tensor_scalar(cell, score[:, sc_at[i]:sc_at[i] + span[i]], -2e38, MASKED, ALU.is_gt,
                                      ALU.mult).then_inc(s_hide, 1)
                else:
                    dve.memset(cell, 0.0).then_inc(s_hide, 1)
                    dve.wait_ge(s_hide, i + 1)
            for i in range(TB):
                if i not in picky:
                    end = at_of[i] + span[i]
                    dve.memset(hide[0:CHUNK, end - CHUNK:end], MASKED).then_inc(s_hide, 1)

        room = Room(arena + 8 * KB + 2 * TB * LATENT * 2 + (sum(span) * 2 + 31) // 32 * 32)
        prob7 = [room(f"prob7_{b}", [P, SEQ], F32) for b in range(4)]
        parts7 = [[room(f"prob7_{n}{b}", [P, SEQ], BF16) for n in ("hi", "lo")] for b in range(4)]
        uv_at = room.at
        pt7 = [room("pt7_0", [P, 2, TB, 512], BF16), room("pt7_1", [P, 2, TB // 2, 512], BF16)]
        ctx_hi, ctx_lo = [room(n, [P, 2, 512], BF16) for n in ("ctx_hi", "ctx_lo")]
        uv_hi, uv_lo = [room(n, [P, 2, N_DSA, 64], BF16) for n in ("uv_hi", "uv_lo")]
        uvn_hi, uvn_lo = [room(n, [P, 2, 2, 64], BF16) for n in ("uvn_hi", "uvn_lo")]
        uv_f = sb("uv_f", [P, 2, N_DSA, 64], F32, uv_at)
        assert room.at <= q_now_at

        s_uvl, s_uvh, s_uvs, s_uvn = sem("uv_loaded"), sem("uv_hi_written"), sem("uv_lo_written"), sem("uv_current")
        t_qk, t_mx, t_nm, t_ex, t_ri, t_w = [sem(n) for n in
            ("lat_scores", "lat_masked_max", "lat_neg_max", "lat_exp", "lat_inverse", "lat_weights")]
        t_ph = sem("lat_prob_hi")
        t_pv, t_ch, t_cl = sem("lat_context"), sem("lat_context_hi"), sem("lat_context_lo")

        s_turned = sem("lat_turned")
        s_near, s_far = sem("lat_near_moved"), sem("lat_far_moved")
        batch_order = [(t, far) for t in range(STEPS) for far in range(len(batch_list(t)))]

        def moved(t, far):
            return (s_far, STEPS // 2, 4 * (t // 8) + t % 8 + 1) if far else (s_near, STEPS, t + 1)

        def turn_parts(pe, pair, t):
            pe.wait_ge(t_w, STEPS * pair + t + 1)
            for n, j0, m in batch_list(t):
                semaphore, per_pair, value = moved(*batch_order[n - 2])
                wait_if(pe, semaphore, per_pair * (pair if n >= 2 else pair - 1) + value)
                for j in range(m):
                    for a, part in enumerate(parts7[t % 4]):
                        mm = pe.transpose(turned_bank(n)[:, a, j * P:(j + 1) * P],
                                          part[:, (j0 + j) * P:(j0 + j + 1) * P], ident_b[:, :])
                mm.then_inc(s_turned, 1)

        def turned_bank(n):
            return ps[:, 5 + n % 2, :].bitcast(BF16).rearrange("p (a n) -> p a n", a=2)

        def move_parts(eng, pair, t, far):
            if far >= len(batch_list(t)):
                return
            n, j0, m = batch_list(t)[far]
            g, qs = t % 8 // 4, query_block(t) % 4 * P
            if t % 4 == 0:
                wait_if(eng, t_pv, 4 * pair + t // 4 - 1)
            eng.wait_ge(s_turned, BATCHES * pair + n + 1)
            dst = pt7[g][:, :, j0:j0 + m, qs:qs + P]
            src = turned_bank(n)[:, :, 0:m * P].rearrange("p a (b n) -> p a b n", b=m)
            if far:
                eng.tensor_copy(dst, src).then_inc(s_far, 1)
            else:
                eng.activation(dst, src, ACT.Copy).then_inc(s_near, 1)

        def parts_free(pair, t):
            p, last = before(pair, t, 4)
            return BATCHES * p + batches_through(last)

        s_up, s_uph, s_upl = sem("up_projected"), sem("up_hi_written"), sem("up_lo_written")

        def up_views(group, pair):
            hh, g = group // 2, group % 2
            rows, cols = slice(hh * 64, hh * 64 + 64), slice((1 - g) * 512, (1 - g) * 512 + 512)
            return xt_hi[rows, pair, cols], xt_lo[rows, pair, cols], ps[rows, 4, :]

        def context_views(ct):
            return ctx_hi[:, ct, :], ctx_lo[:, ct, :], ps[:, (7, 4)[ct], :]

        def latent_tensor(pe, pair, kind, prev):
            for slot in slots_of(kind, prev, 7):
                if kind:
                    t, i, hh = slot, query_block(slot), slot // 8
                    n = span[i]
                    if t % 8 == 0:
                        pe.wait_ge(s_q7[hh], 16 * (pair + 1))
                    wait_if(pe, t_mx, STEPS * pair + t - 1)
                    qs = slice(i * P, (i + 1) * P)
                    for c in range(0, n, 512):
                        w = min(512, n - c)
                        for kt in range(2):
                            qh, ql = q_now[hh][:, kt, 0, qs], q_now[hh][:, kt, 1, qs]
                            kh, kl = lat_hi[:, kt, c:c + w], lat_lo[:, kt, c:c + w]
                            for m, (a, b) in enumerate(((qh, kh), (qh, kl), (ql, kh))):
                                mm = pe.matmul(ps[:, 2 * (t % 2) + c // 512, 0:w], a, b,
                                               start=(kt == 0 and m == 0), stop=(kt == 1 and m == 2))
                    mm.then_inc(t_qk, 1)
                for part, cuts in enumerate((((0, 2), (0, 1)), ((2, 4), (1, 2)), ((4, TB), (2, TB // 2)))):
                    found = group_in(slot, 2 + part, pair, kind, prev)
                    if not found:
                        continue
                    p, group = found
                    g = group % 2
                    if part == 0:
                        pe.wait_ge(s_near, STEPS * p + 4 * group + 4)
                        if g == 0:
                            pe.wait_ge(s_far, STEPS // 2 * p + 4 * (group // 2) + 4)
                        wait_if(pe, t_cl, 2 * (4 * p + group))
                    low_cols, high_cols, both = slice(0, P), slice(P, LATENT), slice(P, LATENT + 64)
                    for ct, parts in enumerate((((val_hi, low_cols, 0), (val_hi, low_cols, 1),
                                                 (val_lo, low_cols, 0)),
                                                ((val_hi, both, 0), (val_hi, high_cols, 1)))):
                        _, _, dst = context_views(ct)
                        if part == 0 and ct == 1:
                            wait_if(pe, s_upl, 4 * p + group)
                        for j in range(*cuts[g]):
                            qs = max(0, j - 4) * P if g == 0 else j * P
                            ends = j == (TB, TB // 2)[g] - 1
                            for m, (v, cols, hi_or_lo) in enumerate(parts):
                                mm = pe.matmul(dst[0:cols.stop - cols.start, qs:512], v[:, j, cols],
                                               pt7[g][:, hi_or_lo, j, qs:512], start=(j == 0 and m == 0),
                                               stop=(ends and m == len(parts) - 1), skip_group_check=True)
                    if part == 2:
                        mm.then_inc(t_pv, 1)
                if not kind:
                    start_product(pe, slot, feed_o1, xt_hi, xt_lo, (s_upl, 4 * (N_PAIRS - 1)),
                                  (t_mx, STEPS * N_PAIRS))
                turned, p, t = trailing(pair, slot, kind, prev, None, 0)
                if turned:
                    turn_parts(pe, p, t)
                found = group_in(slot, 5, pair, kind, prev)
                if found:
                    p, group = found
                    if group == 0:
                        pe.wait_ge(s_uvn, 2 * (p + 1))
                    pe.wait_ge(t_cl, 2 * (4 * p + group + 1))
                    _, _, dst = up_views(group, p)
                    for ct in range(2):
                        uh, ul = uvn_hi[:, ct, group // 2, :], uvn_lo[:, ct, group // 2, :]
                        xh, xl = ctx_hi[:, ct, :], ctx_lo[:, ct, :]
                        for m, (a, b) in enumerate(((uh, xh), (uh, xl), (ul, xh))):
                            mm = pe.matmul(dst, a, b, start=(ct == 0 and m == 0), stop=(ct == 1 and m == 2))
                    mm.then_inc(s_up, 1)

        def latent_scalar(act, pair, kind, prev):
            for slot in slots_of(kind, prev, 7):
                turned, p, at = trailing(pair, slot, kind, prev, None, 1)
                if turned:
                    if prev is None and at == 0:
                        act.wait_ge(s_uvs, 1)
                    move_parts(act, p, at, 0)
                found = group_in(slot, 6, pair, kind, prev)
                if found:
                    p, group = found
                    hi, _, src = up_views(group, p)
                    act.wait_ge(s_up, 4 * p + group + 1)
                    act.activation(hi, src, ACT.Copy).then_inc(s_uph, 1)
                found = group_in(slot, 5, pair, kind, prev)
                if found:
                    p, group = found
                    act.wait_ge(t_pv, 4 * p + group + 1)
                    wait_if(act, s_up, 4 * p + group)
                    for ct in range(2):
                        hi, _, src = context_views(ct)
                        act.activation(hi, src, ACT.Copy).then_inc(t_ch, 1)
                two_back, p, t = trailing(pair, slot, kind, prev, 2)
                if two_back:
                    n = span[query_block(t)]
                    act.wait_ge(t_ri, STEPS * p + t + 1)
                    wait_if(act, s_turned, parts_free(p, t))
                    act.activation(parts7[t % 4][0][:, 0:n], prob7[t % 4][:, 0:n], ACT.Copy,
                                   scale=row_inv[:, t % 4:t % 4 + 1]).then_inc(t_ph, 1)
                if kind:
                    t, n = slot, span[query_block(slot)]
                    act.wait_ge(t_nm, STEPS * pair + t + 1)
                    act.activation(prob7[t % 4][:, 0:n], prob7[t % 4][:, 0:n], ACT.Exp, scale=DSA_SCALE,
                                   bias=neg_max[:, t % 4:t % 4 + 1],
                                   accum_out=row_sum[:, t % 4:t % 4 + 1]).then_inc(t_ex, 1)

        def latent_vector(dve, pair, kind, prev):
            for slot in slots_of(kind, prev, 7):
                turned, p, at = trailing(pair, slot, kind, prev, None, 1)
                if turned:
                    if prev is None and at == 0:
                        dve.wait_ge(s_uvs, 1)
                    move_parts(dve, p, at, 1)
                found = group_in(slot, 6, pair, kind, prev)
                if found:
                    p, group = found
                    hi, lo, src = up_views(group, p)
                    dve.wait_ge(s_uph, 4 * p + group + 1)
                    dve.tensor_tensor(lo, src, hi, ALU.subtract).then_inc(s_upl, 1)
                found = group_in(slot, 5, pair, kind, prev)
                if found:
                    p, group = found
                    for ct in range(2):
                        hi, lo, src = context_views(ct)
                        dve.wait_ge(t_ch, 2 * (4 * p + group) + ct + 1)
                        dve.tensor_tensor(lo, src, hi, ALU.subtract).then_inc(t_cl, 1)
                if kind:
                    t, i = slot, query_block(slot)
                    n = span[i]
                    wait_apart(dve, (t_qk, 1), (t_qk, STEPS * pair + t + 1), (t_w, STEPS * pair + t - 3))
                    dve.tensor_tensor_reduce(prob7[t % 4][:, 0:n], banks(2 * (t % 2))[:, 0:n],
                                             hide[:, at_of[i]:at_of[i] + n], 1.0, 3.0 * MASKED, ALU.add,
                                             ALU.max, row_max[:, t % 4:t % 4 + 1]).then_inc(t_mx, 1)
                    dve.wait_ge(t_mx, STEPS * pair + t + 1)
                    dve.tensor_scalar(neg_max[:, t % 4:t % 4 + 1], row_max[:, t % 4:t % 4 + 1], -DSA_SCALE,
                                      None, ALU.mult).then_inc(t_nm, 1)
                one_back, p, t = trailing(pair, slot, kind, prev, 1)
                if one_back:
                    n = span[query_block(t)]
                    dve.wait_ge(t_ex, STEPS * p + t + 1)
                    dve.reciprocal(row_inv[:, t % 4:t % 4 + 1], row_sum[:, t % 4:t % 4 + 1]).then_inc(t_ri, 1)
                two_back, p, t = trailing(pair, slot, kind, prev, 2)
                if two_back:
                    n = span[query_block(t)]
                    dve.wait_ge(t_ph, STEPS * p + t + 1)
                    dve.scalar_tensor_tensor(parts7[t % 4][1][:, 0:n], prob7[t % 4][:, 0:n],
                                             row_inv[:, t % 4:t % 4 + 1], parts7[t % 4][0][:, 0:n],
                                             ALU.mult, ALU.subtract).then_inc(t_w, 1)

        def all_latent_pairs(eng, each):
            each(eng, 0, "latent", None)
            with eng.Fori(1, N_PAIRS) as pair:
                each(eng, pair, "latent", "latent")
            each(eng, N_PAIRS, None, "latent")

        def attend_sync(sp):
            def load_q(h, pair):
                sp.dma_start(q_now[h][:, :, :, :],
                             q_dram[bass.ds(4 * pair + 2 * h, 2)].rearrange("s p l t -> p s l t")
                             ).then_inc(s_q7[h], 16)

            for r in range(4):
                sp.wait_ge(s_qst[r], 16 * feed_q.iters)
            sp.dma_start(uv_f[:, :, :, :], t_in["l1_uv"]).then_inc(s_uvl, 16)
            with sp.Fori(1, N_PAIRS) as pair:
                for h in range(2):
                    sp.wait_ge(t_qk, STEPS * (pair - 1) + 8 * (h + 1))
                    load_q(h, pair)

        def attend_gpsimd(pool):
            flat = "p a h n -> p (a h n)"
            whole, hi, lo = [u[:, :, :, :].rearrange(flat) for u in (uv_f, uv_hi, uv_lo)]
            pool.wait_ge(s_uvl, 16)
            pool.tensor_tensor(hi, whole, ones[:, 0:1].to_broadcast([P, 2 * N_DSA * 64]),
                               ALU.mult).then_inc(s_uvh, 1)
            pool.wait_ge(s_uvh, 1)
            pool.tensor_tensor(lo, whole, hi, ALU.subtract).then_inc(s_uvs, 1)
            pool.wait_ge(s_uvs, 1)

            def uv_pair(pair):
                for dst, src in ((uvn_hi, uv_hi), (uvn_lo, uv_lo)):
                    pool.tensor_copy(dst[:, :, :, :], src[:, :, bass.ds(2 * pair, 2), :]).then_inc(s_uvn, 1)

            uv_pair(0)
            split_first(pool, feed_o1)
            with pool.Fori(1, N_PAIRS) as pair:
                pool.wait_ge(s_up, 4 * pair)
                uv_pair(pair)

        def attend_tensor(pe):
            pe.wait_ge(s_cp, 4 * feed_q.iters)
            all_latent_pairs(pe, latent_tensor)

        def attend_scalar(act):
            all_latent_pairs(act, latent_scalar)

        def attend_vector(dve):
            dve.wait_ge(s_ql, 4 * feed_q.iters)
            dve.wait_ge(s_hide, 2 * TB - len(picky))
            all_latent_pairs(dve, latent_vector)

        up1, up1_sems = feed_forward_up("up1", feed_up1, t_in["l1_conv"], feed_down1)
        run_phases(
            phase(index_sync, index_gpsimd, index_tensor, index_scalar, index_vector),
            phase(topk_sync, topk_gpsimd, topk_tensor, topk_scalar, topk_vector),
            phase(attend_sync, attend_gpsimd, attend_tensor, attend_scalar, attend_vector),
            back_and_norm("o1", feed_o1, xt_hi, xt_lo, [(0, KT)], (t_in["l1_ln1_g"], t_in["l1_ln1_b"]),
                          arena, feed_up1, meanwhile=early_strips(feed_up1), started=(s_upl, 4 * N_PAIRS)),
            up1,
            back_and_norm("dn1", feed_down1, hid_hi, hid_lo, DOWN_CUT, (t_in["l1_ln2_g"], t_in["l1_ln2_b"]),
                          after_hid, None, final=out, after=up1_sems))



def tiles(w, cols=P):
    k, n = w.shape
    return np.ascontiguousarray(w.reshape(k // P, P, n // cols, cols).transpose(2, 1, 0, 3).reshape(n // cols, P, -1))


def rotary_order():
    return np.array(list(range(0, 8)) + list(range(16, 40)) + list(range(8, 16)) + list(range(40, 64)))


def rope_row_constants():
    rows = np.zeros((P, 4), np.float32)
    for r in range(P):
        half, u = IDX_DIM // 8, r % 32
        if u < half:
            rows[r, 0] = np.float32(THETA) ** np.float32(-u / half)
            rows[r, 1] = -1.0 if r % 64 < 32 else 1.0
        if r < ROPE:
            half = KEY_DIM // 8
            rows[r, 2] = np.float32(THETA) ** np.float32(-(r % 32) / half)
            rows[r, 3] = -1.0 if r < 32 else 1.0
    return rows


def kernel(**inputs):
    import concourse.bacc as bacc
    from concourse.bass_utils import run_bass_kernel_spmd

    a = {k: np.asarray(v) for k, v in inputs.items()}
    c = np.ascontiguousarray
    x = a["x"][0]
    d = {}
    d["x"] = c(x.reshape(TB, P, D_MODEL).transpose(1, 0, 2))
    d["xt"] = c(x.T.reshape(KT, P, SEQ).transpose(1, 0, 2))
    d["positions"] = c(np.broadcast_to(a["positions"], (P, SEQ)))
    d["rope_rows"] = rope_row_constants()
    w = a["l0_w_in"]
    s = tiles(w[:, :3072])
    d["l0_qkv"] = c(s.reshape(2, 3, 4, P, -1).transpose(0, 2, 1, 3, 4).reshape(24, P, -1))
    d["l0_wf"] = c(w[:, 3072:].reshape(KT, P, 8).transpose(1, 0, 2))
    d["l0_bf"] = c(a["l0_b_f"].reshape(8, 1))
    d["l0_o"] = tiles(a["l0_w_o"])
    w = a["l1_w_in"]
    c0 = N_DSA * KEY_DIM
    c2 = c0 + ROPE + LATENT
    c3 = c2 + IDX_HEADS * IDX_DIM
    c4 = c3 + IDX_DIM
    order = rotary_order()
    d["l1_q"] = tiles(w[:, :c0])
    d["l1_qidx"] = tiles(w[:, c2:c3].reshape(D_MODEL, IDX_HEADS, IDX_DIM)[:, :, order].reshape(D_MODEL, -1))
    kidx = w[:, c3:c4][:, order]
    d["l1_kidx"] = tiles(np.concatenate([kidx, kidx], 1))[0]
    d["l1_klat0"], d["l1_klat1"] = tiles(w[:, c0:c2])
    lat = w[:, c0 + ROPE:c2]
    d["l1_v128"] = tiles(lat[:, :P])[0]
    d["l1_v64w"] = tiles(np.concatenate([lat[:, P:], w[:, c4:]], 1), 80)[0]
    uv = np.zeros((2, P, N_DSA, 64), np.float32)
    wuv = a["l1_w_uv"].transpose(1, 0, 2)
    uv[0], uv[1, :64], uv[1, 64:] = wuv[:P], wuv[P:], wuv[P:]
    d["l1_uv"] = c(uv.transpose(1, 0, 2, 3))
    d["l1_o"] = tiles(a["l1_w_o"])
    for n in range(2):
        up = tiles(a[f"l{n}_w_up"])
        d[f"l{n}_up"] = c(up.reshape(2, FT, P, -1).transpose(1, 0, 2, 3).reshape(2 * FT, P, -1))
        conv = np.concatenate([a[f"l{n}_conv_w"], a[f"l{n}_conv_b"][None]])
        d[f"l{n}_conv"] = c(conv.reshape(4, FT, P).transpose(2, 1, 0).reshape(P, -1))
        d[f"l{n}_down"] = tiles(a[f"l{n}_w_down"])
        for m in (1, 2):
            for q in "gb":
                d[f"l{n}_ln{m}_{q}"] = c(np.broadcast_to(a[f"l{n}_ln{m}_{q}"], (P, D_MODEL)))

    nc = bacc.Bacc("TRN2", target_bir_lowering=False, num_devices=1)
    arrays, t_in = {}, {}
    for name, v in d.items():
        arrays[f"in_{name}"] = v
        t_in[name] = nc.dram_tensor(f"in_{name}", v.shape, mybir.dt.from_np(v.dtype), kind="ExternalInput").ap()
    out = nc.dram_tensor("out", (TB, P, D_MODEL), F32, kind="ExternalOutput").ap()
    program(nc, t_in, out)
    r = run_bass_kernel_spmd(nc, [arrays], core_ids=[0])
    return r.results[0]["out"].reshape(1, SEQ, D_MODEL)
```
